# Optimizing a Trainium2 kernel written in Bass

```python
import math
import jax, jax.numpy as jnp
from jax import lax
import numpy as np

D_MODEL = 2048
BATCH = 1
SEQ = 256
DEPTH = 1
DEC_BATCH = 8
DEC_SEQ = 1
PAST_LEN = 2048
PAGE_SIZE = 128

D_RNN = D_MODEL
RNN_BLOCKS = 16
RNN_BW = D_RNN // RNN_BLOCKS
LRU_C = 8.0
CONV_W = 4
SSM_EXPAND = 2
D_SSM = SSM_EXPAND * D_MODEL
SSM_HEAD_DIM = 64
SSM_HEADS = D_SSM // SSM_HEAD_DIM
SSM_GROUPS = 8
SSM_STATE = 128
SSM_CHUNK = 128
D_XBC = D_SSM + 2 * SSM_GROUPS * SSM_STATE
MOE_GROUPS = 4
MOE_EXPERTS_PER_GROUP = 4
N_EXPERTS = MOE_GROUPS * MOE_EXPERTS_PER_GROUP
MOE_TOPK = 2
D_EXPERT = 512
EPS = 1e-6
IN_SIZES = (D_RNN, D_RNN, D_SSM, D_XBC, SSM_HEADS, D_MODEL, D_MODEL)
D_IN = sum(IN_SIZES)
IN_SPLITS = [int(v) for v in np.cumsum(IN_SIZES)[:-1]]

kernel_name = "griffin_ssd_hier_moe_step"

def rmsnorm(x, g):
    xf = x.astype(jnp.float32)
    y = xf * lax.rsqrt(jnp.mean(xf * xf, axis=-1, keepdims=True) + EPS) * g.astype(jnp.float32)
    return y.astype(x.dtype)

def causal_conv(x, prev, w, b):
    t = x.shape[1]
    xp = jnp.concatenate([prev.astype(x.dtype), x], axis=1)
    out = b + sum(xp[:, k:k + t] * w[k] for k in range(CONV_W))
    return out.astype(x.dtype), xp[:, -(CONV_W - 1):]

def rglru(x, h0, w_a, b_a, w_x, b_x, lam, reset_first):
    bsz, t, _ = x.shape
    xb = x.reshape(bsz, t, RNN_BLOCKS, RNN_BW)
    r = jax.nn.sigmoid((jnp.einsum('btnc,ncd->btnd', xb, w_a) + b_a).astype(jnp.float32)).reshape(bsz, t, D_RNN)
    i = jax.nn.sigmoid((jnp.einsum('btnc,ncd->btnd', xb, w_x) + b_x).astype(jnp.float32)).reshape(bsz, t, D_RNN)
    log_a = -LRU_C * r * jax.nn.softplus(-lam.astype(jnp.float32))
    a = jnp.exp(log_a)
    mult = jnp.sqrt(-jnp.expm1(2.0 * log_a))
    if reset_first:
        mult = mult.at[:, 0].set(1.0)
    bterm = mult * (i * x.astype(jnp.float32))
    bterm = bterm.at[:, 0].add(a[:, 0] * h0.astype(jnp.float32))

    def combine(lhs, rhs):
        a1, b1 = lhs
        a2, b2 = rhs
        return a1 * a2, a2 * b1 + b2

    _, h = lax.associative_scan(combine, (a, bterm), axis=1)
    return h.astype(x.dtype), h[:, -1]

def ssd_scan(x, dt, a, bm, cm, h0):
    bsz, t = x.shape[:2]
    hg = SSM_HEADS // SSM_GROUPS
    l = math.gcd(t, SSM_CHUNK)
    nc = t // l
    xc = (x * dt[..., None]).reshape(bsz, nc, l, SSM_GROUPS, hg, SSM_HEAD_DIM)
    da = (dt * a).reshape(bsz, nc, l, SSM_GROUPS, hg)
    bc = bm.reshape(bsz, nc, l, SSM_GROUPS, SSM_STATE)
    cc = cm.reshape(bsz, nc, l, SSM_GROUPS, SSM_STATE)
    cs = jnp.cumsum(da, axis=2)
    seg = cs[:, :, :, None] - cs[:, :, None, :]
    mask = jnp.tril(jnp.ones((l, l), dtype=bool))[None, None, :, :, None, None]
    ldec = jnp.exp(jnp.where(mask, seg, -jnp.inf))
    scores = jnp.einsum('bclgn,bcsgn->bclsg', cc, bc)
    y_diag = jnp.einsum('bclsg,bclsgh,bcsghp->bclghp', scores, ldec, xc)
    decay_states = jnp.exp(cs[:, :, -1:] - cs)
    states = jnp.einsum('bclgn,bclgh,bclghp->bcghpn', bc, decay_states, xc)
    chunk_decay = jnp.exp(cs[:, :, -1])

    def step(h, inp):
        st, dec = inp
        return h * dec[..., None, None] + st, h

    h_init = h0.reshape(bsz, SSM_GROUPS, hg, SSM_HEAD_DIM, SSM_STATE)
    h_fin, h_prev = lax.scan(step, h_init, (jnp.swapaxes(states, 0, 1), jnp.swapaxes(chunk_decay, 0, 1)))
    h_prev = jnp.swapaxes(h_prev, 0, 1)
    y_off = jnp.einsum('bclgn,bcghpn,bclgh->bclghp', cc, h_prev, jnp.exp(cs))
    y = (y_diag + y_off).reshape(bsz, t, SSM_HEADS, SSM_HEAD_DIM)
    return y, h_fin.reshape(bsz, SSM_HEADS, SSM_HEAD_DIM, SSM_STATE)

def token_mixers(xn, conv_r, h_r, conv_s, h_s, reset_first, w_in, conv_rnn_w, conv_rnn_b, lru_wa, lru_ba,
                 lru_wx, lru_bx, lru_lambda, conv_ssd_w, conv_ssd_b, dt_bias, a_log, d_skip, norm_ssd,
                 w_up_rnn, w_up_ssd, w_out):
    bsz, t, _ = xn.shape
    proj = xn @ w_in
    rx, ry, z, xbc, dt_raw, g_rnn, g_ssd = jnp.split(proj, IN_SPLITS, axis=-1)
    rx, conv_r_new = causal_conv(rx, conv_r, conv_rnn_w, conv_rnn_b)
    h, h_r_new = rglru(rx, h_r, lru_wa, lru_ba, lru_wx, lru_bx, lru_lambda, reset_first)
    y_rnn = h * jax.nn.gelu(ry)
    xbc, conv_s_new = causal_conv(xbc, conv_s, conv_ssd_w, conv_ssd_b)
    xbc = jax.nn.silu(xbc)
    xs, bm, cm = jnp.split(xbc, [D_SSM, D_SSM + SSM_GROUPS * SSM_STATE], axis=-1)
    dt = jax.nn.softplus((dt_raw + dt_bias).astype(jnp.float32))
    a = -jnp.exp(a_log.astype(jnp.float32))
    xh = xs.reshape(bsz, t, SSM_HEADS, SSM_HEAD_DIM).astype(jnp.float32)
    y, h_s_new = ssd_scan(xh, dt, a,
                          bm.reshape(bsz, t, SSM_GROUPS, SSM_STATE).astype(jnp.float32),
                          cm.reshape(bsz, t, SSM_GROUPS, SSM_STATE).astype(jnp.float32),
                          h_s.astype(jnp.float32))
    y = y + d_skip.astype(jnp.float32)[:, None] * xh
    y = y.reshape(bsz, t, D_SSM) * jax.nn.silu(z.astype(jnp.float32))
    yg = y.reshape(bsz, t, SSM_GROUPS, D_SSM // SSM_GROUPS)
    yg = yg * lax.rsqrt(jnp.mean(yg * yg, axis=-1, keepdims=True) + EPS)
    y_ssd = (yg.reshape(bsz, t, D_SSM) * norm_ssd.astype(jnp.float32)).astype(xn.dtype)
    merged = jax.nn.sigmoid(g_rnn) * (y_rnn @ w_up_rnn) + jax.nn.sigmoid(g_ssd) * (y_ssd @ w_up_ssd)
    return merged @ w_out, conv_r_new, h_r_new, conv_s_new, h_s_new

def hier_moe(xn, w_rg, b_rg, w_re, b_re, w_gate, w_up, w_down):
    bsz, t, d = xn.shape
    xt = xn.reshape(-1, d)
    n = xt.shape[0]
    gl = (xt @ w_rg + b_rg).astype(jnp.float32)
    gp = jax.nn.softmax(gl, axis=-1)
    g_idx = jnp.argmax(gl, axis=-1)
    g_w = jnp.take_along_axis(gp, g_idx[:, None], axis=1)[:, 0]
    el = (xt @ w_re + b_re).astype(jnp.float32).reshape(n, MOE_GROUPS, MOE_EXPERTS_PER_GROUP)
    el_sel = jnp.take_along_axis(el, g_idx[:, None, None], axis=1)[:, 0]
    top_p, top_i = lax.top_k(jax.nn.softmax(el_sel, axis=-1), MOE_TOPK)
    top_p = top_p / jnp.sum(top_p, axis=-1, keepdims=True)
    expert_id = g_idx[:, None] * MOE_EXPERTS_PER_GROUP + top_i
    weights = g_w[:, None] * top_p
    combine = jnp.sum(jax.nn.one_hot(expert_id, N_EXPERTS, dtype=jnp.float32) * weights[..., None], axis=1)
    combine = combine.astype(xt.dtype)
    out = jnp.zeros_like(xt)
    for e in range(N_EXPERTS):
        hid = jax.nn.silu(xt @ w_gate[e]) * (xt @ w_up[e])
        out = out + combine[:, e:e + 1] * (hid @ w_down[e])
    return out.reshape(bsz, t, d)

def setup_inputs(seed: int = 0) -> dict:
    key = jax.random.key(seed)
    ks = iter(jax.random.split(key, 40))
    f32 = jnp.float32

    def nrm(shape, scale):
        return jax.random.normal(next(ks), shape, f32) * scale

    def gain(shape):
        return 1.0 + nrm(shape, 0.02)

    u = jax.random.uniform(next(ks), (DEPTH, D_RNN), f32, 0.9, 0.999)
    s = u ** (1.0 / LRU_C)
    lru_lambda = jnp.log(s / (1.0 - s))
    dt0 = jnp.exp(jax.random.uniform(next(ks), (DEPTH, SSM_HEADS), f32, math.log(1e-3), math.log(1e-1)))
    dt_bias = dt0 + jnp.log(-jnp.expm1(-dt0))
    a_log = jnp.log(jax.random.uniform(next(ks), (DEPTH, SSM_HEADS), f32, 1.0, 16.0))
    return {
        "x_prompt": nrm((BATCH, SEQ, D_MODEL), 1.0),
        "x_sample": nrm((DEC_BATCH, DEC_SEQ, D_MODEL), 1.0),
        "state_rglru_conv": nrm((DEPTH, DEC_BATCH, CONV_W - 1, D_RNN), 1.0),
        "state_rglru_h": nrm((DEPTH, DEC_BATCH, D_RNN), 0.5),
        "state_ssd_conv": nrm((DEPTH, DEC_BATCH, CONV_W - 1, D_XBC), 1.0),
        "state_ssd_h": nrm((DEPTH, DEC_BATCH, SSM_HEADS, SSM_HEAD_DIM, SSM_STATE), 0.5),
        "norm_mix": gain((DEPTH, D_MODEL)),
        "w_in": nrm((DEPTH, D_MODEL, D_IN), D_MODEL ** -0.5),
        "conv_rnn_w": nrm((DEPTH, CONV_W, D_RNN), CONV_W ** -0.5),
        "conv_rnn_b": nrm((DEPTH, D_RNN), 0.02),
        "lru_wa": nrm((DEPTH, RNN_BLOCKS, RNN_BW, RNN_BW), RNN_BW ** -0.5),
        "lru_ba": nrm((DEPTH, RNN_BLOCKS, RNN_BW), 0.02),
        "lru_wx": nrm((DEPTH, RNN_BLOCKS, RNN_BW, RNN_BW), RNN_BW ** -0.5),
        "lru_bx": nrm((DEPTH, RNN_BLOCKS, RNN_BW), 0.02),
        "lru_lambda": lru_lambda,
        "conv_ssd_w": nrm((DEPTH, CONV_W, D_XBC), CONV_W ** -0.5),
        "conv_ssd_b": nrm((DEPTH, D_XBC), 0.02),
        "dt_bias": dt_bias,
        "a_log": a_log,
        "d_skip": gain((DEPTH, SSM_HEADS)),
        "norm_ssd": gain((DEPTH, D_SSM)),
        "w_up_rnn": nrm((DEPTH, D_RNN, D_MODEL), D_RNN ** -0.5),
        "w_up_ssd": nrm((DEPTH, D_SSM, D_MODEL), D_SSM ** -0.5),
        "w_out": nrm((DEPTH, D_MODEL, D_MODEL), D_MODEL ** -0.5),
        "norm_ffn": gain((DEPTH, D_MODEL)),
        "w_route_group": nrm((DEPTH, D_MODEL, MOE_GROUPS), D_MODEL ** -0.5),
        "b_route_group": nrm((DEPTH, MOE_GROUPS), 0.01),
        "w_route_expert": nrm((DEPTH, D_MODEL, N_EXPERTS), D_MODEL ** -0.5),
        "b_route_expert": nrm((DEPTH, N_EXPERTS), 0.01),
        "w_exp_gate": nrm((DEPTH, N_EXPERTS, D_MODEL, D_EXPERT), D_MODEL ** -0.5),
        "w_exp_up": nrm((DEPTH, N_EXPERTS, D_MODEL, D_EXPERT), D_MODEL ** -0.5),
        "w_exp_down": nrm((DEPTH, N_EXPERTS, D_EXPERT, D_MODEL), D_EXPERT ** -0.5),
        "norm_final": gain((D_MODEL,)),
    }

def reference(x_prompt, x_sample, state_rglru_conv, state_rglru_h, state_ssd_conv, state_ssd_h,
              norm_mix, w_in, conv_rnn_w, conv_rnn_b, lru_wa, lru_ba, lru_wx, lru_bx, lru_lambda,
              conv_ssd_w, conv_ssd_b, dt_bias, a_log, d_skip, norm_ssd, w_up_rnn, w_up_ssd, w_out,
              norm_ffn, w_route_group, b_route_group, w_route_expert, b_route_expert,
              w_exp_gate, w_exp_up, w_exp_down, norm_final):
    hp, hs = x_prompt, x_sample
    bp = x_prompt.shape[0]
    p_cr, p_hr, p_cs, p_hs = [], [], [], []
    s_cr, s_hr, s_cs, s_hs = [], [], [], []
    for l in range(DEPTH):
        mix_w = (w_in[l], conv_rnn_w[l], conv_rnn_b[l], lru_wa[l], lru_ba[l], lru_wx[l], lru_bx[l],
                 lru_lambda[l], conv_ssd_w[l], conv_ssd_b[l], dt_bias[l], a_log[l], d_skip[l], norm_ssd[l],
                 w_up_rnn[l], w_up_ssd[l], w_out[l])
        moe_w = (w_route_group[l], b_route_group[l], w_route_expert[l], b_route_expert[l],
                 w_exp_gate[l], w_exp_up[l], w_exp_down[l])
        zc_r = jnp.zeros((bp, CONV_W - 1, D_RNN), hp.dtype)
        zh_r = jnp.zeros((bp, D_RNN), jnp.float32)
        zc_s = jnp.zeros((bp, CONV_W - 1, D_XBC), hp.dtype)
        zh_s = jnp.zeros((bp, SSM_HEADS, SSM_HEAD_DIM, SSM_STATE), jnp.float32)
        mo, cr, hr, cs_, hs_ = token_mixers(rmsnorm(hp, norm_mix[l]), zc_r, zh_r, zc_s, zh_s, True, *mix_w)
        hp = hp + mo
        hp = hp + hier_moe(rmsnorm(hp, norm_ffn[l]), *moe_w)
        p_cr.append(cr); p_hr.append(hr); p_cs.append(cs_); p_hs.append(hs_)
        mo, cr, hr, cs_, hs_ = token_mixers(rmsnorm(hs, norm_mix[l]), state_rglru_conv[l], state_rglru_h[l],
                                            state_ssd_conv[l], state_ssd_h[l], False, *mix_w)
        hs = hs + mo
        hs = hs + hier_moe(rmsnorm(hs, norm_ffn[l]), *moe_w)
        s_cr.append(cr); s_hr.append(hr); s_cs.append(cs_); s_hs.append(hs_)
    y_prompt = rmsnorm(hp, norm_final)
    y_sample = rmsnorm(hs, norm_final)
    return (y_prompt, y_sample,
            jnp.stack(p_cr), jnp.stack(p_hr), jnp.stack(p_cs), jnp.stack(p_hs),
            jnp.stack(s_cr), jnp.stack(s_hr), jnp.stack(s_cs), jnp.stack(s_hs))


_drawn_inputs = setup_inputs


def setup_inputs(seed=0):
    import zlib

    import numpy as np

    out = dict(_drawn_inputs(seed))
    spreads = {}
    factors = {'lru_ba': 8.0,
     'lru_bx': 7.206,
     'd_skip': 3.611,
     'norm_ssd': 3.062,
     'norm_ffn': 3.687,
     'b_route_group': 57.976,
     'b_route_expert': 22.492,
     'norm_final': 7.505}
    for name, (base, spread) in spreads.items():
        noise = np.random.default_rng([zlib.crc32(name.encode()), seed]).standard_normal(out[name].shape)
        drawn = base * np.exp(spread * noise) if base else spread * noise
        out[name] = __import__('jax').numpy.asarray(drawn.astype(out[name].dtype))
    for name, factor in factors.items():
        out[name] = (out[name] * factor).astype(out[name].dtype)
    return out
```

```python
from contextlib import ExitStack

import concourse.bass as bass
from concourse import mybir
from concourse.alu_op_type import AluOpType as ALU

F32 = mybir.dt.float32
ACT = mybir.ActivationFunctionType
AX = mybir.AxisListType

P = 128
D = 2048
ND = D // P
SEQ = 256
NB = 8
T = SEQ + NB
CH = 128
HEADS, HD, NS, GROUPS = 64, 64, 128, 8
HG = HEADS // GROUPS
D_SSM = HEADS * HD
D_XBC = D_SSM + 2 * GROUPS * NS
NX = D_XBC // P
TAPS = 4
HIST = TAPS - 1
EXPERTS, EG, FE = 16, 4, 512
EPS = 1e-6
XPW = HIST + SEQ + NB * TAPS
CVW = XPW - HIST
S0 = HIST + SEQ

RX, RY, Z, XBC = 0, D, 2 * D, 2 * D + D_SSM
DT = XBC + D_XBC
GR = DT + HEADS
GS = GR + D

V_MIX, V_CRW, V_CRB, V_BA, V_BX = 0, 16, 80, 96, 112
V_LAM, V_NSSD, V_FFN, V_FIN, V_CSB, V_CSW = 128, 144, 176, 192, 208, 256
NV = V_CSW + TAPS * NX

FIRST = ND

RNN_N, BC_N, SSD_N, GATE_N, OUT_N = 4, 4, GROUPS, 4, 4
BC_SLAB, BC_ROUND = 12, 24
SSD_SLAB, SSD_ROUND = 16, 28
GATE_SLAB, GATE_ROUND = 40, 76
OUT_SLAB, OUT_ROUND = 48, 84
MOE_SLAB, MOE_ROUND = 52, 88

RNN_EVENTS = [("r0", 0), ("r1", 1), ("r2", 2), ("r3", 3), ("i0", 0), ("i1", 1), ("i2", 2), ("i3", 3)]
SSD_EVENTS = [("G", 0), ("cs0", 1), ("cs1", 2), ("cs2", 1), ("cs3", 2), ("btok", 0), ("sd", 3),
              ("Bb0", 0), ("Bb1", 3), ("Cb0", 1), ("Cb1", 2), ("xt0", 0), ("xt1", 3),
              ("st0", 1), ("hf", 2), ("y0", 0), ("y1", 3), ("gn", 1)]
ROW_EVENTS = [(f"row{k}", k % 4) for k in range(20)]
OUTT_EVENTS = [(f"o{k}", k % 4) for k in range(12)]


class Events:

    def __init__(self, events, before=None, repeats=1):
        self.events, self.repeats = events, repeats
        self.start = before.end if before else 0
        self.bank_start = list(before.bank_end) if before else [0] * 4
        self.index = {n: k for k, (n, _) in enumerate(events)}
        self.bank = dict(events)
        self.per_bank = [sum(b == k for _, b in events) for k in range(4)]
        self.end = self.start + repeats * len(events)
        self.bank_end = [s + repeats * n for s, n in zip(self.bank_start, self.per_bank)]

    def full(self, name, it=0):
        return it * len(self.events) + (self.start + self.index[name] + 1)

    def earlier(self, name, it=0):
        b, k = self.bank[name], self.index[name]
        return it * self.per_bank[b] + (self.bank_start[b] + sum(x == b for _, x in self.events[:k]))


SETUP = Events([("vec", 0), ("hr", 1), ("hs0", 2), ("hs1", 3), ("hs2", 0), ("ss1", 1), ("dt", 2),
                ("dtt", 3), ("tot", 0)])
RNN = Events(RNN_EVENTS, SETUP, RNN_N)
SSD = Events(SSD_EVENTS, RNN, SSD_N)
ROWS = Events(ROW_EVENTS, SSD)
ROUTE = Events([("ss2", 0), ("logit", 1), ("combt", 2)], ROWS)
MOE = Events([("cb", 3)], ROUTE, EXPERTS)
FINAL = Events([("ss3", 0)], MOE)
OUTT = Events(OUTT_EVENTS, FINAL)


def wait_pos(eng, sem, value):
    if not (isinstance(value, int) and value <= 0):
        eng.wait_ge(sem, value)


def build_program(nc, a, o):
    w_in = a["w_in"][0].rearrange("(k p) n -> p k n", p=P)
    w_upr = a["w_up_rnn"][0].rearrange("(s k p) n -> s p k n", p=P, k=4)
    w_ups = a["w_up_ssd"][0].rearrange("(s k p) n -> s p k n", p=P, k=4)
    w_out = a["w_out"][0].rearrange("(k p) n -> p k n", p=P)
    w_gate = a["w_exp_gate"][0].rearrange("e (k p) n -> e p k n", p=P)
    w_up = a["w_exp_up"][0].rearrange("e (k p) n -> e p k n", p=P)
    w_down = a["w_exp_down"][0].rearrange("e (k p) n -> e p k n", p=P)
    h0_dram = a["state_ssd_h"][0].rearrange("b (t h) p n -> t (h p) b n", h=2)
    h1_dram = o["s_hs"][0].rearrange("b (t h) p n -> t (h p) b n", h=2)
    hp_dram = o["p_hs"][0, 0].rearrange("(t h) p n -> (h p) t n", h=2)
    lru_w = [a[n][0].rearrange("t c d -> c t d") for n in ("lru_wa", "lru_wx")]

    with ExitStack() as ctx:
        def sb(name, *free):
            return ctx.enter_context(nc.sbuf_tensor(name, [P, *free], F32))

        def sem(name):
            return ctx.enter_context(nc.semaphore(name))

        ring = sb("ring", 4, 4, 512)
        xn = sb("xn", ND, T)
        big = sb("big", 3 * ND * T)
        part = [big[:, k * ND * T:(k + 1) * ND * T] for k in range(3)]
        acc_rnn, acc_ssd, bc = [p.rearrange("p (t n) -> p t n", n=T) for p in part]
        vec = sb("vec", NV)
        hist_r = sb("hist_r", ND, 32)
        stash_r = sb("stash_r", ND, 27)
        hist_s = sb("hist_s", NX, 27)
        stash_s = hist_s
        stash_h = sb("stash_h", ND, 9)
        ident = sb("ident", P)
        ones = sb("ones", P)
        mask = sb("mask", P)
        eps = sb("eps", 1)
        c8 = sb("c8", 2, ND)
        d_col = sb("d_col", HEADS // 2)
        cs_tok = sb("cs_tok", 2, HEADS)
        wts = sb("wts", 5, HEADS)
        dt_f = sb("dt_f", T)
        cs_f = sb("cs_f", SEQ)
        sd_f = sb("sd_f", 2 * NB)
        rs = sb("rs", T)

        used = (4 * 4 * 512 + ND * T * 4 + NV + ND * 32 + ND * 27 + NX * 27 + ND * 9
                + 3 * P + 1 + 2 * ND + 32 + 7 * HEADS + T + SEQ + 2 * NB + T)
        work = sb("work", 53000 - used)
        size = 53000 - used

        class Area:
            def __init__(self, at=0):
                self.at = at

            def take(self, *free):
                n = 1
                for f in free:
                    n *= f
                assert self.at + n <= size, (self.at + n, size)
                v = work[:, self.at:self.at + n]
                self.at += n
                if len(free) == 2:
                    v = v.rearrange("p (a b) -> p a b", b=free[1])
                if len(free) == 3:
                    v = v.rearrange("p (a b c) -> p a b c", b=free[1], c=free[2])
                return v

        common = Area()
        xp = common.take(4, XPW)
        cv = common.take(4, CVW)
        cx = common.take(4, T)

        s = Area(common.at)
        vrow = s.take(4, P)
        hrow_r = s.take(D)
        hrow_s = s.take(D_XBC)
        sq = s.take(ND, T)
        dtw = s.take(ND, HEADS)
        xtok0 = big[:, ND * T:ND * T + 3 * D].rearrange("p (b n) -> p b n", n=D)
        xT0 = acc_rnn
        sm_u, sm_e, sm_r, sm_s, sm_p = [s.take(T) for _ in range(5)]
        dt_b, a_neg, d_bc = s.take(1), s.take(1), s.take(HEADS)
        dt_tok, tot, dg = s.take(2, HEADS), s.take(2, HEADS), s.take(2, HEADS)
        lm = s.take(5, ND)

        s = Area(common.at)
        gr, gi, ga, gt, gm, hh, ge, yr = [s.take(4, T) for _ in range(8)]
        lruw = s.take(2, 4, P)
        gs = s.take(4, NB)

        s = Area(common.at)
        sz, yn = s.take(4, T), s.take(4, T)
        yv = cv[:, :, 0:T]
        dm2 = s.take(2, HG, CH)
        dm = [dm2[:, c, :, :] for c in range(2)]
        sq_g = dm2.rearrange("p c h l -> p (c h l)")[:, 0:4 * T].rearrange("p (t n) -> p t n", n=T)
        ec = s.take(HG, CH)
        bb, cb = s.take(NB, NS), s.take(NB, NS)
        h_ring = s.take(4, NB, NS)
        ub = [s.take(NB, NS) for _ in range(2)]
        xd = [s.take(512) for _ in range(5)]
        st0 = s.take(512)
        btok, gtm = s.take(2, CH), s.take(2, CH)
        bcs = s.take(P)
        ccs = s.take(P)
        sel = s.take(HG, P)
        selb = s.take(NB, P)
        bcur, ccur = s.take(T), s.take(T)
        hf = xd[3].rearrange("p (t n) -> p t n", n=NS)
        sd = s.take(4, 2 * NB)
        xdt_s, ys = s.take(4, NB), s.take(4, NB)
        cur_cs, cur_w, cur_d = s.take(2, HG), s.take(5, HG), s.take(4)

        s = Area(common.at)
        row_s, row_r, row_h = s.take(D_XBC), s.take(D), s.take(D)
        g1, g2 = s.take(4, T), s.take(4, T)
        s = Area(0)
        xtok = s.take(3, D)
        xtile = s.take(3, 512)
        xres = acc_ssd
        s = Area(0)
        sq2 = bc
        wr = s.take(ND, 20)
        br = s.take(20)
        lg = s.take(3, 20)
        rt = [s.take(3, 16) for _ in range(10)]
        comb = s.take(3, EXPERTS)
        comb_t = s.take(T)
        sel_e = s.take(P)
        hg, hid = s.take(4, T), s.take(4, T)
        cbs = s.take(T)
        ytok = s.take(3, D)

        acc = [ctx.enter_context(nc.psum_tensor(f"acc{j}", [P, 512], F32)) for j in range(4)]
        side = [ctx.enter_context(nc.psum_tensor(f"side{j}", [P, 512], F32)) for j in range(4)]

        landed = [sem(f"chunk_landed{q}") for q in range(4)]
        tile_done = sem("tile_done")
        acc_free = [sem(f"acc_free{j}") for j in range(4)]
        side_full = sem("side_full")
        side_free = [sem(f"side_free{j}") for j in range(4)]
        barrier = sem("barrier")
        x_landed, small_landed = sem("x_landed"), sem("small_landed")
        dtw_landed, lru_landed = sem("dtw_landed"), sem("lru_landed")
        h_landed = [sem(f"h_landed{q}") for q in range(4)]
        h_stored = [sem(f"h_stored{q}") for q in range(4)]
        hf_stored, stored = sem("hf_stored"), sem("stored")
        consts = sem("consts")
        sq_ready, root_ready, xn_ready = sem("sq_ready"), sem("root_ready"), sem("xn_ready")
        xt_done = sem("xt_done")
        hist_in, xp_in, conv_done, stash_done = sem("hist_in"), sem("xp_in"), sem("conv_done"), sem("stash_done")
        stash_begun = sem("stash_begun")
        act_step, dve_step = sem("act_step"), sem("dve_step")
        gates_ready, decay_ready = sem("gates_ready"), sem("decay_ready")
        m2_ready, mult_ready, gelu_ready, y_ready = (sem("m2_ready"), sem("mult_ready"), sem("gelu_ready"),
                                                     sem("y_ready"))
        h_stashed = sem("h_stashed")
        bc_ready = sem("bc_ready")
        cur_ready = sem("cur_ready")
        diffed, ecs_ready, cts_ready = sem("diffed"), sem("ecs_ready"), sem("cts_ready")
        exp_ready, m_ready, gt_ready = sem("exp_ready"), sem("m_ready"), sem("gt_ready")
        tok_ready, bcb_ready, bcs_ready = sem("tok_ready"), sem("bcb_ready"), sem("bcs_ready")
        xs_ready, xdts_ready, u_ready = sem("xs_ready"), sem("xdts_ready"), sem("u_ready")
        h_new, xd_ready, st_ready, hf_ready = sem("h_new"), sem("xd_ready"), sem("st_ready"), sem("hf_ready")
        sz_ready, yz_ready, sqg_ready, yn_ready = sem("sz_ready"), sem("yz_ready"), sem("sqg_ready"), sem("yn_ready")
        rows_ready = sem("rows_ready")
        sg_ready, merged_ready, xtile_ready = sem("sg_ready"), sem("merged_ready"), sem("xtile_ready")
        wr_landed, comb_ready, combt_ready = sem("wr_landed"), sem("comb_ready"), sem("combt_ready")
        sele_ready, hg_ready, cb_ready, hid_ready = sem("sele_ready"), sem("hg_ready"), sem("cb_ready"), sem("hid_ready")
        ytok_ready = sem("ytok_ready")

        block = ctx.enter_context(nc.Block())
        ENG = 4

        def meet(eng, n):
            eng.drain().then_inc(barrier, 1)
            eng.wait_ge(barrier, ENG * n)

        @block.sync
        def _(sp):
            def chunk(slab, q, src):
                if not (isinstance(slab, int) and slab == 0):
                    sp.wait_ge(tile_done, (slab - 1) * 16 + (FIRST + 4 * q + 4))
                sp.dma_start(ring[:, q, :, :], src).then_inc(landed[q], 16)

            def k_chunk(slab, q, w, col):
                chunk(slab, q, w[:, 4 * q:4 * q + 4, bass.ds(col, 512)])

            def row_chunk(slab, q, w, i):
                chunk(slab, q, w[bass.ds(i, 1), :, :, 512 * q:512 * q + 512].squeeze(0)
                      if not isinstance(i, int) else w[i, :, :, 512 * q:512 * q + 512])

            def e_chunk(slab, q, w, e):
                chunk(slab, q, w[bass.ds(e, 1), :, 4 * q:4 * q + 4, :].squeeze(0)
                      if not isinstance(e, int) else w[e, :, 4 * q:4 * q + 4, :])

            xp_rows = a["x_prompt"][0].rearrange("(b p) n -> p b n", p=P)
            sp.dma_start(xtok0[:, 0:2, :], xp_rows).then_inc(x_landed, 16)
            sp.dma_start(xtok0[0:NB, 2, :], a["x_sample"][:, 0, :]).then_inc(x_landed, 16)
            sp.dma_start(dtw[:, :, :], w_in[:, :, DT:DT + HEADS]).then_inc(dtw_landed, 16)

            def rnn_load(i, slab, up):
                for q in range(4):
                    k_chunk(slab, q, w_in, i * 512 + RX)
                if isinstance(i, int) and i == 0:
                    sp.wait_ge(barrier, ENG * 1)
                else:
                    sp.wait_ge(side_full, RNN.full("i3", i - 1))
                for k in range(2):
                    sp.dma_start(lruw[:, k, :, :], lru_w[k][:, bass.ds(i * 4, 4), :]).then_inc(lru_landed, 16)
                for q in range(4):
                    k_chunk(slab + 1, q, w_in, i * 512 + RY)
                if up:
                    for q in range(4):
                        row_chunk(slab + 2, q, w_upr, i - 1)

            rnn_load(0, 0, False)
            with sp.Fori(1, RNN_N) as i:
                rnn_load(i, i * 3 - 1, True)
            for q in range(4):
                row_chunk(BC_SLAB - 1, q, w_upr, RNN_N - 1)
            with sp.Fori(0, BC_N) as i:
                for q in range(4):
                    k_chunk(i + BC_SLAB, q, w_in, i * 512 + (XBC + D_SSM))

            def store_states(g):
                for q in range(4):
                    sp.wait_ge(h_new, g * 4 + (q + 1))
                    sp.dma_start(h1_dram[bass.ds(g * 4 + q, 1), :, :, :].squeeze(0), h_ring[:, q, :, :])\
                        .then_inc(h_stored[q], 16)
                sp.wait_ge(hf_ready, g + 1)
                sp.dma_start(hp_dram[:, bass.ds(g * 4, 4), :], hf[:, :, :]).then_inc(hf_stored, 16)

            def ssd_load(g, slab, first):
                for q in range(4):
                    k_chunk(slab, q, w_in, g * 512 + XBC)
                if first:
                    sp.wait_ge(barrier, ENG * 2)
                else:
                    store_states(g - 1)
                for q in range(4):
                    k_chunk(slab + 1, q, w_in, g * 512 + Z)
                    if not first:
                        sp.wait_ge(h_stored[q], g * 16)
                    sp.dma_start(h_ring[:, q, :, :], h0_dram[bass.ds(g * 4 + q, 1), :, :, :].squeeze(0))\
                        .then_inc(h_landed[q], 16)
                if not first:
                    for q in range(4):
                        row_chunk(slab + 2, q, w_ups, g - 1)

            ssd_load(0, SSD_SLAB, True)
            with sp.Fori(1, GROUPS) as g:
                ssd_load(g, g * 3 + (SSD_SLAB - 1), False)
            for q in range(4):
                row_chunk(GATE_SLAB - 1, q, w_ups, GROUPS - 1)
            store_states(GROUPS - 1)
            with sp.Fori(0, GATE_N) as j:
                for q in range(4):
                    k_chunk(j * 2 + GATE_SLAB, q, w_in, j * 512 + GR)
                for q in range(4):
                    k_chunk(j * 2 + (GATE_SLAB + 1), q, w_in, j * 512 + GS)
            sp.wait_ge(rows_ready, 1)
            for src, dst in ((row_s[0:24, :], o["s_cs"][0].rearrange("b k n -> (b k) n")),
                             (row_s[24:27, :], o["p_cs"][0, 0]),
                             (row_r[0:24, :], o["s_cr"][0].rearrange("b k n -> (b k) n")),
                             (row_r[24:27, :], o["p_cr"][0, 0]),
                             (row_h[0:1, :], o["p_hr"][0]), (row_h[1:9, :], o["s_hr"][0])):
                sp.dma_start(dst, src).then_inc(stored, 16)
            sp.wait_ge(stored, 96)
            sp.wait_ge(barrier, ENG * 4)
            sp.dma_start(xtok[:, 0:2, :], xp_rows).then_inc(x_landed, 16)
            sp.dma_start(xtok[0:NB, 2, :], a["x_sample"][:, 0, :]).then_inc(x_landed, 16)
            with sp.Fori(0, OUT_N) as j:
                for q in range(4):
                    k_chunk(j + OUT_SLAB, q, w_out, j * 512)
            sp.wait_ge(barrier, ENG * 5)
            sp.dma_start(wr[:, :, 0:4], a["w_route_group"][0].rearrange("(k p) n -> p k n", p=P)).then_inc(wr_landed, 16)
            sp.dma_start(wr[:, :, 4:20], a["w_route_expert"][0].rearrange("(k p) n -> p k n", p=P)).then_inc(wr_landed, 16)
            sp.dma_start(br[:, 0:4], a["b_route_group"].broadcast_to([P, 4])).then_inc(wr_landed, 16)
            sp.dma_start(br[:, 4:20], a["b_route_expert"].broadcast_to([P, 16])).then_inc(wr_landed, 16)

            def moe_load(e, slab, first):
                for q in range(4):
                    e_chunk(slab, q, w_gate, e)
                for q in range(4):
                    e_chunk(slab + 1, q, w_up, e)
                if not first:
                    for q in range(4):
                        row_chunk(slab + 2, q, w_down, e - 1)

            moe_load(0, MOE_SLAB, True)
            with sp.Fori(1, EXPERTS) as e:
                moe_load(e, e * 3 + (MOE_SLAB - 1), False)
            for q in range(4):
                row_chunk(MOE_SLAB + 47, q, w_down, EXPERTS - 1)
            sp.wait_ge(ytok_ready, 12)
            sp.dma_start(o["y_p"][0].rearrange("(b p) n -> p b n", p=P), ytok[:, 0:2, :]).then_inc(stored, 16)
            sp.dma_start(o["y_s"][:, 0, :], ytok[0:NB, 2, :]).then_inc(stored, 16)
            sp.wait_ge(stored, 128)
            sp.wait_ge(hf_stored, 16 * GROUPS)
            for q in range(4):
                sp.wait_ge(h_stored[q], 16 * GROUPS)

        @block.tensor
        def _(pe):
            def event(table, name, it=0):
                b = table.bank[name]
                wait_pos(pe, side_free[b], table.earlier(name, it))
                return side[b]

            def k_chunk(slab, rnd, q, rhs):
                pe.wait_ge(landed[q], slab * 16 + 16)
                for j in range(4):
                    if q == 0:
                        wait_pos(pe, acc_free[j], rnd)
                    for k in range(4):
                        mm = pe.matmul(acc[j][:, 0:T], ring[:, q, k, j * P:(j + 1) * P], rhs[:, 4 * q + k, :],
                                       start=(q == 0 and k == 0), stop=(q == 3 and k == 3))
                    mm.then_inc(tile_done, 1)

            def k_slab(slab, rnd, rhs):
                for q in range(4):
                    k_chunk(slab, rnd, q, rhs)

            def row_chunk(slab, rnd, q, rhs):
                pe.wait_ge(landed[q], slab * 16 + 16)
                for j in range(4):
                    wait_pos(pe, acc_free[j], rnd + q)
                    for k in range(4):
                        mm = pe.matmul(acc[j][:, 0:T], ring[:, q, k, j * P:(j + 1) * P], rhs[:, k, :],
                                       start=(k == 0), stop=(k == 3))
                    mm.then_inc(tile_done, 1)

            def norm_sum(table, name, squares, n, count):
                pe.wait_ge(sq_ready, count)
                b = event(table, name)
                for k in range(n):
                    mm = pe.matmul(b[:, 0:T], ones[:, :], squares[:, k, :], start=(k == 0), stop=(k == n - 1))
                mm.then_inc(side_full, 1)

            pe.wait_ge(consts, 4)
            pe.wait_ge(small_landed, 16 * 18)
            b = event(SETUP, "vec")
            for k in range(4):
                n = min(P, NV - k * P)
                mm = pe.transpose(b[:, k * P:k * P + n], vrow[0:n, k, :], ident[0:n, 0:n])
            mm.then_inc(side_full, 1)
            b = event(SETUP, "hr")
            for t in range(ND):
                mm = pe.transpose(b[:, 32 * t:32 * t + 32], hrow_r[0:32, t * P:(t + 1) * P], ident[0:32, 0:32])
            mm.then_inc(side_full, 1)
            for m in range(3):
                b = event(SETUP, f"hs{m}")
                for t in range(16):
                    c = (16 * m + t) * P
                    mm = pe.transpose(b[:, 24 * t:24 * t + 24], hrow_s[0:24, c:c + P], ident[0:24, 0:24])
                mm.then_inc(side_full, 1)
            pe.wait_ge(x_landed, 32)
            for t in range(ND):
                j = t % 4
                wait_pos(pe, xt_done, t - 3)
                for b2, n in ((0, P), (1, P), (2, NB)):
                    mm = pe.transpose(acc[j][:, b2 * P:b2 * P + n], xtok0[0:n, b2, t * P:(t + 1) * P],
                                      ident[0:n, 0:n])
                mm.then_inc(tile_done, 1)
            norm_sum(SETUP, "ss1", sq, ND, 1)
            pe.wait_ge(xn_ready, 1)
            pe.wait_ge(dtw_landed, 16)
            b = event(SETUP, "dt")
            for k in range(ND):
                mm = pe.matmul(b[0:HEADS, 0:T], dtw[:, k, :], xn[:, k, :], start=(k == 0), stop=(k == ND - 1))
            mm.then_inc(side_full, 1)
            pe.wait_ge(tok_ready, 1)
            b = event(SETUP, "dtt")
            for c in range(2):
                pe.transpose(b[:, c * HEADS:(c + 1) * HEADS], dt_f[0:HEADS, c * CH:(c + 1) * CH],
                             ident[0:HEADS, 0:HEADS])
            for c in range(2):
                mm = pe.transpose(b[:, (2 + c) * HEADS:(3 + c) * HEADS], cs_f[0:HEADS, c * CH:(c + 1) * CH],
                                  ident[0:HEADS, 0:HEADS])
            mm.then_inc(side_full, 1)
            b = event(SETUP, "tot")
            mm = pe.matmul(b[:, 0:2 * HEADS], ones[0:HEADS, :], dg[0:HEADS, :, :], start=True, stop=True)
            mm.then_inc(side_full, 1)
            meet(pe, 1)

            def gates(i, k, name):
                for j in range(4):
                    b = event(RNN, f"{name}{j}", i)
                    pe.matmul(b[:, 0:T], lruw[:, k, j, :], cx[:, j, :], start=True, stop=True)\
                        .then_inc(side_full, 1)

            def rnn(i, slab, rnd, up):
                k_slab(slab, rnd, xn)
                k_slab(slab + 1, rnd + 1, xn)
                pe.wait_ge(conv_done, i + 1)
                pe.wait_ge(lru_landed, i * 32 + 32)
                gates(i, 0, "r")
                gates(i, 1, "i")
                if up:
                    pe.wait_ge(y_ready, i)
                    for q in range(4):
                        row_chunk(slab + 2, rnd + 2, q, yr)

            rnn(0, 0, 0, False)
            with pe.Fori(1, RNN_N) as i:
                rnn(i, i * 3 - 1, i * 6 - 4, True)
            pe.wait_ge(y_ready, RNN_N)
            for q in range(4):
                row_chunk(BC_SLAB - 1, BC_ROUND - 4, q, yr)
            with pe.Fori(0, BC_N) as i:
                k_slab(i + BC_SLAB, i + BC_ROUND, xn)
            meet(pe, 2)

            def ssd(g, slab, rnd, up):
                pe.wait_ge(cur_ready, g * 4 + 3)
                b = event(SSD, "G", g)
                for c in range(2):
                    mm = pe.matmul(b[:, c * CH:(c + 1) * CH], bcur[:, c * CH:(c + 1) * CH],
                                   ccur[:, c * CH:(c + 1) * CH], start=True, stop=True)
                mm.then_inc(side_full, 1)

                def cs_rows(k):
                    b = event(SSD, f"cs{k}", g)
                    for m in range(2):
                        mm = pe.matmul(b[:, m * SEQ:(m + 1) * SEQ], sel[0:HEADS, 2 * k + m, :],
                                       cs_f[0:HEADS, :], start=True, stop=True)
                    mm.then_inc(side_full, 1)

                cs_rows(0)
                cs_rows(1)
                k_chunk(slab, rnd, 0, xn)
                cs_rows(2)
                cs_rows(3)
                b = event(SSD, "btok", g)
                for c in range(2):
                    pe.transpose(b[:, c * CH:(c + 1) * CH], bcur[:, c * CH:(c + 1) * CH], ident[:, :])
                pe.transpose(b[0:NB, 2 * CH:3 * CH], bcur[:, SEQ:T], ident[:, :])
                pe.transpose(b[0:NB, 3 * CH:4 * CH], ccur[:, SEQ:T], ident[:, :]).then_inc(side_full, 1)
                b = event(SSD, "sd", g)
                for m in range(4):
                    at = 2 * m * P + HD
                    mm = pe.matmul(b[:, m * 16:(m + 1) * 16], sel[0:HEADS, :, :].rearrange("p h m -> p (h m)")[:, at:at + P],
                                   sd_f[0:HEADS, :], start=True, stop=True)
                mm.then_inc(side_full, 1)
                k_chunk(slab, rnd, 1, xn)
                pe.wait_ge(bcs_ready, g + 1)
                for name, src in (("Bb", bcs), ("Cb", ccs)):
                    for m in range(2):
                        b = event(SSD, f"{name}{m}", g)
                        for n in range(4):
                            mm = pe.matmul(b[:, n * NS:(n + 1) * NS], selb[0:NB, 4 * m + n, :],
                                           src[0:NB, :], start=True, stop=True)
                        mm.then_inc(side_full, 1)
                    if name == "Bb":
                        k_chunk(slab, rnd, 2, xn)
                k_chunk(slab, rnd, 3, xn)
                k_slab(slab + 1, rnd + 1, xn)
                pe.wait_ge(xs_ready, g + 1)
                for c in range(2):
                    b = event(SSD, f"xt{c}", g)
                    for m in range(4):
                        mm = pe.transpose(b[:, m * P:(m + 1) * P], cx[:, m, c * CH:(c + 1) * CH], ident[:, :])
                    mm.then_inc(side_full, 1)
                if up:
                    pe.wait_ge(yn_ready, g)
                    row_chunk(slab + 2, rnd + 2, 0, yn)
                    row_chunk(slab + 2, rnd + 2, 1, yn)
                pe.wait_ge(xd_ready, g + 1)
                b = event(SSD, "st0", g)
                pe.matmul(b[:, :], btok[:, 0, :], xd[2], start=True, stop=True).then_inc(side_full, 1)
                b = event(SSD, "hf", g)
                for m in range(4):
                    pe.matmul(b[:, m * NS:(m + 1) * NS], xd[3][:, m * P:(m + 1) * P], btok[:, 0, :],
                              start=True, stop=False)
                    mm = pe.matmul(b[:, m * NS:(m + 1) * NS], xd[4][:, m * P:(m + 1) * P], btok[:, 1, :],
                                   start=False, stop=True)
                mm.then_inc(side_full, 1)
                if up:
                    row_chunk(slab + 2, rnd + 2, 2, yn)
                pe.wait_ge(m_ready, g + 1)
                pe.wait_ge(cts_ready, g + 1)
                pe.wait_ge(st_ready, g + 1)
                for m in range(2):
                    b = event(SSD, f"y{m}", g)
                    for tt in range(2):
                        for c in range(2):
                            for n in range(2):
                                h = 4 * m + 2 * tt + n
                                to = b[n * HD:(n + 1) * HD, tt * SEQ + c * CH:tt * SEQ + (c + 1) * CH]
                                mm = pe.matmul(to, xd[c][:, h * HD:(h + 1) * HD], dm[c][:, h, :],
                                               start=True, stop=(c == 0))
                                if c == 1:
                                    mm = pe.matmul(to, st0[:, h * HD:(h + 1) * HD], ec[:, h, :],
                                                   start=False, stop=True)
                    mm.then_inc(side_full, 1)
                if up:
                    row_chunk(slab + 2, rnd + 2, 3, yn)
                pe.wait_ge(sqg_ready, g + 1)
                b = event(SSD, "gn", g)
                for m in range(4):
                    mm = pe.matmul(b[:, 0:T], ones[:, :], sq_g[:, m, :], start=(m == 0), stop=(m == 3))
                mm.then_inc(side_full, 1)

            ssd(0, SSD_SLAB, SSD_ROUND, False)
            with pe.Fori(1, GROUPS) as g:
                ssd(g, g * 3 + (SSD_SLAB - 1), g * 6 + (SSD_ROUND - 4), True)
            pe.wait_ge(yn_ready, GROUPS)
            for q in range(4):
                row_chunk(GATE_SLAB - 1, GATE_ROUND - 4, q, yn)
            meet(pe, 3)
            for k in range(20):
                b = event(ROWS, f"row{k}")
                for m in range(4):
                    if k < 12:
                        mm = pe.transpose(b[0:27, m * P:(m + 1) * P], stash_s[:, 4 * k + m, :], ident[:, :])
                    elif k < 16:
                        mm = pe.transpose(b[0:27, m * P:(m + 1) * P], stash_r[:, 4 * (k - 12) + m, :], ident[:, :])
                    else:
                        mm = pe.transpose(b[0:9, m * P:(m + 1) * P], stash_h[:, 4 * (k - 16) + m, :], ident[:, :])
                mm.then_inc(side_full, 1)
            with pe.Fori(0, GATE_N) as j:
                k_slab(j * 2 + GATE_SLAB, j * 2 + GATE_ROUND, xn)
                k_slab(j * 2 + (GATE_SLAB + 1), j * 2 + (GATE_ROUND + 1), xn)
            meet(pe, 4)
            with pe.Fori(0, OUT_N) as j:
                for q in range(3):
                    k_chunk(j + OUT_SLAB, j + OUT_ROUND, q, acc_rnn)
                pe.wait_ge(xtile_ready, j + 1)
                for m in range(4):
                    for b2, n in ((0, P), (1, P), (2, NB)):
                        pe.matmul(acc[m][:, b2 * P:b2 * P + n], xtile[0:n, b2, m * P:(m + 1) * P],
                                  ident[0:n, 0:n], start=False, stop=False)
                k_chunk(j + OUT_SLAB, j + OUT_ROUND, 3, acc_rnn)
            meet(pe, 5)
            norm_sum(ROUTE, "ss2", sq2, ND, 2)
            pe.wait_ge(xn_ready, 2)
            pe.wait_ge(wr_landed, 64)
            b = event(ROUTE, "logit")
            for b2, n in ((0, P), (1, P), (2, NB)):
                for k in range(ND):
                    mm = pe.matmul(b[0:n, 20 * b2:20 * b2 + 20], xn[:, k, b2 * P:b2 * P + n], wr[:, k, :],
                                   start=(k == 0), stop=(k == ND - 1))
            mm.then_inc(side_full, 1)
            pe.wait_ge(comb_ready, 1)
            b = event(ROUTE, "combt")
            for b2, n in ((0, P), (1, P), (2, NB)):
                mm = pe.transpose(b[0:EXPERTS, b2 * P:b2 * P + n], comb[0:n, b2, :], ident[0:n, 0:n])
            mm.then_inc(side_full, 1)

            def expert(e, slab, rnd, down):
                k_slab(slab, rnd, xn)
                pe.wait_ge(sele_ready, e + 1)
                pe.wait_ge(combt_ready, 1)
                b = event(MOE, "cb", e)
                pe.matmul(b[:, 0:T], sel_e[0:EXPERTS, :], comb_t[0:EXPERTS, :], start=True, stop=True)\
                    .then_inc(side_full, 1)
                k_slab(slab + 1, rnd + 1, xn)
                if down:
                    pe.wait_ge(hid_ready, e)
                    for q in range(4):
                        row_chunk(slab + 2, rnd + 2, q, hid)

            expert(0, MOE_SLAB, MOE_ROUND, False)
            with pe.Fori(1, EXPERTS) as e:
                expert(e, e * 3 + (MOE_SLAB - 1), e * 6 + (MOE_ROUND - 4), True)
            pe.wait_ge(hid_ready, EXPERTS)
            for q in range(4):
                row_chunk(MOE_SLAB + 47, MOE_ROUND + 92, q, hid)
            meet(pe, 6)
            norm_sum(FINAL, "ss3", sq2, ND, 3)
            pe.wait_ge(xn_ready, 3)
            for k in range(12):
                b = event(OUTT, f"o{k}")
                b2, n = k // 4, (P, P, NB)[k // 4]
                for m in range(4):
                    t = 4 * (k % 4) + m
                    mm = pe.transpose(b[0:n, m * P:(m + 1) * P], xn[:, t, b2 * P:b2 * P + n], ident[:, :])
                mm.then_inc(side_full, 1)

        def copy_out(eng, dst, src):
            if eng.engine == mybir.EngineType.Activation:
                return eng.activation(dst, src, ACT.Copy)
            return eng.tensor_copy(dst, src)

        def states_stored(eng):
            for q in range(4):
                eng.wait_ge(h_stored[q], 16 * GROUPS)
            eng.wait_ge(hf_stored, 16 * GROUPS)

        def rows_out(eng, k):
            eng.wait_ge(side_full, ROWS.full(f"row{k}"))
            b = ROWS.bank[f"row{k}"]
            if k < 12:
                dst, n = row_s[0:27, k * 512:(k + 1) * 512], 27
            elif k < 16:
                dst, n = row_r[0:27, (k - 12) * 512:(k - 11) * 512], 27
            else:
                dst, n = row_h[0:9, (k - 16) * 512:(k - 15) * 512], 9
            copy_out(eng, dst, side[b][0:n, :]).then_inc(side_free[b], 1)

        def out_rows(eng, k):
            eng.wait_ge(side_full, OUTT.full(f"o{k}"))
            b, n = OUTT.bank[f"o{k}"], (P, P, NB)[k // 4]
            copy_out(eng, ytok[0:n, k // 4, (k % 4) * 512:(k % 4 + 1) * 512], side[b][0:n, :])\
                .then_inc(side_free[b], 1)
            eng.drain().then_inc(ytok_ready, 1)

        @block.scalar
        def _(act):
            def acc_wait(slab, j):
                act.wait_ge(tile_done, slab * 16 + (FIRST + 12 + j + 1))

            def pad_in(c, slab):
                wait_pos(act, conv_done, c)
                wait_pos(act, stash_done, c)
                for j in range(4):
                    acc_wait(slab, j)
                    act.activation(xp[:, j, HIST:S0], acc[j][:, 0:SEQ], ACT.Copy)
                    act.activation(xp[:, j, S0:XPW].rearrange("p (b k) -> p b k", k=TAPS)[:, :, HIST],
                                   acc[j][:, SEQ:T], ACT.Copy).then_inc(acc_free[j], 1)
                act.drain().then_inc(xp_in, 1)

            def squares(dst, src, n):
                for k in range(4):
                    act.activation(dst[:, 4 * k:4 * k + 4, :], src[:, 4 * k:4 * k + 4, :], ACT.Square)
                act.drain().then_inc(sq_ready, 1)

            def root(table, name, n, it=0):
                act.wait_ge(side_full, table.full(name, it))
                act.activation(rs[:, :], side[table.bank[name]][:, 0:T], ACT.Sqrt, bias=eps[:, 0:1],
                               scale=1.0 / n).then_inc(side_free[table.bank[name]], 1)
                act.drain().then_inc(root_ready, 1)

            def rows(dst, src):
                act.dma_start(dst, src).then_inc(small_landed, 16)

            def vrows(col, name, n, view="o (r c) -> (o r) c"):
                v = a[name].rearrange(view, c=P)
                done = 0
                while done < n:
                    k, r = divmod(col + done, P)
                    m = min(n - done, P - r)
                    rows(vrow[r:r + m, k, :], v[done:done + m, :])
                    done += m

            vrows(V_MIX, "norm_mix", 16)
            vrows(V_CRW, "conv_rnn_w", 64, "o k (r c) -> (o k r) c")
            vrows(V_CRB, "conv_rnn_b", 16)
            rows(vrow[V_BA:V_BA + 16, 0, :], a["lru_ba"][0])
            rows(vrow[V_BX:V_BX + 16, 0, :], a["lru_bx"][0])
            vrows(V_LAM, "lru_lambda", 16)
            vrows(V_NSSD, "norm_ssd", 32)
            vrows(V_FFN, "norm_ffn", 16)
            rows(vrow[V_FIN - P:V_FIN - P + 16, 1, :], a["norm_final"].rearrange("(r c) -> r c", c=P))
            vrows(V_CSB, "conv_ssd_b", 48)
            vrows(V_CSW, "conv_ssd_w", 192, "o k (r c) -> (o k r) c")
            rows(hrow_r[0:24, :], a["state_rglru_conv"][0].rearrange("b k n -> (b k) n"))
            rows(hrow_r[24:32, :], a["state_rglru_h"][0])
            rows(hrow_s[0:24, :], a["state_ssd_conv"][0].rearrange("b k n -> (b k) n"))
            rows(dt_b[0:HEADS, :], a["dt_bias"].rearrange("o h -> h o"))
            rows(a_neg[0:HEADS, :], a["a_log"].rearrange("o h -> h o"))
            rows(d_bc[:, :], a["d_skip"].broadcast_to([P, HEADS]))

            for t in range(ND):
                act.wait_ge(tile_done, t + 1)
                act.activation(xT0[:, t, :], acc[t % 4][:, 0:T], ACT.Copy).then_inc(xt_done, 1)
            act.wait_ge(xt_done, ND)
            squares(sq, xT0, 1)
            root(SETUP, "ss1", D)
            act.wait_ge(dve_step, 1)
            act.activation(lm[:, 1, :], lm[:, 0, :], ACT.Exp, scale=-1.0).then_inc(act_step, 1)
            act.wait_ge(small_landed, 16 * 18)
            act.activation(a_neg[0:HEADS, :], a_neg[0:HEADS, :], ACT.Exp).then_inc(act_step, 1)
            act.wait_ge(dve_step, 2)
            act.activation(sm_e[0:HEADS, :], sm_u[0:HEADS, :], ACT.Exp, scale=-1.0).then_inc(act_step, 1)
            act.wait_ge(dve_step, 3)
            act.activation(sd_f[0:HEADS, 0:NB], sm_r[0:HEADS, SEQ:T], ACT.Exp).then_inc(act_step, 1)
            act.wait_ge(dve_step, 4)
            act.activation(wts[:, 2:5, :], wts[:, 2:5, :], ACT.Exp).then_inc(act_step, 1)
            meet(act, 1)

            def rnn(i, slab):
                pad_in(i, slab)
                wait_pos(act, y_ready, i)
                for j in range(4):
                    acc_wait(slab + 1, j)
                    act.activation(ge[:, j, :], acc[j][:, 0:T], ACT.Gelu_apprx_tanh).then_inc(acc_free[j], 1)
                act.drain().then_inc(gelu_ready, 1)
                for name, dst, col in (("r", gr, V_BA), ("i", gi, V_BX)):
                    for j in range(4):
                        act.wait_ge(side_full, RNN.full(f"{name}{j}", i))
                        act.activation(dst[:, j, :], side[j][:, 0:T], ACT.Sigmoid,
                                       bias=vec[:, bass.ds(i * 4 + (col + j), 1)]).then_inc(side_free[j], 1)
                act.drain().then_inc(gates_ready, 1)
                for j in range(4):
                    act.activation(ga[:, j, :], gr[:, j, :], ACT.Exp, scale=c8[:, 0, bass.ds(i * 4 + j, 1)])
                for j in range(4):
                    act.activation(gt[:, j, :], gr[:, j, :], ACT.Tanh, scale=c8[:, 1, bass.ds(i * 4 + j, 1)])
                act.drain().then_inc(decay_ready, 1)
                act.wait_ge(m2_ready, i + 1)
                act.activation(gm[:, :, :], gm[:, :, :], ACT.Sqrt, scale=2.0).then_inc(mult_ready, 1)

            rnn(0, 0)
            with act.Fori(1, RNN_N) as i:
                rnn(i, i * 3 - 1)
            with act.Fori(0, BC_N) as i:
                pad_in(i + RNN_N, i + BC_SLAB)
                act.wait_ge(conv_done, i + (RNN_N + 1))
                act.activation(bc[:, bass.ds(i * 4, 4), :], cx[:, :, :], ACT.Silu).then_inc(bc_ready, 1)
            meet(act, 2)

            def ssd(g, slab, first):
                if not first:
                    act.wait_ge(side_full, SSD.full("y1", g - 1))
                for k in range(4):
                    act.wait_ge(diffed, g * 4 + (k + 1))
                    b = SSD.bank[f"cs{k}"]
                    act.activation(ec[:, 2 * k:2 * k + 2, :],
                                   side[b][:, :].rearrange("p (h l) -> p h l", h=2)[:, :, CH:SEQ],
                                   ACT.Exp).then_inc(side_free[b], 1)
                act.drain().then_inc(ecs_ready, 1)
                for c in range(2):
                    act.activation(dm[c], dm[c], ACT.Exp).then_inc(exp_ready, 1)
                for name, dst in (("Bb", bb), ("Cb", cb)):
                    for m in range(2):
                        act.wait_ge(side_full, SSD.full(f"{name}{m}", g))
                        b = SSD.bank[f"{name}{m}"]
                        act.activation(dst[:, 4 * m:4 * m + 4, :], side[b][:, :].rearrange("p (b n) -> p b n", b=4),
                                       ACT.Copy).then_inc(side_free[b], 1)
                act.drain().then_inc(bcb_ready, 1)
                pad_in(g + (RNN_N + BC_N), slab)
                act.wait_ge(conv_done, g + (RNN_N + BC_N + 1))
                act.activation(cx[:, :, :], cx[:, :, :], ACT.Silu).then_inc(xs_ready, 1)
                wait_pos(act, yz_ready, g)
                for j in range(4):
                    acc_wait(slab + 1, j)
                    act.activation(sz[:, j, :], acc[j][:, 0:T], ACT.Silu).then_inc(acc_free[j], 1)
                act.drain().then_inc(sz_ready, 1)
                act.wait_ge(yz_ready, g + 1)
                act.wait_ge(side_full, SSD.full("y1", g))
                act.activation(sq_g, yv, ACT.Square).then_inc(sqg_ready, 1)
                root(SSD, "gn", 4 * P, g)

            ssd(0, SSD_SLAB, True)
            with act.Fori(1, GROUPS) as g:
                ssd(g, g * 3 + (SSD_SLAB - 1), False)
            meet(act, 3)
            states_stored(act)
            for k in range(1, 20, 2):
                rows_out(act, k)

            def sigmoids(slab, dst):
                for j in range(4):
                    acc_wait(slab, j)
                    act.activation(dst[:, j, :], acc[j][:, 0:T], ACT.Sigmoid).then_inc(acc_free[j], 1)
                act.drain().then_inc(sg_ready, 1)

            with act.Fori(0, GATE_N) as j:
                act.wait_ge(merged_ready, j + 1)
                sigmoids(j * 2 + GATE_SLAB, g1)
                sigmoids(j * 2 + (GATE_SLAB + 1), g2)
            meet(act, 4)
            meet(act, 5)
            squares(sq2, xres, 2)
            root(ROUTE, "ss2", D)
            act.wait_ge(dve_step, 5)
            act.activation(rt[0], rt[0], ACT.Exp).then_inc(act_step, 1)

            def expert(e, slab):
                wait_pos(act, hid_ready, e)
                for j in range(4):
                    acc_wait(slab, j)
                    act.activation(hg[:, j, :], acc[j][:, 0:T], ACT.Silu).then_inc(acc_free[j], 1)
                act.drain().then_inc(hg_ready, 1)
                act.wait_ge(side_full, MOE.full("cb", e))
                act.activation(cbs[:, :], side[3][:, 0:T], ACT.Copy).then_inc(side_free[3], 1)
                act.drain().then_inc(cb_ready, 1)

            expert(0, MOE_SLAB)
            with act.Fori(1, EXPERTS) as e:
                expert(e, e * 3 + (MOE_SLAB - 1))
            meet(act, 6)
            squares(sq2, xres, 3)
            root(FINAL, "ss3", D)
            for k in range(1, 12, 2):
                out_rows(act, k)

        @block.vector
        def _(dve):
            def acc_wait(slab, q, j):
                dve.wait_ge(tile_done, slab * 16 + (FIRST + 4 * q + j + 1))

            def free(table, name):
                return side_free[table.bank[name]]

            def evac(table, name, it, dst, src):
                dve.wait_ge(side_full, table.full(name, it))
                dve.tensor_copy(dst, src).then_inc(free(table, name), 1)

            def conv(c, w_col, w_step, b_col):
                dve.wait_ge(xp_in, c + 1)
                dve.wait_ge(hist_in, c + 1)

                def tap(k, j):
                    return vec[:, bass.ds(w_col + (k * w_step + j), 1)]

                for j in range(4):
                    dve.tensor_scalar(cv[:, j, :], xp[:, j, 0:CVW], tap(0, j), vec[:, bass.ds(b_col + j, 1)],
                                      ALU.mult, ALU.add)
                for k in (1, 2):
                    dve.drain()
                    for j in range(4):
                        dve.scalar_tensor_tensor(cv[:, j, :], xp[:, j, k:k + CVW], tap(k, j), cv[:, j, :],
                                                 ALU.mult, ALU.add)
                dve.drain()
                for j in range(4):
                    dve.scalar_tensor_tensor(cx[:, j, 0:SEQ], xp[:, j, 3:3 + SEQ], tap(3, j), cv[:, j, 0:SEQ],
                                             ALU.mult, ALU.add)
                    dve.scalar_tensor_tensor(
                        cx[:, j, SEQ:T],
                        xp[:, j, S0:XPW].rearrange("p (b k) -> p b k", k=TAPS)[:, :, HIST], tap(3, j),
                        cvs(j), ALU.mult, ALU.add)
                dve.drain().then_inc(conv_done, 1)

            def cvs(j):
                return cv[:, j, S0:CVW:TAPS]

            def add_round(slab, q, dst):
                for j in range(4):
                    acc_wait(slab, q, j)
                    dve.tensor_tensor(dst[:, 4 * q + j, :], dst[:, 4 * q + j, :], acc[j][:, 0:T], ALU.add)\
                        .then_inc(acc_free[j], 1)

            def norm_scale(count, src, dst, gain, n=ND):
                dve.wait_ge(root_ready, count)
                dve.reciprocal(rs[:, :], rs[:, :])
                dve.drain()
                for t in range(n):
                    dve.scalar_tensor_tensor(dst[:, t, :], src[:, t, :], gain(t), rs[:, :], ALU.mult, ALU.mult)

            def softplus(dst, v, u, e, r, s2, p, wait):
                dve.scalar_tensor_tensor(u, v, -1.0, v, ALU.mult, ALU.max).then_inc(dve_step, 1)
                dve.wait_ge(act_step, wait)
                dve.tensor_scalar(r, e, 2.0, None, ALU.add)
                dve.drain()
                dve.reciprocal(r, r)
                dve.drain()
                dve.tensor_tensor(r, r, e, ALU.mult)
                dve.drain()
                dve.tensor_tensor(s2, r, r, ALU.mult)
                dve.drain()
                dve.tensor_scalar(p, s2, 1.0 / 17, None, ALU.mult)
                for k in (15, 13, 11, 9, 7, 5, 3):
                    dve.drain()
                    dve.scalar_tensor_tensor(p, p, 1.0 / k, s2, ALU.add, ALU.mult)
                dve.drain()
                dve.scalar_tensor_tensor(p, p, 1.0, r, ALU.add, ALU.mult)
                dve.tensor_scalar(u, v, 0.0, None, ALU.max)
                dve.drain()
                dve.scalar_tensor_tensor(dst, p, 2.0, u, ALU.mult, ALU.add)
                dve.drain()

            dve.wait_ge(side_full, SETUP.full("vec"))
            dve.tensor_copy(vec[:, :], side[0][:, 0:NV]).then_inc(side_free[0], 1)
            evac(SETUP, "hr", 0, hist_r[:, :, :], side[1][:, :].rearrange("p (t n) -> p t n", n=32))
            for m in range(3):
                evac(SETUP, f"hs{m}", 0, hist_s[:, 16 * m:16 * m + 16, 0:24],
                     side[(2, 3, 0)[m]][:, 0:384].rearrange("p (t n) -> p t n", n=24))
            dve.drain()
            dve.wait_ge(small_landed, 16 * 18)
            dve.tensor_copy(d_col[0:HD, :], d_bc[0:HD, 0:HEADS:2])
            dve.tensor_copy(d_col[HD:P, :], d_bc[HD:P, 1:HEADS:2])
            norm_scale(1, xT0, xn, lambda t: vec[:, V_MIX + t:V_MIX + t + 1])
            dve.drain().then_inc(xn_ready, 1)
            dve.tensor_scalar(lm[:, 4, :], vec[:, V_LAM:V_LAM + ND], -1.0, None, ALU.mult)
            dve.drain()
            softplus(lm[:, 2, :], lm[:, 4, :], lm[:, 0, :], lm[:, 1, :], lm[:, 2, :], lm[:, 3, :],
                     sm_p[:, 0:ND], 1)
            dve.tensor_scalar(c8[:, 0, :], lm[:, 2, :], -8.0, None, ALU.mult)
            dve.tensor_scalar(c8[:, 1, :], lm[:, 2, :], 8.0, None, ALU.mult)
            dve.wait_ge(side_full, SETUP.full("dt"))
            dve.tensor_scalar(sm_s[0:HEADS, :], side[2][0:HEADS, 0:T], dt_b[0:HEADS, :], None, ALU.add)\
                .then_inc(side_free[2], 1)
            dve.drain()
            h = slice(0, HEADS)
            softplus(dt_f[h, :], sm_s[h, :], sm_u[h, :], sm_e[h, :], dt_f[h, :], sm_r[h, :], sm_p[h, :], 3)
            dve.tensor_scalar(a_neg[h, :], a_neg[h, :], -1.0, None, ALU.mult)
            dve.drain()
            dve.tensor_scalar(sm_r[h, :], dt_f[h, :], a_neg[h, :], None, ALU.mult)
            dve.tensor_copy(sd_f[h, NB:2 * NB], dt_f[h, SEQ:T])
            dve.drain().then_inc(dve_step, 1)
            for c in range(2):
                dve.tensor_tensor_scan(cs_f[h, c * CH:(c + 1) * CH], ones[h, :], sm_r[h, c * CH:(c + 1) * CH],
                                       0.0, ALU.mult, ALU.add)
            dve.drain()
            for c in range(2):
                dve.tensor_scalar(dg[h, c, :], ident[h, 0:HEADS], cs_f[h, (c + 1) * CH - 1:(c + 1) * CH], None,
                                  ALU.mult)
            dve.drain().then_inc(tok_ready, 1)
            dve.wait_ge(side_full, SETUP.full("tot"))
            dve.tensor_copy(dt_tok[:, :, :], side[3][:, 0:P].rearrange("p (c h) -> p c h", c=2))
            dve.tensor_copy(cs_tok[:, :, :], side[3][:, P:2 * P].rearrange("p (c h) -> p c h", c=2))\
                .then_inc(side_free[3], 1)
            dve.tensor_copy(tot[:, :, :], side[0][:, 0:P].rearrange("p (c h) -> p c h", c=2))\
                .then_inc(side_free[0], 1)
            dve.drain()
            dve.tensor_tensor(wts[:, 2, :], tot[:, 0, :], cs_tok[:, 0, :], ALU.subtract)
            dve.tensor_tensor(wts[:, 4, :], tot[:, 1, :], cs_tok[:, 1, :], ALU.subtract)
            dve.drain()
            dve.tensor_tensor(wts[:, 3, :], wts[:, 2, :], tot[:, 1, :], ALU.add)
            dve.tensor_copy(wts[:, 0:2, :], dt_tok[:, :, :])
            dve.drain().then_inc(dve_step, 1)
            dve.wait_ge(act_step, 5)
            for k, c in ((2, 0), (3, 0), (4, 1)):
                dve.tensor_tensor(wts[:, k, :], wts[:, k, :], dt_tok[:, c, :], ALU.mult)
            meet(dve, 1)

            def rnn(i, slab, up):
                conv(i, i * 4 + V_CRW, ND, i * 4 + V_CRB)
                if up:
                    add_round(slab + 2, 0, acc_rnn)
                dve.wait_ge(decay_ready, i + 1)
                dve.tensor_scalar(gr[:, :, :], gt[:, :, :], 1.0, None, ALU.add)
                dve.drain()
                dve.reciprocal(gr[:, :, :], gr[:, :, :])
                dve.drain()
                dve.tensor_tensor(gm[:, :, :], gt[:, :, :], gr[:, :, :], ALU.mult)
                dve.drain().then_inc(m2_ready, 1)
                dve.tensor_tensor(gi[:, :, :], gi[:, :, :], cx[:, :, :], ALU.mult)
                if up:
                    add_round(slab + 2, 1, acc_rnn)
                dve.wait_ge(mult_ready, i + 1)
                dve.memset(gm[:, :, 0:1], 1.0)
                dve.drain()
                dve.tensor_tensor(gi[:, :, :], gi[:, :, :], gm[:, :, :], ALU.mult)
                dve.tensor_tensor(gs[:, :, :], ga[:, :, SEQ:T], hist_r[:, bass.ds(i * 4, 4), 24:32], ALU.mult)
                dve.drain()
                wait_pos(dve, h_stashed, i)
                for j in range(4):
                    dve.tensor_tensor_scan(hh[:, j, 0:SEQ], ga[:, j, 0:SEQ], gi[:, j, 0:SEQ], 0.0,
                                           ALU.mult, ALU.add)
                dve.tensor_tensor(hh[:, :, SEQ:T], gs[:, :, :], gi[:, :, SEQ:T], ALU.add)
                dve.drain()
                if up:
                    add_round(slab + 2, 2, acc_rnn)
                    add_round(slab + 2, 3, acc_rnn)
                dve.wait_ge(gelu_ready, i + 1)
                dve.tensor_tensor(yr[:, :, :], hh[:, :, :], ge[:, :, :], ALU.mult).then_inc(y_ready, 1)

            rnn(0, 0, False)
            with dve.Fori(1, RNN_N) as i:
                rnn(i, i * 3 - 1, True)
            for q in range(4):
                add_round(BC_SLAB - 1, q, acc_rnn)
            conv(RNN_N, V_CSW + 32, NX, V_CSB + 32)
            with dve.Fori(1, BC_N) as i:
                dve.wait_ge(bc_ready, i)
                conv(i + RNN_N, i * 4 + (V_CSW + 32), NX, i * 4 + (V_CSB + 32))
            meet(dve, 2)

            def ssd(g, slab, up):
                dve.wait_ge(side_full, SSD.full("G", g))
                dve.tensor_tensor(gtm[:, :, :], side[0][:, 0:2 * CH].rearrange("p (c l) -> p c l", c=2),
                                  mask[:, :].unsqueeze(1).broadcast_to([P, 2, CH]), ALU.mult)\
                    .then_inc(side_free[0], 1)
                dve.wait_ge(cur_ready, g * 4 + 4)
                for k in range(4):
                    dve.wait_ge(side_full, SSD.full(f"cs{k}", g))
                    b = SSD.bank[f"cs{k}"]
                    for m in range(2):
                        for c in range(2):
                            dve.tensor_scalar(dm[c][:, 2 * k + m, :],
                                              side[b][:, m * SEQ + c * CH:m * SEQ + (c + 1) * CH],
                                              cur_cs[:, c, 2 * k + m:2 * k + m + 1], 0.0,
                                              ALU.subtract, ALU.min)
                    dve.drain().then_inc(diffed, 1)
                dve.wait_ge(side_full, SSD.full("btok", g))
                dve.tensor_copy(bcs[0:NB, :], side[0][0:NB, 2 * CH:3 * CH])
                dve.tensor_copy(ccs[0:NB, :], side[0][0:NB, 3 * CH:4 * CH])
                dve.tensor_copy(btok[:, :, :], side[0][:, 0:2 * CH].rearrange("p (c n) -> p c n", c=2))\
                    .then_inc(side_free[0], 1)
                dve.drain().then_inc(bcs_ready, 1)
                evac(SSD, "sd", g, sd[:, :, :], side[3][:, 0:64].rearrange("p (t n) -> p t n", t=4))
                for c in range(2):
                    dve.wait_ge(exp_ready, g * 2 + (c + 1))
                    dve.tensor_tensor(dm[c], dm[c], gtm[:, c, :].unsqueeze(1).broadcast_to([P, HG, CH]), ALU.mult)
                dve.drain().then_inc(m_ready, 1)
                conv(g + (RNN_N + BC_N), g * 4 + V_CSW, NX, g * 4 + V_CSB)
                dve.wait_ge(xs_ready, g + 1)
                dve.tensor_tensor(xdt_s[:, :, :], cx[:, :, SEQ:T], sd[:, :, NB:2 * NB], ALU.mult)\
                    .then_inc(xdts_ready, 1)
                dve.wait_ge(bcb_ready, g + 1)

                def decode(q):
                    dve.wait_ge(h_landed[q], g * 16 + 16)
                    hq, u = h_ring[:, q, :, :], ub[q % 2]
                    dve.tensor_tensor(hq, hq, sd[:, q, 0:NB].unsqueeze(2).broadcast_to([P, NB, NS]), ALU.mult)
                    dve.drain()
                    dve.wait_ge(u_ready, g * 4 + (q + 1))
                    dve.tensor_tensor(hq, hq, u, ALU.add)
                    dve.drain()
                    dve.tensor_tensor(u, hq, cb, ALU.mult)
                    dve.drain()
                    dve.tensor_reduce(ys[:, q, :], u, AX.X, ALU.add).then_inc(h_new, 1)

                for q in range(3):
                    decode(q)
                wait_pos(dve, hf_stored, g * 16)
                for c, ks in ((0, (0, 2, 3)), (1, (1, 4))):
                    dve.wait_ge(side_full, SSD.full(f"xt{c}", g))
                    b = SSD.bank[f"xt{c}"]
                    for k in ks:
                        ins = dve.tensor_tensor(
                            xd[k].rearrange("p (h n) -> p h n", h=HG), side[b][:, :].rearrange("p (h n) -> p h n", h=HG),
                            cur_w[:, k, :].unsqueeze(2).broadcast_to([P, HG, HD]), ALU.mult)
                    ins.then_inc(side_free[b], 1)
                dve.drain().then_inc(xd_ready, 1)
                if up:
                    add_round(slab + 2, 0, acc_ssd)
                decode(3)
                if up:
                    add_round(slab + 2, 1, acc_ssd)
                dve.wait_ge(side_full, SSD.full("st0", g))
                dve.tensor_copy(st0, side[1][:, :]).then_inc(side_free[1], 1)
                dve.drain().then_inc(st_ready, 1)
                dve.wait_ge(side_full, SSD.full("hf", g))
                dve.tensor_copy(hf[:, :, :], side[2][:, :].rearrange("p (t n) -> p t n", t=4))\
                    .then_inc(side_free[2], 1)
                dve.drain().then_inc(hf_ready, 1)
                if up:
                    add_round(slab + 2, 2, acc_ssd)
                for m in range(4):
                    if m % 2 == 0:
                        dve.wait_ge(side_full, SSD.full(f"y{m // 2}", g))
                    b = SSD.bank[f"y{m // 2}"]
                    ins = dve.scalar_tensor_tensor(yv[:, m, 0:SEQ], cx[:, m, 0:SEQ], cur_d[:, m:m + 1],
                                                   side[b][:, (m % 2) * SEQ:(m % 2 + 1) * SEQ], ALU.mult, ALU.add)
                    if m % 2 == 1:
                        ins.then_inc(side_free[b], 1)
                    dve.scalar_tensor_tensor(yv[:, m, SEQ:T], cx[:, m, SEQ:T], cur_d[:, m:m + 1], ys[:, m, :],
                                             ALU.mult, ALU.add)
                dve.drain()
                dve.wait_ge(sz_ready, g + 1)
                dve.tensor_tensor(yv, yv, sz[:, :, :], ALU.mult).then_inc(yz_ready, 1)
                if up:
                    add_round(slab + 2, 3, acc_ssd)
                norm_scale(g + 2, yv, yn, lambda t: vec[:, bass.ds(g * 4 + (V_NSSD + t), 1)], 4)
                dve.drain().then_inc(yn_ready, 1)

            ssd(0, SSD_SLAB, False)
            with dve.Fori(1, GROUPS) as g:
                ssd(g, g * 3 + (SSD_SLAB - 1), True)
            for q in range(4):
                add_round(GATE_SLAB - 1, q, acc_ssd)
            meet(dve, 3)
            states_stored(dve)
            for k in range(0, 20, 2):
                rows_out(dve, k)
            dve.drain()
            dve.drain().then_inc(merged_ready, 1)
            for n in range(4):
                dve.wait_ge(side_free[n], ROWS.bank_end[n])
            dve.drain().then_inc(rows_ready, 1)
            with dve.Fori(0, GATE_N) as j:
                dve.wait_ge(sg_ready, j * 2 + 1)
                ar, asd = acc_rnn[:, bass.ds(j * 4, 4), :], acc_ssd[:, bass.ds(j * 4, 4), :]
                dve.tensor_tensor(ar, ar, g1[:, :, :], ALU.mult)
                dve.wait_ge(sg_ready, j * 2 + 2)
                dve.tensor_tensor(g2[:, :, :], asd, g2[:, :, :], ALU.mult)
                dve.drain()
                dve.tensor_tensor(ar, ar, g2[:, :, :], ALU.add).then_inc(merged_ready, 1)
            meet(dve, 4)
            with dve.Fori(0, OUT_N) as j:
                for m in range(4):
                    acc_wait(j + OUT_SLAB, 3, m)
                    dve.tensor_copy(xres[:, bass.ds(j * 4 + m, 1), :].squeeze(1), acc[m][:, 0:T])\
                        .then_inc(acc_free[m], 1)
            meet(dve, 5)
            norm_scale(GROUPS + 2, xres, xn, lambda t: vec[:, V_FFN + t:V_FFN + t + 1])
            dve.drain().then_inc(xn_ready, 1)

            def tt(out, x, y, op):
                dve.drain()
                return dve.tensor_tensor(out, x, y, op)

            def first_of(eq, tmp):
                dve.drain()
                dve.tensor_copy(tmp[:, :, 0:1], eq[:, :, 0:1])
                for k in range(1, 4):
                    dve.drain()
                    dve.tensor_tensor(tmp[:, :, 1:2], eq[:, :, k:k + 1], tmp[:, :, 0:1], ALU.is_gt)
                    dve.drain()
                    dve.tensor_tensor(tmp[:, :, 0:1], tmp[:, :, 0:1], eq[:, :, k:k + 1], ALU.max)
                    dve.drain()
                    dve.tensor_copy(eq[:, :, k:k + 1], tmp[:, :, 1:2])
                dve.drain()

            dve.memset(lg[:, :, :], 0.0)
            dve.drain()
            dve.wait_ge(side_full, ROUTE.full("logit"))
            dve.wait_ge(wr_landed, 64)
            for b2, n in ((0, P), (1, P), (2, NB)):
                ins = dve.tensor_tensor(lg[0:n, b2, :], side[1][0:n, 20 * b2:20 * b2 + 20], br[0:n, :], ALU.add)
            ins.then_inc(side_free[1], 1)
            dve.drain()
            gl, el = lg[:, :, 0:4], lg[:, :, 4:20]
            m1, goh, es, oh1, esm, m2, oh2, tmp = [r[:, :, 0:4] for r in rt[1:9]]
            ex = rt[0]

            def wide(x):
                return x[:, :, 0:1].broadcast_to([P, 3, 4])

            dve.tensor_reduce(m1[:, :, 0:1], gl, AX.X, ALU.max)
            tt(goh, gl, wide(m1), ALU.is_equal)
            tt(ex[:, :, 0:4], gl, wide(m1), ALU.subtract)
            first_of(goh, tmp)
            for k in range(4):
                tt(rt[9][:, :, 0:4], el[:, :, 4 * k:4 * k + 4], goh[:, :, k:k + 1].broadcast_to([P, 3, 4]), ALU.mult)
                if k == 0:
                    dve.drain()
                    dve.tensor_copy(es, rt[9][:, :, 0:4])
                else:
                    tt(es, es, rt[9][:, :, 0:4], ALU.add)
            dve.drain()
            dve.tensor_reduce(m2[:, :, 0:1], es, AX.X, ALU.max)
            tt(oh1, es, wide(m2), ALU.is_equal)
            tt(ex[:, :, 4:8], es, wide(m2), ALU.subtract)
            first_of(oh1, tmp)
            dve.tensor_scalar(tmp, oh1, -3.0e38, None, ALU.mult)
            dve.tensor_scalar(esm, oh1, -1.0, 1.0, ALU.mult, ALU.add)
            tt(esm, esm, es, ALU.mult)
            tt(esm, esm, tmp, ALU.add)
            dve.drain()
            dve.tensor_reduce(m2[:, :, 0:1], esm, AX.X, ALU.max)
            tt(oh2, esm, wide(m2), ALU.is_equal)
            first_of(oh2, tmp)
            dve.memset(ex[:, :, 8:16], 0.0)
            dve.drain().then_inc(dve_step, 1)
            dve.wait_ge(act_step, 6)
            dve.tensor_reduce(m1[:, :, 0:1], ex[:, :, 0:4], AX.X, ALU.add)
            dve.tensor_tensor(tmp, oh2, ex[:, :, 4:8], ALU.mult)
            dve.drain()
            dve.tensor_reduce(m1[:, :, 1:2], tmp, AX.X, ALU.add)
            dve.drain()
            dve.tensor_scalar(m1[:, :, 1:2], m1[:, :, 1:2], 1.0, None, ALU.add)
            dve.drain()
            dve.tensor_tensor(m1[:, :, 0:1], m1[:, :, 0:1], m1[:, :, 1:2], ALU.mult)
            dve.drain()
            dve.reciprocal(m1[:, :, 0:1], m1[:, :, 0:1])
            tt(tmp, tmp, oh1, ALU.add)
            tt(tmp, tmp, wide(m1), ALU.mult)
            for k in range(4):
                tt(comb[:, :, 4 * k:4 * k + 4], tmp, goh[:, :, k:k + 1].broadcast_to([P, 3, 4]), ALU.mult)
            dve.drain().then_inc(comb_ready, 1)
            dve.wait_ge(side_full, ROUTE.full("combt"))
            dve.tensor_copy(comb_t[0:EXPERTS, :], side[2][0:EXPERTS, 0:T]).then_inc(side_free[2], 1)
            dve.drain().then_inc(combt_ready, 1)

            def expert(e, slab, down):
                dve.wait_ge(hg_ready, e + 1)
                dve.wait_ge(cb_ready, e + 1)
                dve.tensor_tensor(hg[:, :, :], hg[:, :, :], cbs[:, :].unsqueeze(1).broadcast_to([P, 4, T]), ALU.mult)
                dve.drain()
                for j in range(4):
                    acc_wait(slab + 1, 3, j)
                    dve.tensor_tensor(hg[:, j, :], hg[:, j, :], acc[j][:, 0:T], ALU.mult).then_inc(acc_free[j], 1)
                if down:
                    for q in range(4):
                        add_round(slab + 2, q, xres)
                dve.drain()
                dve.tensor_copy(hid[:, :, :], hg[:, :, :]).then_inc(hid_ready, 1)

            expert(0, MOE_SLAB, False)
            with dve.Fori(1, EXPERTS) as e:
                expert(e, e * 3 + (MOE_SLAB - 1), True)
            for q in range(4):
                add_round(MOE_SLAB + 47, q, xres)
            meet(dve, 6)
            norm_scale(GROUPS + 3, xres, xn, lambda t: vec[:, V_FIN + t:V_FIN + t + 1])
            dve.drain().then_inc(xn_ready, 1)
            for k in range(0, 12, 2):
                out_rows(dve, k)

        @block.gpsimd
        def _(pool):
            pool.memset(ident[:, :], 0.0)
            pool.memset(ones[:, :], 1.0)
            pool.memset(mask[:, :], 1.0)
            pool.memset(eps[:, :], EPS)
            pool.memset(xp[:, :, :], 0.0)
            pool.drain().then_inc(consts, 1)
            pool.wait_ge(consts, 1)
            pool.affine_select(out=ident[:, :], in_=ident[:, :], compare_op=ALU.not_equal, fill=1.0, base=0,
                               pattern=[[-1, P]], channel_multiplier=1).then_inc(consts, 1)
            pool.affine_select(out=mask[:, :], in_=mask[:, :], compare_op=ALU.is_ge, fill=0.0, base=0,
                               pattern=[[1, P]], channel_multiplier=-1).then_inc(consts, 1)
            pool.drain().then_inc(consts, 1)
            pool.wait_ge(xn_ready, 1)
            pool.memset(acc_rnn[:, :, :], 0.0)
            pool.memset(acc_ssd[:, :, :], 0.0)
            meet(pool, 1)

            def hist(c, src):
                wait_pos(pool, conv_done, c)
                pool.tensor_copy(xp[:, :, S0:XPW].rearrange("p t (b k) -> p t b k", k=TAPS)[:, :, :, 0:HIST],
                                 src.rearrange("p t (b k) -> p t b k", k=HIST)).then_inc(hist_in, 1)

            def stash(c, dst):
                pool.wait_ge(hist_in, c + 1)
                pool.wait_ge(xp_in, c + 1)
                pool.sem_inc(stash_begun, 1)
                pool.tensor_copy(dst[:, :, 0:24].rearrange("p t (b k) -> p t b k", k=HIST),
                                 xp[:, :, S0:XPW].rearrange("p t (b k) -> p t b k", k=TAPS)[:, :, :, 1:TAPS])
                pool.tensor_copy(dst[:, :, 24:27], xp[:, :, S0 - HIST:S0])
                pool.drain().then_inc(stash_done, 1)

            def rnn(i):
                t4 = bass.ds(i * 4, 4)
                hist(i, hist_r[:, t4, 0:24])
                stash(i, stash_r[:, t4, :])
                pool.wait_ge(y_ready, i + 1)
                pool.tensor_copy(stash_h[:, t4, :], hh[:, :, SEQ - 1:T]).then_inc(h_stashed, 1)

            rnn(0)
            with pool.Fori(1, RNN_N) as i:
                rnn(i)
            with pool.Fori(0, BC_N) as i:
                t4 = bass.ds(i * 4 + 32, 4)
                hist(i + RNN_N, hist_s[:, t4, 0:24])
                stash(i + RNN_N, stash_s[:, t4, :])
            meet(pool, 2)
            pool.tensor_copy(selb[0:NB, :, :], ident[0:NB, 0:NB].unsqueeze(2).broadcast_to([NB, NB, P]))

            def ssd(g, first):
                t4 = bass.ds(g * 4, 4)
                if not first:
                    pool.wait_ge(side_full, SSD.full("sd", g - 1))
                    pool.wait_ge(xd_ready, g)
                    pool.wait_ge(yz_ready, g)
                pool.tensor_copy(bcur[:, :], bc[:, bass.ds(g, 1), :].squeeze(1)).then_inc(cur_ready, 1)
                pool.tensor_copy(ccur[:, :], bc[:, bass.ds(g + GROUPS, 1), :].squeeze(1)).then_inc(cur_ready, 1)
                pool.tensor_copy(sel[0:HEADS, :, :], ident[0:HEADS, bass.ds(g * HG, HG)].unsqueeze(2)
                                 .broadcast_to([HEADS, HG, P])).then_inc(cur_ready, 1)
                pool.tensor_copy(cur_cs[:, :, :], cs_tok[:, :, bass.ds(g * HG, HG)])
                pool.tensor_copy(cur_d[:, :], d_col[:, t4])
                pool.tensor_copy(cur_w[:, :, :], wts[:, :, bass.ds(g * HG, HG)]).then_inc(cur_ready, 1)
                hist(g + (RNN_N + BC_N), hist_s[:, t4, 0:24])
                pool.wait_ge(ecs_ready, g + 1)
                pool.wait_ge(cur_ready, g * 4 + 2)
                pool.tensor_tensor(ec, ec, ccur[:, CH:SEQ].unsqueeze(1).broadcast_to([P, HG, CH]), ALU.mult)\
                    .then_inc(cts_ready, 1)
                stash(g + (RNN_N + BC_N), stash_s[:, t4, :])
                pool.wait_ge(xdts_ready, g + 1)
                pool.wait_ge(bcb_ready, g + 1)
                for q in range(4):
                    if q >= 2:
                        pool.wait_ge(h_new, g * 4 + (q - 1))
                    elif not first:
                        pool.wait_ge(h_new, g * 4 + (q - 1))
                    pool.tensor_tensor(ub[q % 2], bb, xdt_s[:, q, :].unsqueeze(2).broadcast_to([P, NB, NS]),
                                       ALU.mult).then_inc(u_ready, 1)

            ssd(0, True)
            with pool.Fori(1, GROUPS) as g:
                ssd(g, False)
            meet(pool, 3)
            meet(pool, 4)
            pool.wait_ge(x_landed, 64)
            with pool.Fori(0, OUT_N) as j:
                pool.wait_ge(tile_done, j * 16 + (FIRST + 16 * OUT_SLAB))
                pool.tensor_copy(xtile[:, 0:2, :], xtok[:, 0:2, bass.ds(j * 512, 512)])
                pool.tensor_copy(xtile[0:NB, 2, :], xtok[0:NB, 2, bass.ds(j * 512, 512)])
                pool.drain().then_inc(xtile_ready, 1)
            meet(pool, 5)
            with pool.Fori(0, EXPERTS) as e:
                pool.wait_ge(side_full, e + ROUTE.end)
                pool.tensor_copy(sel_e[0:EXPERTS, :], ident[0:EXPERTS, bass.ds(e, 1)].broadcast_to([EXPERTS, P]))\
                    .then_inc(sele_ready, 1)
            meet(pool, 6)


_INS = ["x_prompt", "x_sample", "state_rglru_conv", "state_rglru_h", "state_ssd_conv", "state_ssd_h",
        "norm_mix", "w_in", "conv_rnn_w", "conv_rnn_b", "lru_wa", "lru_ba", "lru_wx", "lru_bx", "lru_lambda",
        "conv_ssd_w", "conv_ssd_b", "dt_bias", "a_log", "d_skip", "norm_ssd", "w_up_rnn", "w_up_ssd", "w_out",
        "norm_ffn", "w_route_group", "b_route_group", "w_route_expert", "b_route_expert",
        "w_exp_gate", "w_exp_up", "w_exp_down", "norm_final"]
_OUTS = [("y_p", (1, SEQ, D)), ("y_s", (NB, 1, D)),
         ("p_cr", (1, 1, HIST, D)), ("p_hr", (1, 1, D)), ("p_cs", (1, 1, HIST, D_XBC)),
         ("p_hs", (1, 1, HEADS, HD, NS)),
         ("s_cr", (1, NB, HIST, D)), ("s_hr", (1, NB, D)), ("s_cs", (1, NB, HIST, D_XBC)),
         ("s_hs", (1, NB, HEADS, HD, NS))]


def kernel(**inputs):
    import numpy as np
    import concourse.bacc as bacc
    from concourse.bass_utils import run_bass_kernel_spmd

    nc = bacc.Bacc("TRN2", target_bir_lowering=False, num_devices=1)
    arrays, ins, outs = {}, {}, {}
    for name in _INS:
        arr = np.ascontiguousarray(inputs[name])
        arrays[f"in_{name}"] = arr
        ins[name] = nc.dram_tensor(f"in_{name}", arr.shape, mybir.dt.from_np(arr.dtype), kind="ExternalInput").ap()
    for name, shape in _OUTS:
        outs[name] = nc.dram_tensor(f"out_{name}", shape, F32, kind="ExternalOutput").ap()
    build_program(nc, ins, outs)
    r = run_bass_kernel_spmd(nc, [arrays], core_ids=[0])
    return tuple(r.results[0][f"out_{name}"] for name, _ in _OUTS)
```

```python
from contextlib import ExitStack

import concourse.bass as bass
from concourse import mybir
from concourse.alu_op_type import AluOpType as ALU

F32 = mybir.dt.float32
F32R = mybir.dt.float32r
ACT = mybir.ActivationFunctionType
AX = mybir.AxisListType

P = 128
D = 2048
ND = D // P
SEQ = 256
NB = 8
T = SEQ + NB
CH = 128
HEADS, HD, NS, GROUPS = 64, 64, 128, 8
HG = HEADS // GROUPS
D_SSM = HEADS * HD
D_XBC = D_SSM + 2 * GROUPS * NS
NX = D_XBC // P
TAPS = 4
HIST = TAPS - 1
EXPERTS, EG, FE = 16, 4, 512
SLOTS = 64
PAIRS = EXPERTS // 2
MAX_ROUNDS = -(-T // SLOTS)
ROUND_SLABS = 3 * EXPERTS
EPS = 1e-6
XPW = HIST + SEQ + NB * TAPS
CVW = XPW - HIST
S0 = HIST + SEQ

RX, RY, Z, XBC = 0, D, 2 * D, 2 * D + D_SSM
DT = XBC + D_XBC
GR = DT + HEADS
GS = GR + D

V_MIX, V_CRW, V_CRB, V_BA, V_BX = 0, 16, 80, 96, 112
V_LAM, V_NSSD, V_FFN, V_FIN, V_CSB, V_CSW = 128, 144, 176, 192, 208, 256
NV = V_CSW + TAPS * NX

FIRST = ND

RNN_N, BC_N, SSD_N, GATE_N, OUT_N = 4, 4, GROUPS, 4, 4
BC_SLAB, BC_ROUND = 12, 24
SSD_SLAB, SSD_ROUND = 16, 28
GATE_SLAB, GATE_ROUND = 40, 76
OUT_SLAB, OUT_ROUND = 48, 84
MOE_SLAB, MOE_ROUND = 52, 88

RNN_EVENTS = [("r0", 0), ("r1", 1), ("r2", 2), ("r3", 3), ("i0", 0), ("i1", 1), ("i2", 2), ("i3", 3)]
SSD_EVENTS = [("G", 0), ("cs0", 1), ("cs1", 2), ("cs2", 1), ("cs3", 2), ("btok", 0), ("sd", 3),
              ("Bb0", 0), ("Bb1", 3), ("Cb0", 1), ("Cb1", 2), ("xt0", 0), ("xt1", 3),
              ("st0", 1), ("hf", 2), ("y0", 0), ("y1", 3), ("gn", 1)]
ROW_EVENTS = [(f"row{k}", k % 4) for k in range(20)]
OUTT_EVENTS = [(f"o{k}", (k + 1) % 4) for k in range(12)]


class Events:

    def __init__(self, events, before=None, repeats=1):
        self.events, self.repeats = events, repeats
        self.start = before.end if before else 0
        self.bank_start = list(before.bank_end) if before else [0] * 4
        self.index = {n: k for k, (n, _) in enumerate(events)}
        self.bank = dict(events)
        self.per_bank = [sum(b == k for _, b in events) for k in range(4)]
        self.end = self.start + repeats * len(events)
        self.bank_end = [s + repeats * n for s, n in zip(self.bank_start, self.per_bank)]

    def full(self, name, it=0):
        return it * len(self.events) + (self.start + self.index[name] + 1)

    def earlier(self, name, it=0):
        b, k = self.bank[name], self.index[name]
        return it * self.per_bank[b] + (self.bank_start[b] + sum(x == b for _, x in self.events[:k]))


SETUP = Events([("vec", 0), ("hr", 1), ("hs0", 2), ("hs1", 3), ("hs2", 0), ("ss1", 1), ("dt", 2),
                ("dtt", 3), ("tot", 0)])
RNN = Events(RNN_EVENTS, SETUP, RNN_N)
SSD = Events(SSD_EVENTS, RNN, SSD_N)
ROWS = Events(ROW_EVENTS, SSD)
ROUTE = Events([("ss2", 0), ("logit", 1), ("rank", 2)] + [(f"xt{k}", k % 4) for k in range(12)], ROWS)
SCATTER = [(f"S{k}", k % 4) for k in range(ND)]
GATHER = [(f"G{k}", k) for k in range(4)]
MOE_BEGIN = Events(GATHER, ROUTE)
MOE_FIRST = Events([("spread", 0)] + GATHER[:3] + [("hidT", 0)] + GATHER[3:], MOE_BEGIN)
MOE_MID = Events(SCATTER + [("spread", 0)] + GATHER[:3] + [("hidT", 0)] + GATHER[3:], MOE_FIRST, PAIRS - 2)
MOE_LAST = Events(SCATTER + [("spread", 0), ("hidT", 0)], MOE_MID)
MOE_END = Events(SCATTER, MOE_LAST)
ROUND_EVENTS = MOE_END.end - ROUTE.end
ROUND_BANK = [x - y for x, y in zip(MOE_END.bank_end, ROUTE.bank_end)]
GATE0, UP0, GATE1, UP1, DOWN0, DOWN1 = range(0, 24, 4)
PAIR_CHUNKS = 24
TURNS = 6
AHEAD = TURNS // 2
ROUND_CHUNKS = PAIRS * PAIR_CHUNKS
FINAL = Events([("ss3", 0)] + OUTT_EVENTS)


def wait_pos(eng, sem, value):
    if not (isinstance(value, int) and value <= 0):
        eng.wait_ge(sem, value)


def build_program(nc, a, o):
    w_in = a["w_in"][0].rearrange("(k p) n -> p k n", p=P)
    w_upr = a["w_up_rnn"][0].rearrange("(s k p) n -> s p k n", p=P, k=4)
    w_ups = a["w_up_ssd"][0].rearrange("(s k p) n -> s p k n", p=P, k=4)
    w_out = a["w_out"][0].rearrange("(k p) n -> p k n", p=P)
    w_gate = a["w_exp_gate"][0].rearrange("e (k p) n -> e p k n", p=P)
    w_up = a["w_exp_up"][0].rearrange("e (k p) n -> e p k n", p=P)
    w_down = a["w_exp_down"][0].rearrange("e (k p) n -> e p k n", p=P)
    h0_dram = a["state_ssd_h"][0].rearrange("b (t h) p n -> t (h p) b n", h=2)
    h1_dram = o["s_hs"][0].rearrange("b (t h) p n -> t (h p) b n", h=2)
    hp_dram = o["p_hs"][0, 0].rearrange("(t h) p n -> (h p) t n", h=2)
    lru_w = [a[n][0].rearrange("t c d -> c t d") for n in ("lru_wa", "lru_wx")]

    with ExitStack() as ctx:
        def sb(name, *free):
            return ctx.enter_context(nc.sbuf_tensor(name, [P, *free], F32))

        def sem(name):
            return ctx.enter_context(nc.semaphore(name))

        ring = sb("ring", 4, 4, 512)
        big = sb("big", 3 * ND * T)
        part = [big[:, k * ND * T:(k + 1) * ND * T] for k in range(3)]
        acc_rnn, acc_ssd, bc = [p.rearrange("p (t n) -> p t n", n=T) for p in part]
        vec = sb("vec", NV)
        hist_r = sb("hist_r", ND, 32)
        stash_r = sb("stash_r", ND, 27)
        hist_s = sb("hist_s", NX, 27)
        stash_s = hist_s
        stash_h = sb("stash_h", ND, 9)
        ident = sb("ident", P)
        ones = sb("ones", P)
        mask = sb("mask", P)
        eps = sb("eps", 1)
        c8 = sb("c8", 2, ND)
        d_col = sb("d_col", HEADS // 2)
        cs_tok = sb("cs_tok", 2, HEADS)
        wts = sb("wts", 5, HEADS)
        dt_f = sb("dt_f", T)
        cs_f = sb("cs_f", SEQ)
        sd_f = sb("sd_f", 2 * NB)
        rs = sb("rs", T)

        class Scope(ExitStack):

            def take(self, name, *free, dt=F32):
                return self.enter_context(nc.sbuf_tensor(name, [P, *free], dt))

        norm = Scope()
        xn = norm.take("xn", ND, T)
        mixer = Scope()
        xp = mixer.take("xp", 4, XPW)
        cv = mixer.take("cv", 4, CVW)
        cx = mixer.take("cx", 4, T)
        yv = cv[:, :, 0:T]

        with Scope() as s:
            vrow = s.take("vrow", 4, P)
            hrow_r = s.take("hrow_r", D)
            hrow_s = s.take("hrow_s", D_XBC)
            sq = s.take("sq", ND, T)
            dtw = s.take("dtw", ND, HEADS)
            sm_u, sm_e, sm_r, sm_s, sm_p = [s.take(f"sm{k}", T) for k in range(5)]
            dt_b, a_neg, d_bc = s.take("dt_b", 1), s.take("a_neg", 1), s.take("d_bc", HEADS)
            dt_tok, tot, dg = s.take("dt_tok", 2, HEADS), s.take("tot", 2, HEADS), s.take("dg", 2, HEADS)
            lm = s.take("lm", 5, ND)
        xtok0 = big[:, ND * T:ND * T + 3 * D].rearrange("p (b n) -> p b n", n=D)
        xT0 = acc_rnn

        with Scope() as s:
            gr, gi, ga, gt, gm, hh, ge, yr = [s.take(n, 4, T) for n in
                                              ("gr", "gi", "ga", "gt", "gm", "hh", "ge", "yr")]
            lruw = s.take("lruw", 2, 4, P)
            gs = s.take("gs", 4, NB)

        with Scope() as s:
            sz, yn = s.take("sz", 4, T), s.take("yn", 4, T)
            dm2 = s.take("dm2", 2, HG, CH)
            dm = [dm2[:, c, :, :] for c in range(2)]
            sq_g = dm2[:, :, :, :].rearrange("p c h l -> p (c h l)")[:, 0:4 * T].rearrange("p (t n) -> p t n", n=T)
            ec = s.take("ec", HG, CH)[:, :, :]
            bb, cb = s.take("bb", NB, NS)[:, :, :], s.take("cb", NB, NS)[:, :, :]
            h_ring = s.take("h_ring", 4, NB, NS)
            ub = [s.take(f"ub{k}", NB, NS)[:, :, :] for k in range(2)]
            xd = [s.take(f"xd{k}", 512)[:, :] for k in range(5)]
            st0 = s.take("st0", 512)[:, :]
            btok, gtm = s.take("btok", 2, CH), s.take("gtm", 2, CH)
            bcs, ccs = s.take("bcs", P), s.take("ccs", P)
            sel = s.take("sel", HG, P)
            selb = s.take("selb", NB, P)
            bcur, ccur = s.take("bcur", T), s.take("ccur", T)
            hf = xd[3].rearrange("p (t n) -> p t n", n=NS)
            sd = s.take("sd", 4, 2 * NB)
            xdt_s, ys = s.take("xdt_s", 4, NB), s.take("ys", 4, NB)
            cur_cs, cur_w, cur_d = s.take("cur_cs", 2, HG), s.take("cur_w", 5, HG), s.take("cur_d", 4)

        with Scope() as s:
            row_s, row_r, row_h = s.take("row_s", D_XBC), s.take("row_r", D), s.take("row_h", D)
            g1, g2 = s.take("g1", 4, T), s.take("g2", 4, T)
        mixer.close()

        with Scope() as s:
            xtok = s.take("xtok", 3, D)
            xtile = s.take("xtile", 3, 512)

        xres = bc
        sq2 = acc_rnn
        norm.close()
        with Scope() as s:
            w_l, w_h = zip(*[(s.take(f"w_l{k}", 2, 512, dt=F32R), s.take(f"w_h{k}", 2, 512, dt=F32R))
                             for k in range(TURNS)])
            xg_h, xg_l = s.take("xg_h", ND, P, dt=F32R), s.take("xg_l", ND, P, dt=F32R)
            hid_h, hid_l = s.take("hid_h", 4, P, dt=F32R), s.take("hid_l", 4, P, dt=F32R)
            y_h, y_l = s.take("y_h", D, dt=F32R), s.take("y_l", D, dt=F32R)
            wr = s.take("wr", ND, 20)
            br = s.take("br", 20)
            lg = s.take("lg", 3, 20)
            rt = [s.take(f"rt{k}", 3, 16) for k in range(10)]
            comb = s.take("comb", 3, EXPERTS)
            member = s.take("member", 3, EXPERTS)
            slot = s.take("slot", 3, EXPERTS)
            before = s.take("before", P)
            valid = s.take("valid", 3)
            iota = s.take("iota", SLOTS)
            most = s.take("most", 8)
            rounds = s.take("rounds", 1, dt=mybir.dt.int32)
            pick = s.take("pick", 3, 2 * SLOTS)
            spread = s.take("spread", T, dt=F32R)
            w_slot = s.take("w_slot", 1)
        xt = big[:, 0:3 * D].rearrange("p (b n) -> p b n", n=D)
        hgate, hid = big[:, 3 * D:3 * D + FE], big[:, 3 * D + FE:3 * D + 2 * FE]
        ytok = xt

        acc = [ctx.enter_context(nc.psum_tensor(f"acc{j}", [P, 512], F32)) for j in range(4)]
        side = [ctx.enter_context(nc.psum_tensor(f"side{j}", [P, 512], F32)) for j in range(4)]

        landed = [sem(f"chunk_landed{q}") for q in range(4)]
        tile_done = sem("tile_done")
        acc_free = [sem(f"acc_free{j}") for j in range(4)]
        side_full = sem("side_full")
        side_free = [sem(f"side_free{j}") for j in range(4)]
        barrier = sem("barrier")
        x_landed, small_landed = sem("x_landed"), sem("small_landed")
        dtw_landed, lru_landed = sem("dtw_landed"), sem("lru_landed")
        h_landed = [sem(f"h_landed{q}") for q in range(4)]
        h_stored = [sem(f"h_stored{q}") for q in range(4)]
        hf_stored, stored = sem("hf_stored"), sem("stored")
        consts = sem("consts")
        sq_ready, root_ready, xn_ready = sem("sq_ready"), sem("root_ready"), sem("xn_ready")
        xt_done = sem("xt_done")
        hist_in, xp_in, conv_done, stash_done = sem("hist_in"), sem("xp_in"), sem("conv_done"), sem("stash_done")
        stash_begun = sem("stash_begun")
        xt_clear = sem("xt_clear")
        act_step, dve_step = sem("act_step"), sem("dve_step")
        gates_ready, decay_ready = sem("gates_ready"), sem("decay_ready")
        m2_ready, mult_ready, gelu_ready, y_ready = (sem("m2_ready"), sem("mult_ready"), sem("gelu_ready"),
                                                     sem("y_ready"))
        h_stashed = sem("h_stashed")
        bc_ready = sem("bc_ready")
        cur_ready = sem("cur_ready")
        diffed, ecs_ready, cts_ready = sem("diffed"), sem("ecs_ready"), sem("cts_ready")
        exp_ready, m_ready, gt_ready = sem("exp_ready"), sem("m_ready"), sem("gt_ready")
        tok_ready, bcb_ready, bcs_ready = sem("tok_ready"), sem("bcb_ready"), sem("bcs_ready")
        xs_ready, xdts_ready, u_ready = sem("xs_ready"), sem("xdts_ready"), sem("u_ready")
        h_new, xd_ready, st_ready, hf_ready = sem("h_new"), sem("xd_ready"), sem("st_ready"), sem("hf_ready")
        sz_ready, yz_ready, sqg_ready, yn_ready = sem("sz_ready"), sem("yz_ready"), sem("sqg_ready"), sem("yn_ready")
        rows_ready = sem("rows_ready")
        sg_ready, merged_ready, xtile_ready = sem("sg_ready"), sem("merged_ready"), sem("xtile_ready")
        wr_landed, member_ready, rounds_ready = sem("wr_landed"), sem("member_ready"), sem("rounds_ready")
        moe_consts, xt_ready, route_exp = sem("moe_consts"), sem("xt_ready"), sem("route_exp")
        pick_ready, spread_ready = sem("pick_ready"), sem("spread_ready")
        hi_ready, lo_ready = sem("hi_ready"), sem("lo_ready")
        moe_used = sem("moe_used")
        xgh_ready, xg_ready = sem("xgh_ready"), sem("xg_ready")
        hgate_ready, hid_ready = sem("hgate_ready"), sem("hid_ready")
        hidh_ready, hidt_ready = sem("hidh_ready"), sem("hidt_ready")
        yh_ready, y_out = sem("yh_ready"), sem("y_out")
        fin_full, fin_free = sem("fin_full"), [sem(f"fin_free{j}") for j in range(4)]
        fin_sq, fin_root = sem("fin_sq"), sem("fin_root")
        ytok_ready = sem("ytok_ready")

        block = ctx.enter_context(nc.Block())
        ENG = 4

        def meet(eng, n):
            eng.drain().then_inc(barrier, 1)
            eng.wait_ge(barrier, ENG * n)

        @block.sync
        def _(sp):
            def chunk(slab, q, src):
                if not (isinstance(slab, int) and slab == 0):
                    sp.wait_ge(tile_done, (slab - 1) * 16 + (FIRST + 4 * q + 4))
                sp.dma_start(ring[:, q, :, :], src).then_inc(landed[q], 16)

            def k_chunk(slab, q, w, col):
                chunk(slab, q, w[:, 4 * q:4 * q + 4, bass.ds(col, 512)])

            def row_chunk(slab, q, w, i):
                chunk(slab, q, w[bass.ds(i, 1), :, :, 512 * q:512 * q + 512].squeeze(0)
                      if not isinstance(i, int) else w[i, :, :, 512 * q:512 * q + 512])

            def e_chunk(slab, q, w, e):
                chunk(slab, q, w[bass.ds(e, 1), :, 4 * q:4 * q + 4, :].squeeze(0)
                      if not isinstance(e, int) else w[e, :, 4 * q:4 * q + 4, :])

            xp_rows = a["x_prompt"][0].rearrange("(b p) n -> p b n", p=P)
            sp.dma_start(xtok0[:, 0:2, :], xp_rows).then_inc(x_landed, 16)
            sp.dma_start(xtok0[0:NB, 2, :], a["x_sample"][:, 0, :]).then_inc(x_landed, 16)
            sp.dma_start(dtw[:, :, :], w_in[:, :, DT:DT + HEADS]).then_inc(dtw_landed, 16)

            def rnn_load(i, slab, up):
                for q in range(4):
                    k_chunk(slab, q, w_in, i * 512 + RX)
                if isinstance(i, int) and i == 0:
                    sp.wait_ge(barrier, ENG * 1)
                else:
                    sp.wait_ge(side_full, RNN.full("i3", i - 1))
                for k in range(2):
                    sp.dma_start(lruw[:, k, :, :], lru_w[k][:, bass.ds(i * 4, 4), :]).then_inc(lru_landed, 16)
                for q in range(4):
                    k_chunk(slab + 1, q, w_in, i * 512 + RY)
                if up:
                    for q in range(4):
                        row_chunk(slab + 2, q, w_upr, i - 1)

            rnn_load(0, 0, False)
            with sp.Fori(1, RNN_N) as i:
                rnn_load(i, i * 3 - 1, True)
            for q in range(4):
                row_chunk(BC_SLAB - 1, q, w_upr, RNN_N - 1)
            with sp.Fori(0, BC_N) as i:
                for q in range(4):
                    k_chunk(i + BC_SLAB, q, w_in, i * 512 + (XBC + D_SSM))

            def store_states(g):
                for q in range(4):
                    sp.wait_ge(h_new, g * 4 + (q + 1))
                    sp.dma_start(h1_dram[bass.ds(g * 4 + q, 1), :, :, :].squeeze(0), h_ring[:, q, :, :])\
                        .then_inc(h_stored[q], 16)
                sp.wait_ge(hf_ready, g + 1)
                sp.dma_start(hp_dram[:, bass.ds(g * 4, 4), :], hf[:, :, :]).then_inc(hf_stored, 16)

            def ssd_load(g, slab, first):
                for q in range(4):
                    k_chunk(slab, q, w_in, g * 512 + XBC)
                if first:
                    sp.wait_ge(barrier, ENG * 2)
                else:
                    store_states(g - 1)
                for q in range(4):
                    k_chunk(slab + 1, q, w_in, g * 512 + Z)
                    if not first:
                        sp.wait_ge(h_stored[q], g * 16)
                    sp.dma_start(h_ring[:, q, :, :], h0_dram[bass.ds(g * 4 + q, 1), :, :, :].squeeze(0))\
                        .then_inc(h_landed[q], 16)
                if not first:
                    for q in range(4):
                        row_chunk(slab + 2, q, w_ups, g - 1)

            ssd_load(0, SSD_SLAB, True)
            with sp.Fori(1, GROUPS) as g:
                ssd_load(g, g * 3 + (SSD_SLAB - 1), False)
            for q in range(4):
                row_chunk(GATE_SLAB - 1, q, w_ups, GROUPS - 1)
            store_states(GROUPS - 1)
            with sp.Fori(0, GATE_N) as j:
                for q in range(4):
                    k_chunk(j * 2 + GATE_SLAB, q, w_in, j * 512 + GR)
                for q in range(4):
                    k_chunk(j * 2 + (GATE_SLAB + 1), q, w_in, j * 512 + GS)
            sp.wait_ge(rows_ready, 1)
            for src, dst in ((row_s[0:24, :], o["s_cs"][0].rearrange("b k n -> (b k) n")),
                             (row_s[24:27, :], o["p_cs"][0, 0]),
                             (row_r[0:24, :], o["s_cr"][0].rearrange("b k n -> (b k) n")),
                             (row_r[24:27, :], o["p_cr"][0, 0]),
                             (row_h[0:1, :], o["p_hr"][0]), (row_h[1:9, :], o["s_hr"][0])):
                sp.dma_start(dst, src).then_inc(stored, 16)
            sp.wait_ge(stored, 96)
            sp.wait_ge(barrier, ENG * 4)
            sp.dma_start(xtok[:, 0:2, :], xp_rows).then_inc(x_landed, 16)
            sp.dma_start(xtok[0:NB, 2, :], a["x_sample"][:, 0, :]).then_inc(x_landed, 16)
            with sp.Fori(0, OUT_N) as j:
                for q in range(4):
                    k_chunk(j + OUT_SLAB, q, w_out, j * 512)
            sp.wait_ge(barrier, ENG * 5)
            sp.dma_start(wr[:, :, 0:4], a["w_route_group"][0].rearrange("(k p) n -> p k n", p=P)).then_inc(wr_landed, 16)
            sp.dma_start(wr[:, :, 4:20], a["w_route_expert"][0].rearrange("(k p) n -> p k n", p=P)).then_inc(wr_landed, 16)
            sp.dma_start(br[:, 0:4], a["b_route_group"].broadcast_to([P, 4])).then_inc(wr_landed, 16)
            sp.dma_start(br[:, 4:20], a["b_route_expert"].broadcast_to([P, 16])).then_inc(wr_landed, 16)

            def moe_chunk(n, q, src):
                sp.wait_ge(lo_ready, n * 2 - 6)
                sp.dma_start(ring[:, q, :, :], src).then_inc(landed[q], 16)

            def e_src(w, e, q):
                if isinstance(e, int):
                    return w[e, :, 4 * q:4 * q + 4, :]
                return w[bass.ds(e, 1), :, 4 * q:4 * q + 4, :].squeeze(0)

            def d_src(e, q):
                return w_down[bass.ds(e, 1), :, :, 512 * q:512 * q + 512].squeeze(0)

            def pair_load(n, i, skip):
                for k in range(skip, PAIR_CHUNKS):
                    q, e = k % 4, i * 2 + (1 if GATE1 <= k < DOWN0 or k >= DOWN1 else 0)
                    if k >= DOWN0:
                        src = d_src(e, q)
                    else:
                        src = e_src(w_gate if k // 4 in (GATE0 // 4, GATE1 // 4) else w_up, e, q)
                    moe_chunk(n + k, q, src)

            for q in range(4):
                e_chunk(MOE_SLAB, q, w_gate, 0)
            sp.wait_ge(rounds_ready, 1)
            n_rounds = sp.value_load(rounds[0:1, 0:1], min_val=1, max_val=MAX_ROUNDS)
            with sp.Fori(0, n_rounds) as r:
                with sp.If(r > 0):
                    sp.wait_ge(lo_ready, r * (2 * ROUND_CHUNKS))
                    for q in range(4):
                        sp.dma_start(ring[:, q, :, :], e_src(w_gate, 0, q)).then_inc(landed[q], 16)
                pair_load(r * ROUND_CHUNKS, 0, 4)
                with sp.Fori(1, PAIRS) as i:
                    pair_load(r * ROUND_CHUNKS + i * PAIR_CHUNKS, i, 0)
            sp.wait_ge(ytok_ready, 12)
            sp.dma_start(o["y_p"][0].rearrange("(b p) n -> p b n", p=P), ytok[:, 0:2, :]).then_inc(stored, 16)
            sp.dma_start(o["y_s"][:, 0, :], ytok[0:NB, 2, :]).then_inc(stored, 16)
            sp.wait_ge(stored, 128)
            sp.wait_ge(hf_stored, 16 * GROUPS)
            for q in range(4):
                sp.wait_ge(h_stored[q], 16 * GROUPS)

        @block.tensor
        def _(pe):
            def event(table, name, it=0):
                b = table.bank[name]
                wait_pos(pe, side_free[b], table.earlier(name, it))
                return side[b]

            def k_chunk(slab, rnd, q, rhs):
                pe.wait_ge(landed[q], slab * 16 + 16)
                for j in range(4):
                    if q == 0:
                        wait_pos(pe, acc_free[j], rnd)
                    for k in range(4):
                        mm = pe.matmul(acc[j][:, 0:T], ring[:, q, k, j * P:(j + 1) * P], rhs[:, 4 * q + k, :],
                                       start=(q == 0 and k == 0), stop=(q == 3 and k == 3))
                    mm.then_inc(tile_done, 1)

            def k_slab(slab, rnd, rhs):
                for q in range(4):
                    k_chunk(slab, rnd, q, rhs)

            def row_chunk(slab, rnd, q, rhs):
                pe.wait_ge(landed[q], slab * 16 + 16)
                for j in range(4):
                    wait_pos(pe, acc_free[j], rnd + q)
                    for k in range(4):
                        mm = pe.matmul(acc[j][:, 0:T], ring[:, q, k, j * P:(j + 1) * P], rhs[:, k, :],
                                       start=(k == 0), stop=(k == 3))
                    mm.then_inc(tile_done, 1)

            def norm_sum(table, name, squares, n, count):
                pe.wait_ge(sq_ready, count)
                b = event(table, name)
                for k in range(n):
                    mm = pe.matmul(b[:, 0:T], ones[:, :], squares[:, k, :], start=(k == 0), stop=(k == n - 1))
                mm.then_inc(side_full, 1)

            pe.wait_ge(consts, 4)
            pe.wait_ge(small_landed, 16 * 18)
            b = event(SETUP, "vec")
            for k in range(4):
                n = min(P, NV - k * P)
                mm = pe.transpose(b[:, k * P:k * P + n], vrow[0:n, k, :], ident[0:n, 0:n])
            mm.then_inc(side_full, 1)
            b = event(SETUP, "hr")
            for t in range(ND):
                mm = pe.transpose(b[:, 32 * t:32 * t + 32], hrow_r[0:32, t * P:(t + 1) * P], ident[0:32, 0:32])
            mm.then_inc(side_full, 1)
            for m in range(3):
                b = event(SETUP, f"hs{m}")
                for t in range(16):
                    c = (16 * m + t) * P
                    mm = pe.transpose(b[:, 24 * t:24 * t + 24], hrow_s[0:24, c:c + P], ident[0:24, 0:24])
                mm.then_inc(side_full, 1)
            pe.wait_ge(x_landed, 32)
            for t in range(ND):
                j = t % 4
                wait_pos(pe, xt_done, t - 3)
                for b2, n in ((0, P), (1, P), (2, NB)):
                    mm = pe.transpose(acc[j][:, b2 * P:b2 * P + n], xtok0[0:n, b2, t * P:(t + 1) * P],
                                      ident[0:n, 0:n])
                mm.then_inc(tile_done, 1)
            norm_sum(SETUP, "ss1", sq, ND, 1)
            pe.wait_ge(xn_ready, 1)
            pe.wait_ge(dtw_landed, 16)
            b = event(SETUP, "dt")
            for k in range(ND):
                mm = pe.matmul(b[0:HEADS, 0:T], dtw[:, k, :], xn[:, k, :], start=(k == 0), stop=(k == ND - 1))
            mm.then_inc(side_full, 1)
            pe.wait_ge(tok_ready, 1)
            b = event(SETUP, "dtt")
            for c in range(2):
                pe.transpose(b[:, c * HEADS:(c + 1) * HEADS], dt_f[0:HEADS, c * CH:(c + 1) * CH],
                             ident[0:HEADS, 0:HEADS])
            for c in range(2):
                mm = pe.transpose(b[:, (2 + c) * HEADS:(3 + c) * HEADS], cs_f[0:HEADS, c * CH:(c + 1) * CH],
                                  ident[0:HEADS, 0:HEADS])
            mm.then_inc(side_full, 1)
            b = event(SETUP, "tot")
            mm = pe.matmul(b[:, 0:2 * HEADS], ones[0:HEADS, :], dg[0:HEADS, :, :], start=True, stop=True)
            mm.then_inc(side_full, 1)
            meet(pe, 1)

            def gates(i, k, name):
                for j in range(4):
                    b = event(RNN, f"{name}{j}", i)
                    pe.matmul(b[:, 0:T], lruw[:, k, j, :], cx[:, j, :], start=True, stop=True)\
                        .then_inc(side_full, 1)

            def rnn(i, slab, rnd, up):
                k_slab(slab, rnd, xn)
                k_slab(slab + 1, rnd + 1, xn)
                pe.wait_ge(conv_done, i + 1)
                pe.wait_ge(lru_landed, i * 32 + 32)
                gates(i, 0, "r")
                gates(i, 1, "i")
                if up:
                    pe.wait_ge(y_ready, i)
                    for q in range(4):
                        row_chunk(slab + 2, rnd + 2, q, yr)

            rnn(0, 0, 0, False)
            with pe.Fori(1, RNN_N) as i:
                rnn(i, i * 3 - 1, i * 6 - 4, True)
            pe.wait_ge(y_ready, RNN_N)
            for q in range(4):
                row_chunk(BC_SLAB - 1, BC_ROUND - 4, q, yr)
            with pe.Fori(0, BC_N) as i:
                k_slab(i + BC_SLAB, i + BC_ROUND, xn)
            meet(pe, 2)

            def ssd(g, slab, rnd, up):
                pe.wait_ge(cur_ready, g * 4 + 3)
                b = event(SSD, "G", g)
                for c in range(2):
                    mm = pe.matmul(b[:, c * CH:(c + 1) * CH], bcur[:, c * CH:(c + 1) * CH],
                                   ccur[:, c * CH:(c + 1) * CH], start=True, stop=True)
                mm.then_inc(side_full, 1)

                def cs_rows(k):
                    b = event(SSD, f"cs{k}", g)
                    for m in range(2):
                        mm = pe.matmul(b[:, m * SEQ:(m + 1) * SEQ], sel[0:HEADS, 2 * k + m, :],
                                       cs_f[0:HEADS, :], start=True, stop=True)
                    mm.then_inc(side_full, 1)

                cs_rows(0)
                cs_rows(1)
                k_chunk(slab, rnd, 0, xn)
                cs_rows(2)
                cs_rows(3)
                b = event(SSD, "btok", g)
                for c in range(2):
                    pe.transpose(b[:, c * CH:(c + 1) * CH], bcur[:, c * CH:(c + 1) * CH], ident[:, :])
                pe.transpose(b[0:NB, 2 * CH:3 * CH], bcur[:, SEQ:T], ident[:, :])
                pe.transpose(b[0:NB, 3 * CH:4 * CH], ccur[:, SEQ:T], ident[:, :]).then_inc(side_full, 1)
                b = event(SSD, "sd", g)
                for m in range(4):
                    at = 2 * m * P + HD
                    mm = pe.matmul(b[:, m * 16:(m + 1) * 16], sel[0:HEADS, :, :].rearrange("p h m -> p (h m)")[:, at:at + P],
                                   sd_f[0:HEADS, :], start=True, stop=True)
                mm.then_inc(side_full, 1)
                k_chunk(slab, rnd, 1, xn)
                pe.wait_ge(bcs_ready, g + 1)
                for name, src in (("Bb", bcs), ("Cb", ccs)):
                    for m in range(2):
                        b = event(SSD, f"{name}{m}", g)
                        for n in range(4):
                            mm = pe.matmul(b[:, n * NS:(n + 1) * NS], selb[0:NB, 4 * m + n, :],
                                           src[0:NB, :], start=True, stop=True)
                        mm.then_inc(side_full, 1)
                    if name == "Bb":
                        k_chunk(slab, rnd, 2, xn)
                k_chunk(slab, rnd, 3, xn)
                k_slab(slab + 1, rnd + 1, xn)
                pe.wait_ge(xs_ready, g + 1)
                for c in range(2):
                    b = event(SSD, f"xt{c}", g)
                    for m in range(4):
                        mm = pe.transpose(b[:, m * P:(m + 1) * P], cx[:, m, c * CH:(c + 1) * CH], ident[:, :])
                    mm.then_inc(side_full, 1)
                if up:
                    pe.wait_ge(yn_ready, g)
                    row_chunk(slab + 2, rnd + 2, 0, yn)
                    row_chunk(slab + 2, rnd + 2, 1, yn)
                pe.wait_ge(xd_ready, g + 1)
                b = event(SSD, "st0", g)
                pe.matmul(b[:, :], btok[:, 0, :], xd[2], start=True, stop=True).then_inc(side_full, 1)
                b = event(SSD, "hf", g)
                for m in range(4):
                    pe.matmul(b[:, m * NS:(m + 1) * NS], xd[3][:, m * P:(m + 1) * P], btok[:, 0, :],
                              start=True, stop=False)
                    mm = pe.matmul(b[:, m * NS:(m + 1) * NS], xd[4][:, m * P:(m + 1) * P], btok[:, 1, :],
                                   start=False, stop=True)
                mm.then_inc(side_full, 1)
                if up:
                    row_chunk(slab + 2, rnd + 2, 2, yn)
                pe.wait_ge(m_ready, g + 1)
                pe.wait_ge(cts_ready, g + 1)
                pe.wait_ge(st_ready, g + 1)
                for m in range(2):
                    b = event(SSD, f"y{m}", g)
                    for tt in range(2):
                        for c in range(2):
                            for n in range(2):
                                h = 4 * m + 2 * tt + n
                                to = b[n * HD:(n + 1) * HD, tt * SEQ + c * CH:tt * SEQ + (c + 1) * CH]
                                mm = pe.matmul(to, xd[c][:, h * HD:(h + 1) * HD], dm[c][:, h, :],
                                               start=True, stop=(c == 0))
                                if c == 1:
                                    mm = pe.matmul(to, st0[:, h * HD:(h + 1) * HD], ec[:, h, :],
                                                   start=False, stop=True)
                    mm.then_inc(side_full, 1)
                if up:
                    row_chunk(slab + 2, rnd + 2, 3, yn)
                pe.wait_ge(sqg_ready, g + 1)
                b = event(SSD, "gn", g)
                for m in range(4):
                    mm = pe.matmul(b[:, 0:T], ones[:, :], sq_g[:, m, :], start=(m == 0), stop=(m == 3))
                mm.then_inc(side_full, 1)

            ssd(0, SSD_SLAB, SSD_ROUND, False)
            with pe.Fori(1, GROUPS) as g:
                ssd(g, g * 3 + (SSD_SLAB - 1), g * 6 + (SSD_ROUND - 4), True)
            pe.wait_ge(yn_ready, GROUPS)
            for q in range(4):
                row_chunk(GATE_SLAB - 1, GATE_ROUND - 4, q, yn)
            meet(pe, 3)
            for k in range(20):
                b = event(ROWS, f"row{k}")
                for m in range(4):
                    if k < 12:
                        mm = pe.transpose(b[0:27, m * P:(m + 1) * P], stash_s[:, 4 * k + m, :], ident[:, :])
                    elif k < 16:
                        mm = pe.transpose(b[0:27, m * P:(m + 1) * P], stash_r[:, 4 * (k - 12) + m, :], ident[:, :])
                    else:
                        mm = pe.transpose(b[0:9, m * P:(m + 1) * P], stash_h[:, 4 * (k - 16) + m, :], ident[:, :])
                mm.then_inc(side_full, 1)
            with pe.Fori(0, GATE_N) as j:
                k_slab(j * 2 + GATE_SLAB, j * 2 + GATE_ROUND, xn)
                k_slab(j * 2 + (GATE_SLAB + 1), j * 2 + (GATE_ROUND + 1), xn)
            meet(pe, 4)
            with pe.Fori(0, OUT_N) as j:
                for q in range(3):
                    k_chunk(j + OUT_SLAB, j + OUT_ROUND, q, acc_rnn)
                pe.wait_ge(xtile_ready, j + 1)
                for m in range(4):
                    for b2, n in ((0, P), (1, P), (2, NB)):
                        pe.matmul(acc[m][:, b2 * P:b2 * P + n], xtile[0:n, b2, m * P:(m + 1) * P],
                                  ident[0:n, 0:n], start=False, stop=False)
                k_chunk(j + OUT_SLAB, j + OUT_ROUND, 3, acc_rnn)
            meet(pe, 5)
            norm_sum(ROUTE, "ss2", sq2, ND, 2)
            pe.wait_ge(xn_ready, 2)
            pe.wait_ge(wr_landed, 64)
            b = event(ROUTE, "logit")
            for b2, n in ((0, P), (1, P), (2, NB)):
                for k in range(ND):
                    mm = pe.matmul(b[0:n, 20 * b2:20 * b2 + 20], xn[:, k, b2 * P:b2 * P + n], wr[:, k, :],
                                   start=(k == 0), stop=(k == ND - 1))
            mm.then_inc(side_full, 1)
            pe.wait_ge(member_ready, 1)
            pe.wait_ge(moe_consts, 1)
            b = event(ROUTE, "rank")
            for b2 in range(3):
                for b3 in range(b2 + 1):
                    pe.matmul(b[:, 16 * b2:16 * b2 + 16], before[:, :] if b3 == b2 else ones[:, :],
                              member[:, b3, :], start=(b3 == 0), stop=(b3 == b2))
            for b3 in range(3):
                mm = pe.matmul(b[:, 48:64], ones[:, :], member[:, b3, :], start=(b3 == 0), stop=(b3 == 2))
            mm.then_inc(side_full, 1)
            for k in range(12):
                b = event(ROUTE, f"xt{k}")
                b2, n = k // 4, (P, P, NB)[k // 4]
                for m in range(4):
                    mm = pe.transpose(b[0:n, m * P:(m + 1) * P], xn[:, 4 * (k % 4) + m, b2 * P:b2 * P + n],
                                      ident[:, :])
                mm.then_inc(side_full, 1)
            pe.wait_ge(xt_ready, 12)
            pe.wait_ge(rounds_ready, 1)
            n_rounds = pe.value_load(rounds[0:1, 0:1], min_val=1, max_val=MAX_ROUNDS)

            def moe_event(table, name, r, it=0):
                b = table.bank[name]
                pe.wait_ge(side_free[b], r * ROUND_BANK[b] + table.earlier(name, it))
                return side[b]

            def bank(pair_n, k):
                j = {GATE0: 0, UP0: 1, GATE1: 2, UP1: 3}.get(k - k % 4, k % 4)
                if k >= DOWN0 or k % 4 == 0:
                    uses = MOE_ROUND + (0 if k < DOWN0 else 1 if k < DOWN1 else 2)
                    pe.wait_ge(acc_free[j], pair_n * 3 + uses)
                return acc[j]

            def moe_chunk(n, pair_n, k):
                b, q = bank(pair_n, k), k % 4
                down = k >= DOWN0
                for m in range(4):
                    s = (2 * k + m // 2) % TURNS
                    if m % 2 == 0:
                        pe.wait_ge(lo_ready, n * 2 + (2 * k + m // 2 + 1))
                    t = m if down else 4 * q + m
                    x_h, x_l = (hid_h, hid_l) if down else (xg_h, xg_l)
                    first, last = (down or q == 0) and m == 0, (down or q == 3) and m == 3
                    pe.matmul(b[:, :], x_h[:, t, :], w_h[s][:, m % 2, :], start=first, stop=False)
                    pe.matmul(b[:, :], x_h[:, t, :], w_l[s][:, m % 2, :], start=False, stop=False)
                    mm = pe.matmul(b[:, :], x_l[:, t, :], w_h[s][:, m % 2, :], start=False, stop=last)
                    if m % 2 == 1:
                        mm.then_inc(moe_used, 1)

            def gather(table, r, it, gs):
                for g in gs:
                    b = moe_event(table, f"G{g}", r, it)
                    for m in range(4):
                        c = (4 * g + m) * P
                        for b2 in range(3):
                            mm = pe.matmul(b[:, m * P:(m + 1) * P], xt[:, b2, c:c + P], pick[:, b2, :],
                                           start=(b2 == 0), stop=(b2 == 2))
                    mm.then_inc(side_full, 1)

            def scatter(table, r, it, ks):
                for k in ks:
                    b = moe_event(table, f"S{k}", r, it)
                    c = slice(k * P, (k + 1) * P)
                    pe.matmul(b[:, 0:T], y_h[:, c], spread[:, :], start=True, stop=False)
                    pe.matmul(b[:, 0:T], y_l[:, c], spread[:, :], start=False, stop=True).then_inc(side_full, 1)

            def pair(table, r, i, it, first, last):
                done = r * PAIRS + i
                n = r * ROUND_CHUNKS + i * PAIR_CHUNKS
                pe.wait_ge(xg_ready, done * 4 + 4)
                for k in range(PAIR_CHUNKS):
                    if k == DOWN0:
                        if not last:
                            pe.wait_ge(pick_ready, done + 2)
                            gather(table, r, it, range(3))
                        pe.wait_ge(hid_ready, done * 2 + 2)
                        b = moe_event(table, "hidT", r, it)
                        for m in range(4):
                            mm = pe.transpose(b[:, m * P:(m + 1) * P], hid[:, m * P:(m + 1) * P], ident[:, :])
                        mm.then_inc(side_full, 1)
                        if not last:
                            gather(table, r, it, range(3, 4))
                        pe.wait_ge(hidt_ready, done + 1)
                    moe_chunk(n, done, k)
                    if not first and 1 <= k <= 4:
                        if k == 1:
                            pe.wait_ge(y_out, done * 8)
                            pe.wait_ge(spread_ready, done)
                        scatter(table, r, it, range(4 * k - 4, 4 * k))
                    if k == 5:
                        b = moe_event(table, "spread", r, it)
                        for b2, m in ((0, P), (1, P), (2, NB)):
                            pe.transpose(b[:, b2 * P:b2 * P + m], pick[0:m, b2, :], ident[0:m, 0:m])
                        for b2 in range(3):
                            mm = pe.matmul(b[:, T:T + 2], pick[:, b2, :], comb[:, b2, bass.ds(i * 2, 2)],
                                           start=(b2 == 0), stop=(b2 == 2))
                        mm.then_inc(side_full, 1)

            with pe.Fori(0, n_rounds) as r:
                pe.wait_ge(pick_ready, r * PAIRS + 1)
                gather(MOE_BEGIN, r, 0, range(4))
                pair(MOE_FIRST, r, 0, 0, True, False)
                with pe.Fori(1, PAIRS - 1) as i:
                    pair(MOE_MID, r, i, i - 1, False, False)
                pair(MOE_LAST, r, PAIRS - 1, 0, False, True)
                pe.wait_ge(y_out, r * (8 * PAIRS) + 8 * PAIRS)
                pe.wait_ge(spread_ready, r * PAIRS + PAIRS)
                scatter(MOE_END, r, 0, range(ND))
            meet(pe, 6)
            pe.wait_ge(fin_sq, 1)
            for k in range(ND):
                mm = pe.matmul(side[0][:, 0:T], ones[:, :], sq2[:, k, :], start=(k == 0), stop=(k == ND - 1))
            mm.then_inc(fin_full, 1)
            pe.wait_ge(xn_ready, 3)
            for k in range(12):
                b = FINAL.bank[f"o{k}"]
                wait_pos(pe, fin_free[b], FINAL.earlier(f"o{k}"))
                b2, n = k // 4, (P, P, NB)[k // 4]
                for m in range(4):
                    t = 4 * (k % 4) + m
                    mm = pe.transpose(side[b][0:n, m * P:(m + 1) * P], xn[:, t, b2 * P:b2 * P + n], ident[:, :])
                mm.then_inc(fin_full, 1)

        def copy_out(eng, dst, src):
            if eng.engine == mybir.EngineType.Activation:
                return eng.activation(dst, src, ACT.Copy)
            return eng.tensor_copy(dst, src)

        def states_stored(eng):
            for q in range(4):
                eng.wait_ge(h_stored[q], 16 * GROUPS)
            eng.wait_ge(hf_stored, 16 * GROUPS)

        def xt_out(eng, k):
            eng.wait_ge(side_full, ROUTE.full(f"xt{k}"))
            b, n = ROUTE.bank[f"xt{k}"], (P, P, NB)[k // 4]
            copy_out(eng, xt[0:n, k // 4, (k % 4) * 512:(k % 4 + 1) * 512], side[b][0:n, :])\
                .then_inc(side_free[b], 1)
            eng.drain().then_inc(xt_ready, 1)

        def rows_out(eng, k):
            eng.wait_ge(side_full, ROWS.full(f"row{k}"))
            b = ROWS.bank[f"row{k}"]
            if k < 12:
                dst, n = row_s[0:27, k * 512:(k + 1) * 512], 27
            elif k < 16:
                dst, n = row_r[0:27, (k - 12) * 512:(k - 11) * 512], 27
            else:
                dst, n = row_h[0:9, (k - 16) * 512:(k - 15) * 512], 9
            copy_out(eng, dst, side[b][0:n, :]).then_inc(side_free[b], 1)

        def out_rows(eng, k):
            eng.wait_ge(fin_full, FINAL.full(f"o{k}"))
            b, n = FINAL.bank[f"o{k}"], (P, P, NB)[k // 4]
            copy_out(eng, ytok[0:n, k // 4, (k % 4) * 512:(k % 4 + 1) * 512], side[b][0:n, :])\
                .then_inc(fin_free[b], 1)
            eng.drain().then_inc(ytok_ready, 1)

        @block.scalar
        def _(act):
            def acc_wait(slab, j):
                act.wait_ge(tile_done, slab * 16 + (FIRST + 12 + j + 1))

            def pad_in(c, slab):
                wait_pos(act, conv_done, c)
                wait_pos(act, stash_done, c)
                for j in range(4):
                    acc_wait(slab, j)
                    act.activation(xp[:, j, HIST:S0], acc[j][:, 0:SEQ], ACT.Copy)
                    act.activation(xp[:, j, S0:XPW].rearrange("p (b k) -> p b k", k=TAPS)[:, :, HIST],
                                   acc[j][:, SEQ:T], ACT.Copy).then_inc(acc_free[j], 1)
                act.drain().then_inc(xp_in, 1)

            def squares(dst, src, n):
                for k in range(4):
                    act.activation(dst[:, 4 * k:4 * k + 4, :], src[:, 4 * k:4 * k + 4, :], ACT.Square)
                act.drain().then_inc(sq_ready, 1)

            def root(table, name, n, it=0):
                act.wait_ge(side_full, table.full(name, it))
                act.activation(rs[:, :], side[table.bank[name]][:, 0:T], ACT.Sqrt, bias=eps[:, 0:1],
                               scale=1.0 / n).then_inc(side_free[table.bank[name]], 1)
                act.drain().then_inc(root_ready, 1)

            def rows(dst, src):
                act.dma_start(dst, src).then_inc(small_landed, 16)

            def vrows(col, name, n, view="o (r c) -> (o r) c"):
                v = a[name].rearrange(view, c=P)
                done = 0
                while done < n:
                    k, r = divmod(col + done, P)
                    m = min(n - done, P - r)
                    rows(vrow[r:r + m, k, :], v[done:done + m, :])
                    done += m

            vrows(V_MIX, "norm_mix", 16)
            vrows(V_CRW, "conv_rnn_w", 64, "o k (r c) -> (o k r) c")
            vrows(V_CRB, "conv_rnn_b", 16)
            rows(vrow[V_BA:V_BA + 16, 0, :], a["lru_ba"][0])
            rows(vrow[V_BX:V_BX + 16, 0, :], a["lru_bx"][0])
            vrows(V_LAM, "lru_lambda", 16)
            vrows(V_NSSD, "norm_ssd", 32)
            vrows(V_FFN, "norm_ffn", 16)
            rows(vrow[V_FIN - P:V_FIN - P + 16, 1, :], a["norm_final"].rearrange("(r c) -> r c", c=P))
            vrows(V_CSB, "conv_ssd_b", 48)
            vrows(V_CSW, "conv_ssd_w", 192, "o k (r c) -> (o k r) c")
            rows(hrow_r[0:24, :], a["state_rglru_conv"][0].rearrange("b k n -> (b k) n"))
            rows(hrow_r[24:32, :], a["state_rglru_h"][0])
            rows(hrow_s[0:24, :], a["state_ssd_conv"][0].rearrange("b k n -> (b k) n"))
            rows(dt_b[0:HEADS, :], a["dt_bias"].rearrange("o h -> h o"))
            rows(a_neg[0:HEADS, :], a["a_log"].rearrange("o h -> h o"))
            rows(d_bc[:, :], a["d_skip"].broadcast_to([P, HEADS]))

            for t in range(ND):
                act.wait_ge(tile_done, t + 1)
                act.activation(xT0[:, t, :], acc[t % 4][:, 0:T], ACT.Copy).then_inc(xt_done, 1)
            act.wait_ge(xt_done, ND)
            squares(sq, xT0, 1)
            root(SETUP, "ss1", D)
            act.wait_ge(dve_step, 1)
            act.activation(lm[:, 1, :], lm[:, 0, :], ACT.Exp, scale=-1.0).then_inc(act_step, 1)
            act.wait_ge(small_landed, 16 * 18)
            act.activation(a_neg[0:HEADS, :], a_neg[0:HEADS, :], ACT.Exp).then_inc(act_step, 1)
            act.wait_ge(dve_step, 2)
            act.activation(sm_e[0:HEADS, :], sm_u[0:HEADS, :], ACT.Exp, scale=-1.0).then_inc(act_step, 1)
            act.wait_ge(dve_step, 3)
            act.activation(sd_f[0:HEADS, 0:NB], sm_r[0:HEADS, SEQ:T], ACT.Exp).then_inc(act_step, 1)
            act.wait_ge(dve_step, 4)
            act.activation(wts[:, 2:5, :], wts[:, 2:5, :], ACT.Exp).then_inc(act_step, 1)
            meet(act, 1)

            def rnn(i, slab):
                pad_in(i, slab)
                wait_pos(act, y_ready, i)
                for j in range(4):
                    acc_wait(slab + 1, j)
                    act.activation(ge[:, j, :], acc[j][:, 0:T], ACT.Gelu_apprx_tanh).then_inc(acc_free[j], 1)
                act.drain().then_inc(gelu_ready, 1)
                for name, dst, col in (("r", gr, V_BA), ("i", gi, V_BX)):
                    for j in range(4):
                        act.wait_ge(side_full, RNN.full(f"{name}{j}", i))
                        act.activation(dst[:, j, :], side[j][:, 0:T], ACT.Sigmoid,
                                       bias=vec[:, bass.ds(i * 4 + (col + j), 1)]).then_inc(side_free[j], 1)
                act.drain().then_inc(gates_ready, 1)
                for j in range(4):
                    act.activation(ga[:, j, :], gr[:, j, :], ACT.Exp, scale=c8[:, 0, bass.ds(i * 4 + j, 1)])
                for j in range(4):
                    act.activation(gt[:, j, :], gr[:, j, :], ACT.Tanh, scale=c8[:, 1, bass.ds(i * 4 + j, 1)])
                act.drain().then_inc(decay_ready, 1)
                act.wait_ge(m2_ready, i + 1)
                act.activation(gm[:, :, :], gm[:, :, :], ACT.Sqrt, scale=2.0).then_inc(mult_ready, 1)

            rnn(0, 0)
            with act.Fori(1, RNN_N) as i:
                rnn(i, i * 3 - 1)
            with act.Fori(0, BC_N) as i:
                pad_in(i + RNN_N, i + BC_SLAB)
                act.wait_ge(conv_done, i + (RNN_N + 1))
                act.activation(bc[:, bass.ds(i * 4, 4), :], cx[:, :, :], ACT.Silu).then_inc(bc_ready, 1)
            meet(act, 2)

            def ssd(g, slab, first):
                if not first:
                    act.wait_ge(side_full, SSD.full("y1", g - 1))
                for k in range(4):
                    act.wait_ge(diffed, g * 4 + (k + 1))
                    b = SSD.bank[f"cs{k}"]
                    act.activation(ec[:, 2 * k:2 * k + 2, :],
                                   side[b][:, :].rearrange("p (h l) -> p h l", h=2)[:, :, CH:SEQ],
                                   ACT.Exp).then_inc(side_free[b], 1)
                act.drain().then_inc(ecs_ready, 1)
                for c in range(2):
                    act.activation(dm[c], dm[c], ACT.Exp).then_inc(exp_ready, 1)
                for name, dst in (("Bb", bb), ("Cb", cb)):
                    for m in range(2):
                        act.wait_ge(side_full, SSD.full(f"{name}{m}", g))
                        b = SSD.bank[f"{name}{m}"]
                        act.activation(dst[:, 4 * m:4 * m + 4, :], side[b][:, :].rearrange("p (b n) -> p b n", b=4),
                                       ACT.Copy).then_inc(side_free[b], 1)
                act.drain().then_inc(bcb_ready, 1)
                pad_in(g + (RNN_N + BC_N), slab)
                act.wait_ge(conv_done, g + (RNN_N + BC_N + 1))
                act.activation(cx[:, :, :], cx[:, :, :], ACT.Silu).then_inc(xs_ready, 1)
                wait_pos(act, yz_ready, g)
                for j in range(4):
                    acc_wait(slab + 1, j)
                    act.activation(sz[:, j, :], acc[j][:, 0:T], ACT.Silu).then_inc(acc_free[j], 1)
                act.drain().then_inc(sz_ready, 1)
                act.wait_ge(yz_ready, g + 1)
                act.wait_ge(side_full, SSD.full("y1", g))
                act.activation(sq_g, yv, ACT.Square).then_inc(sqg_ready, 1)
                root(SSD, "gn", 4 * P, g)

            ssd(0, SSD_SLAB, True)
            with act.Fori(1, GROUPS) as g:
                ssd(g, g * 3 + (SSD_SLAB - 1), False)
            meet(act, 3)
            states_stored(act)
            for k in range(1, 20, 2):
                rows_out(act, k)

            def sigmoids(slab, dst):
                for j in range(4):
                    acc_wait(slab, j)
                    act.activation(dst[:, j, :], acc[j][:, 0:T], ACT.Sigmoid).then_inc(acc_free[j], 1)
                act.drain().then_inc(sg_ready, 1)

            with act.Fori(0, GATE_N) as j:
                act.wait_ge(merged_ready, j + 1)
                sigmoids(j * 2 + GATE_SLAB, g1)
                sigmoids(j * 2 + (GATE_SLAB + 1), g2)
            meet(act, 4)
            meet(act, 5)
            squares(sq2, xres, 2)
            root(ROUTE, "ss2", D)
            act.wait_ge(dve_step, 5)
            act.activation(rt[0][:, :, :], rt[0][:, :, :], ACT.Exp).then_inc(route_exp, 1)
            act.wait_ge(xt_clear, 1)
            for k in range(1, 12, 2):
                xt_out(act, k)
            act.wait_ge(xt_ready, 12)
            act.wait_ge(rounds_ready, 1)
            n_rounds = act.value_load(rounds[0:1, 0:1], min_val=1, max_val=MAX_ROUNDS)

            def high(n, slab, k, first=False):
                act.wait_ge(landed[k % 4], slab * 16 + (16 * (k // 4) + 16))
                for half in range(2):
                    h = 2 * k + half
                    if not first:
                        act.wait_ge(moe_used, n * 2 + (h - TURNS + 1))
                    act.activation(w_h[h % TURNS][:, :, :], ring[:, k % 4, 2 * half:2 * half + 2, :], ACT.Copy)\
                        .then_inc(hi_ready, 1)

            def gathered(table, r, it, gs):
                for g in gs:
                    act.wait_ge(side_full, r * ROUND_EVENTS + table.full(f"G{g}", it))
                    act.activation(xg_h[:, 4 * g:4 * g + 4, :], side[g][:, :].rearrange("p (t n) -> p t n", n=P),
                                   ACT.Copy).then_inc(xgh_ready, 1)

            def pair(table, r, i, it, last):
                done = r * PAIRS + i
                n = r * ROUND_CHUNKS + i * PAIR_CHUNKS
                slab = r * ROUND_SLABS + i * 6 + MOE_SLAB
                for k in range(PAIR_CHUNKS):
                    if not (last and k >= PAIR_CHUNKS - AHEAD):
                        high(n, slab, k + AHEAD)
                    if k in (GATE0 + 3, GATE1 + 3):
                        half = slice(0, SLOTS) if k < GATE1 else slice(SLOTS, P)
                        j = 0 if k < GATE1 else 2
                        act.wait_ge(moe_used, n * 2 + (2 * k + 2))
                        act.activation(hgate[half, :], acc[j][half, :], ACT.Silu).then_inc(acc_free[j], 1)
                        act.drain().then_inc(hgate_ready, 1)
                    if k == UP1 + 3:
                        if not last:
                            gathered(table, r, it, range(3))
                        act.wait_ge(side_full, r * ROUND_EVENTS + table.full("hidT", it))
                        act.activation(hid_h[:, :, :], side[0][:, :].rearrange("p (t n) -> p t n", n=P), ACT.Copy)\
                            .then_inc(hidh_ready, 1)
                        if not last:
                            gathered(table, r, it, range(3, 4))
                    if k >= DOWN0:
                        half = slice(0, SLOTS) if k < DOWN1 else slice(SLOTS, P)
                        q = k % 4
                        act.wait_ge(spread_ready, done + 1)
                        act.wait_ge(moe_used, n * 2 + (2 * k + 2))
                        act.activation(y_h[half, q * 512:(q + 1) * 512], acc[q][half, :], ACT.Copy,
                                       scale=w_slot[half, 0:1]).then_inc(yh_ready, 1)

            with act.Fori(0, n_rounds) as r:
                act.wait_ge(pick_ready, r * PAIRS + 1)
                for k in range(AHEAD):
                    high(0, r * ROUND_SLABS + MOE_SLAB, k, first=True)
                gathered(MOE_BEGIN, r, 0, range(4))
                pair(MOE_FIRST, r, 0, 0, False)
                with act.Fori(1, PAIRS - 1) as i:
                    pair(MOE_MID, r, i, i - 1, False)
                pair(MOE_LAST, r, PAIRS - 1, 0, True)
            meet(act, 6)
            for k in range(4):
                act.activation(sq2[:, 4 * k:4 * k + 4, :], xres[:, 4 * k:4 * k + 4, :], ACT.Square)
            act.drain().then_inc(fin_sq, 1)
            act.wait_ge(fin_full, 1)
            act.activation(rs[:, :], side[0][:, 0:T], ACT.Sqrt, bias=eps[:, 0:1], scale=1.0 / D)\
                .then_inc(fin_free[0], 1)
            act.drain().then_inc(fin_root, 1)
            for k in range(1, 12, 2):
                out_rows(act, k)

        @block.vector
        def _(dve):
            def acc_wait(slab, q, j):
                dve.wait_ge(tile_done, slab * 16 + (FIRST + 4 * q + j + 1))

            def free(table, name):
                return side_free[table.bank[name]]

            def evac(table, name, it, dst, src):
                dve.wait_ge(side_full, table.full(name, it))
                dve.tensor_copy(dst, src).then_inc(free(table, name), 1)

            def conv(c, w_col, w_step, b_col):
                dve.wait_ge(xp_in, c + 1)
                dve.wait_ge(hist_in, c + 1)

                def tap(k, j):
                    return vec[:, bass.ds(w_col + (k * w_step + j), 1)]

                for j in range(4):
                    dve.tensor_scalar(cv[:, j, :], xp[:, j, 0:CVW], tap(0, j), vec[:, bass.ds(b_col + j, 1)],
                                      ALU.mult, ALU.add)
                for k in (1, 2):
                    dve.drain()
                    for j in range(4):
                        dve.scalar_tensor_tensor(cv[:, j, :], xp[:, j, k:k + CVW], tap(k, j), cv[:, j, :],
                                                 ALU.mult, ALU.add)
                dve.drain()
                for j in range(4):
                    dve.scalar_tensor_tensor(cx[:, j, 0:SEQ], xp[:, j, 3:3 + SEQ], tap(3, j), cv[:, j, 0:SEQ],
                                             ALU.mult, ALU.add)
                    dve.scalar_tensor_tensor(
                        cx[:, j, SEQ:T],
                        xp[:, j, S0:XPW].rearrange("p (b k) -> p b k", k=TAPS)[:, :, HIST], tap(3, j),
                        cvs(j), ALU.mult, ALU.add)
                dve.drain().then_inc(conv_done, 1)

            def cvs(j):
                return cv[:, j, S0:CVW:TAPS]

            def add_round(slab, q, dst):
                for j in range(4):
                    acc_wait(slab, q, j)
                    dve.tensor_tensor(dst[:, 4 * q + j, :], dst[:, 4 * q + j, :], acc[j][:, 0:T], ALU.add)\
                        .then_inc(acc_free[j], 1)

            def norm_scale(count, src, dst, gain, n=ND, root=root_ready):
                dve.wait_ge(root, count)
                dve.reciprocal(rs[:, :], rs[:, :])
                dve.drain()
                for t in range(n):
                    dve.scalar_tensor_tensor(dst[:, t, :], src[:, t, :], gain(t), rs[:, :], ALU.mult, ALU.mult)

            def softplus(dst, v, u, e, r, s2, p, wait):
                dve.scalar_tensor_tensor(u, v, -1.0, v, ALU.mult, ALU.max).then_inc(dve_step, 1)
                dve.wait_ge(act_step, wait)
                dve.tensor_scalar(r, e, 2.0, None, ALU.add)
                dve.drain()
                dve.reciprocal(r, r)
                dve.drain()
                dve.tensor_tensor(r, r, e, ALU.mult)
                dve.drain()
                dve.tensor_tensor(s2, r, r, ALU.mult)
                dve.drain()
                dve.tensor_scalar(p, s2, 1.0 / 17, None, ALU.mult)
                for k in (15, 13, 11, 9, 7, 5, 3):
                    dve.drain()
                    dve.scalar_tensor_tensor(p, p, 1.0 / k, s2, ALU.add, ALU.mult)
                dve.drain()
                dve.scalar_tensor_tensor(p, p, 1.0, r, ALU.add, ALU.mult)
                dve.tensor_scalar(u, v, 0.0, None, ALU.max)
                dve.drain()
                dve.scalar_tensor_tensor(dst, p, 2.0, u, ALU.mult, ALU.add)
                dve.drain()

            dve.wait_ge(side_full, SETUP.full("vec"))
            dve.tensor_copy(vec[:, :], side[0][:, 0:NV]).then_inc(side_free[0], 1)
            evac(SETUP, "hr", 0, hist_r[:, :, :], side[1][:, :].rearrange("p (t n) -> p t n", n=32))
            for m in range(3):
                evac(SETUP, f"hs{m}", 0, hist_s[:, 16 * m:16 * m + 16, 0:24],
                     side[(2, 3, 0)[m]][:, 0:384].rearrange("p (t n) -> p t n", n=24))
            dve.drain()
            dve.wait_ge(small_landed, 16 * 18)
            dve.tensor_copy(d_col[0:HD, :], d_bc[0:HD, 0:HEADS:2])
            dve.tensor_copy(d_col[HD:P, :], d_bc[HD:P, 1:HEADS:2])
            norm_scale(1, xT0, xn, lambda t: vec[:, V_MIX + t:V_MIX + t + 1])
            dve.drain().then_inc(xn_ready, 1)
            dve.tensor_scalar(lm[:, 4, :], vec[:, V_LAM:V_LAM + ND], -1.0, None, ALU.mult)
            dve.drain()
            softplus(lm[:, 2, :], lm[:, 4, :], lm[:, 0, :], lm[:, 1, :], lm[:, 2, :], lm[:, 3, :],
                     sm_p[:, 0:ND], 1)
            dve.tensor_scalar(c8[:, 0, :], lm[:, 2, :], -8.0, None, ALU.mult)
            dve.tensor_scalar(c8[:, 1, :], lm[:, 2, :], 8.0, None, ALU.mult)
            dve.wait_ge(side_full, SETUP.full("dt"))
            dve.tensor_scalar(sm_s[0:HEADS, :], side[2][0:HEADS, 0:T], dt_b[0:HEADS, :], None, ALU.add)\
                .then_inc(side_free[2], 1)
            dve.drain()
            h = slice(0, HEADS)
            softplus(dt_f[h, :], sm_s[h, :], sm_u[h, :], sm_e[h, :], dt_f[h, :], sm_r[h, :], sm_p[h, :], 3)
            dve.tensor_scalar(a_neg[h, :], a_neg[h, :], -1.0, None, ALU.mult)
            dve.drain()
            dve.tensor_scalar(sm_r[h, :], dt_f[h, :], a_neg[h, :], None, ALU.mult)
            dve.tensor_copy(sd_f[h, NB:2 * NB], dt_f[h, SEQ:T])
            dve.drain().then_inc(dve_step, 1)
            for c in range(2):
                dve.tensor_tensor_scan(cs_f[h, c * CH:(c + 1) * CH], ones[h, :], sm_r[h, c * CH:(c + 1) * CH],
                                       0.0, ALU.mult, ALU.add)
            dve.drain()
            for c in range(2):
                dve.tensor_scalar(dg[h, c, :], ident[h, 0:HEADS], cs_f[h, (c + 1) * CH - 1:(c + 1) * CH], None,
                                  ALU.mult)
            dve.drain().then_inc(tok_ready, 1)
            dve.wait_ge(side_full, SETUP.full("tot"))
            dve.tensor_copy(dt_tok[:, :, :], side[3][:, 0:P].rearrange("p (c h) -> p c h", c=2))
            dve.tensor_copy(cs_tok[:, :, :], side[3][:, P:2 * P].rearrange("p (c h) -> p c h", c=2))\
                .then_inc(side_free[3], 1)
            dve.tensor_copy(tot[:, :, :], side[0][:, 0:P].rearrange("p (c h) -> p c h", c=2))\
                .then_inc(side_free[0], 1)
            dve.drain()
            dve.tensor_tensor(wts[:, 2, :], tot[:, 0, :], cs_tok[:, 0, :], ALU.subtract)
            dve.tensor_tensor(wts[:, 4, :], tot[:, 1, :], cs_tok[:, 1, :], ALU.subtract)
            dve.drain()
            dve.tensor_tensor(wts[:, 3, :], wts[:, 2, :], tot[:, 1, :], ALU.add)
            dve.tensor_copy(wts[:, 0:2, :], dt_tok[:, :, :])
            dve.drain().then_inc(dve_step, 1)
            dve.wait_ge(act_step, 5)
            for k, c in ((2, 0), (3, 0), (4, 1)):
                dve.tensor_tensor(wts[:, k, :], wts[:, k, :], dt_tok[:, c, :], ALU.mult)
            meet(dve, 1)

            def rnn(i, slab, up):
                conv(i, i * 4 + V_CRW, ND, i * 4 + V_CRB)
                if up:
                    add_round(slab + 2, 0, acc_rnn)
                dve.wait_ge(decay_ready, i + 1)
                dve.tensor_scalar(gr[:, :, :], gt[:, :, :], 1.0, None, ALU.add)
                dve.drain()
                dve.reciprocal(gr[:, :, :], gr[:, :, :])
                dve.drain()
                dve.tensor_tensor(gm[:, :, :], gt[:, :, :], gr[:, :, :], ALU.mult)
                dve.drain().then_inc(m2_ready, 1)
                dve.tensor_tensor(gi[:, :, :], gi[:, :, :], cx[:, :, :], ALU.mult)
                if up:
                    add_round(slab + 2, 1, acc_rnn)
                dve.wait_ge(mult_ready, i + 1)
                dve.memset(gm[:, :, 0:1], 1.0)
                dve.drain()
                dve.tensor_tensor(gi[:, :, :], gi[:, :, :], gm[:, :, :], ALU.mult)
                dve.tensor_tensor(gs[:, :, :], ga[:, :, SEQ:T], hist_r[:, bass.ds(i * 4, 4), 24:32], ALU.mult)
                dve.drain()
                wait_pos(dve, h_stashed, i)
                for j in range(4):
                    dve.tensor_tensor_scan(hh[:, j, 0:SEQ], ga[:, j, 0:SEQ], gi[:, j, 0:SEQ], 0.0,
                                           ALU.mult, ALU.add)
                dve.tensor_tensor(hh[:, :, SEQ:T], gs[:, :, :], gi[:, :, SEQ:T], ALU.add)
                dve.drain()
                if up:
                    add_round(slab + 2, 2, acc_rnn)
                    add_round(slab + 2, 3, acc_rnn)
                dve.wait_ge(gelu_ready, i + 1)
                dve.tensor_tensor(yr[:, :, :], hh[:, :, :], ge[:, :, :], ALU.mult).then_inc(y_ready, 1)

            rnn(0, 0, False)
            with dve.Fori(1, RNN_N) as i:
                rnn(i, i * 3 - 1, True)
            for q in range(4):
                add_round(BC_SLAB - 1, q, acc_rnn)
            conv(RNN_N, V_CSW + 32, NX, V_CSB + 32)
            with dve.Fori(1, BC_N) as i:
                dve.wait_ge(bc_ready, i)
                conv(i + RNN_N, i * 4 + (V_CSW + 32), NX, i * 4 + (V_CSB + 32))
            meet(dve, 2)

            def ssd(g, slab, up):
                dve.wait_ge(side_full, SSD.full("G", g))
                dve.tensor_tensor(gtm[:, :, :], side[0][:, 0:2 * CH].rearrange("p (c l) -> p c l", c=2),
                                  mask[:, :].unsqueeze(1).broadcast_to([P, 2, CH]), ALU.mult)\
                    .then_inc(side_free[0], 1)
                dve.wait_ge(cur_ready, g * 4 + 4)
                for k in range(4):
                    dve.wait_ge(side_full, SSD.full(f"cs{k}", g))
                    b = SSD.bank[f"cs{k}"]
                    for m in range(2):
                        for c in range(2):
                            dve.tensor_scalar(dm[c][:, 2 * k + m, :],
                                              side[b][:, m * SEQ + c * CH:m * SEQ + (c + 1) * CH],
                                              cur_cs[:, c, 2 * k + m:2 * k + m + 1], 0.0,
                                              ALU.subtract, ALU.min)
                    dve.drain().then_inc(diffed, 1)
                dve.wait_ge(side_full, SSD.full("btok", g))
                dve.tensor_copy(bcs[0:NB, :], side[0][0:NB, 2 * CH:3 * CH])
                dve.tensor_copy(ccs[0:NB, :], side[0][0:NB, 3 * CH:4 * CH])
                dve.tensor_copy(btok[:, :, :], side[0][:, 0:2 * CH].rearrange("p (c n) -> p c n", c=2))\
                    .then_inc(side_free[0], 1)
                dve.drain().then_inc(bcs_ready, 1)
                evac(SSD, "sd", g, sd[:, :, :], side[3][:, 0:64].rearrange("p (t n) -> p t n", t=4))
                for c in range(2):
                    dve.wait_ge(exp_ready, g * 2 + (c + 1))
                    dve.tensor_tensor(dm[c], dm[c], gtm[:, c, :].unsqueeze(1).broadcast_to([P, HG, CH]), ALU.mult)
                dve.drain().then_inc(m_ready, 1)
                conv(g + (RNN_N + BC_N), g * 4 + V_CSW, NX, g * 4 + V_CSB)
                dve.wait_ge(xs_ready, g + 1)
                dve.tensor_tensor(xdt_s[:, :, :], cx[:, :, SEQ:T], sd[:, :, NB:2 * NB], ALU.mult)\
                    .then_inc(xdts_ready, 1)
                dve.wait_ge(bcb_ready, g + 1)

                def decode(q):
                    dve.wait_ge(h_landed[q], g * 16 + 16)
                    hq, u = h_ring[:, q, :, :], ub[q % 2]
                    dve.tensor_tensor(hq, hq, sd[:, q, 0:NB].unsqueeze(2).broadcast_to([P, NB, NS]), ALU.mult)
                    dve.drain()
                    dve.wait_ge(u_ready, g * 4 + (q + 1))
                    dve.tensor_tensor(hq, hq, u, ALU.add)
                    dve.drain()
                    dve.tensor_tensor(u, hq, cb, ALU.mult)
                    dve.drain()
                    dve.tensor_reduce(ys[:, q, :], u, AX.X, ALU.add).then_inc(h_new, 1)

                for q in range(3):
                    decode(q)
                wait_pos(dve, hf_stored, g * 16)
                for c, ks in ((0, (0, 2, 3)), (1, (1, 4))):
                    dve.wait_ge(side_full, SSD.full(f"xt{c}", g))
                    b = SSD.bank[f"xt{c}"]
                    for k in ks:
                        ins = dve.tensor_tensor(
                            xd[k].rearrange("p (h n) -> p h n", h=HG), side[b][:, :].rearrange("p (h n) -> p h n", h=HG),
                            cur_w[:, k, :].unsqueeze(2).broadcast_to([P, HG, HD]), ALU.mult)
                    ins.then_inc(side_free[b], 1)
                dve.drain().then_inc(xd_ready, 1)
                if up:
                    add_round(slab + 2, 0, acc_ssd)
                decode(3)
                if up:
                    add_round(slab + 2, 1, acc_ssd)
                dve.wait_ge(side_full, SSD.full("st0", g))
                dve.tensor_copy(st0, side[1][:, :]).then_inc(side_free[1], 1)
                dve.drain().then_inc(st_ready, 1)
                dve.wait_ge(side_full, SSD.full("hf", g))
                dve.tensor_copy(hf[:, :, :], side[2][:, :].rearrange("p (t n) -> p t n", t=4))\
                    .then_inc(side_free[2], 1)
                dve.drain().then_inc(hf_ready, 1)
                if up:
                    add_round(slab + 2, 2, acc_ssd)
                for m in range(4):
                    if m % 2 == 0:
                        dve.wait_ge(side_full, SSD.full(f"y{m // 2}", g))
                    b = SSD.bank[f"y{m // 2}"]
                    ins = dve.scalar_tensor_tensor(yv[:, m, 0:SEQ], cx[:, m, 0:SEQ], cur_d[:, m:m + 1],
                                                   side[b][:, (m % 2) * SEQ:(m % 2 + 1) * SEQ], ALU.mult, ALU.add)
                    if m % 2 == 1:
                        ins.then_inc(side_free[b], 1)
                    dve.scalar_tensor_tensor(yv[:, m, SEQ:T], cx[:, m, SEQ:T], cur_d[:, m:m + 1], ys[:, m, :],
                                             ALU.mult, ALU.add)
                dve.drain()
                dve.wait_ge(sz_ready, g + 1)
                dve.tensor_tensor(yv, yv, sz[:, :, :], ALU.mult).then_inc(yz_ready, 1)
                if up:
                    add_round(slab + 2, 3, acc_ssd)
                norm_scale(g + 2, yv, yn, lambda t: vec[:, bass.ds(g * 4 + (V_NSSD + t), 1)], 4)
                dve.drain().then_inc(yn_ready, 1)

            ssd(0, SSD_SLAB, False)
            with dve.Fori(1, GROUPS) as g:
                ssd(g, g * 3 + (SSD_SLAB - 1), True)
            for q in range(4):
                add_round(GATE_SLAB - 1, q, acc_ssd)
            meet(dve, 3)
            states_stored(dve)
            for k in range(0, 20, 2):
                rows_out(dve, k)
            dve.drain()
            dve.drain().then_inc(merged_ready, 1)
            for n in range(4):
                dve.wait_ge(side_free[n], ROWS.bank_end[n])
            dve.drain().then_inc(rows_ready, 1)
            with dve.Fori(0, GATE_N) as j:
                dve.wait_ge(sg_ready, j * 2 + 1)
                ar, asd = acc_rnn[:, bass.ds(j * 4, 4), :], acc_ssd[:, bass.ds(j * 4, 4), :]
                dve.tensor_tensor(ar, ar, g1[:, :, :], ALU.mult)
                dve.wait_ge(sg_ready, j * 2 + 2)
                dve.tensor_tensor(g2[:, :, :], asd, g2[:, :, :], ALU.mult)
                dve.drain()
                dve.tensor_tensor(ar, ar, g2[:, :, :], ALU.add).then_inc(merged_ready, 1)
            meet(dve, 4)
            with dve.Fori(0, OUT_N) as j:
                for m in range(4):
                    acc_wait(j + OUT_SLAB, 3, m)
                    dve.tensor_copy(xres[:, bass.ds(j * 4 + m, 1), :].squeeze(1), acc[m][:, 0:T])\
                        .then_inc(acc_free[m], 1)
            meet(dve, 5)
            norm_scale(GROUPS + 2, xres, xn, lambda t: vec[:, V_FFN + t:V_FFN + t + 1])
            dve.drain().then_inc(xn_ready, 1)

            def tt(out, x, y, op):
                dve.drain()
                return dve.tensor_tensor(out, x, y, op)

            def first_of(eq, tmp):
                dve.drain()
                dve.tensor_copy(tmp[:, :, 0:1], eq[:, :, 0:1])
                for k in range(1, 4):
                    dve.drain()
                    dve.tensor_tensor(tmp[:, :, 1:2], eq[:, :, k:k + 1], tmp[:, :, 0:1], ALU.is_gt)
                    dve.drain()
                    dve.tensor_tensor(tmp[:, :, 0:1], tmp[:, :, 0:1], eq[:, :, k:k + 1], ALU.max)
                    dve.drain()
                    dve.tensor_copy(eq[:, :, k:k + 1], tmp[:, :, 1:2])
                dve.drain()

            dve.memset(lg[:, :, :], 0.0)
            dve.drain()
            dve.wait_ge(side_full, ROUTE.full("logit"))
            dve.wait_ge(wr_landed, 64)
            for b2, n in ((0, P), (1, P), (2, NB)):
                ins = dve.tensor_tensor(lg[0:n, b2, :], side[1][0:n, 20 * b2:20 * b2 + 20], br[0:n, :], ALU.add)
            ins.then_inc(side_free[1], 1)
            dve.drain()
            gl, el = lg[:, :, 0:4], lg[:, :, 4:20]
            m1, goh, es, oh1, esm, m2, oh2, tmp = [r[:, :, 0:4] for r in rt[1:9]]
            ex = rt[0]

            def wide(x):
                return x[:, :, 0:1].broadcast_to([P, 3, 4])

            dve.tensor_reduce(m1[:, :, 0:1], gl, AX.X, ALU.max)
            tt(goh, gl, wide(m1), ALU.is_equal)
            tt(ex[:, :, 0:4], gl, wide(m1), ALU.subtract)
            first_of(goh, tmp)
            for k in range(4):
                tt(rt[9][:, :, 0:4], el[:, :, 4 * k:4 * k + 4], goh[:, :, k:k + 1].broadcast_to([P, 3, 4]), ALU.mult)
                if k == 0:
                    dve.drain()
                    dve.tensor_copy(es, rt[9][:, :, 0:4])
                else:
                    tt(es, es, rt[9][:, :, 0:4], ALU.add)
            dve.drain()
            dve.tensor_reduce(m2[:, :, 0:1], es, AX.X, ALU.max)
            tt(oh1, es, wide(m2), ALU.is_equal)
            tt(ex[:, :, 4:8], es, wide(m2), ALU.subtract)
            first_of(oh1, tmp)
            dve.tensor_scalar(tmp, oh1, -3.0e38, None, ALU.mult)
            dve.tensor_scalar(esm, oh1, -1.0, 1.0, ALU.mult, ALU.add)
            tt(esm, esm, es, ALU.mult)
            tt(esm, esm, tmp, ALU.add)
            dve.drain()
            dve.tensor_reduce(m2[:, :, 0:1], esm, AX.X, ALU.max)
            tt(oh2, esm, wide(m2), ALU.is_equal)
            first_of(oh2, tmp)
            dve.memset(ex[:, :, 8:16], 0.0)
            dve.drain().then_inc(dve_step, 1)
            dve.wait_ge(route_exp, 1)
            dve.tensor_reduce(m1[:, :, 0:1], ex[:, :, 0:4], AX.X, ALU.add)
            dve.tensor_tensor(tmp, oh2, ex[:, :, 4:8], ALU.mult)
            dve.drain()
            dve.tensor_reduce(m1[:, :, 1:2], tmp, AX.X, ALU.add)
            dve.drain()
            dve.tensor_scalar(m1[:, :, 1:2], m1[:, :, 1:2], 1.0, None, ALU.add)
            dve.drain()
            dve.tensor_tensor(m1[:, :, 0:1], m1[:, :, 0:1], m1[:, :, 1:2], ALU.mult)
            dve.drain()
            dve.reciprocal(m1[:, :, 0:1], m1[:, :, 0:1])
            tt(tmp, tmp, oh1, ALU.add)
            tt(tmp, tmp, wide(m1), ALU.mult)
            for k in range(4):
                tt(comb[:, :, 4 * k:4 * k + 4], tmp, goh[:, :, k:k + 1].broadcast_to([P, 3, 4]), ALU.mult)
            dve.drain()
            tt(tmp, oh1, oh2, ALU.add)
            dve.wait_ge(moe_consts, 1)
            for k in range(4):
                tt(member[:, :, 4 * k:4 * k + 4], tmp, goh[:, :, k:k + 1].broadcast_to([P, 3, 4]), ALU.mult)
            tt(member[:, :, :], member[:, :, :], valid[:, :].unsqueeze(2).broadcast_to([P, 3, EXPERTS]), ALU.mult)
            dve.drain().then_inc(member_ready, 1)
            dve.memset(most[:, :], 0.0)
            dve.wait_ge(side_full, ROUTE.full("rank"))
            dve.tensor_scalar(slot[:, :, :], member[:, :, :], -4096.0, 4096.0, ALU.mult, ALU.add)
            dve.drain()
            dve.tensor_tensor(slot[:, :, :], side[2][:, 0:48].rearrange("p (b e) -> p b e", b=3), slot[:, :, :], ALU.add)
            dve.tensor_reduce(most[:, 0:1], side[2][:, 48:64], AX.X, ALU.max).then_inc(side_free[2], 1)
            dve.drain()
            for k in range(1, MAX_ROUNDS):
                dve.tensor_scalar(most[:, k:k + 1], most[:, 0:1], float(k * SLOTS), None, ALU.is_gt)
            dve.memset(most[:, MAX_ROUNDS:MAX_ROUNDS + 1], 1.0)
            dve.drain()
            dve.tensor_reduce(most[:, 7:8], most[:, 1:MAX_ROUNDS + 1], AX.X, ALU.add)
            dve.drain()
            dve.tensor_copy(rounds[:, :], most[:, 7:8])
            dve.drain().then_inc(rounds_ready, 1)
            dve.wait_ge(xt_clear, 1)
            for k in range(0, 12, 2):
                xt_out(dve, k)
            dve.wait_ge(rounds_ready, 1)
            n_rounds = dve.value_load(rounds[0:1, 0:1], min_val=1, max_val=MAX_ROUNDS)

            def picks(i):
                for par in range(2):
                    for b2 in range(3):
                        dve.tensor_scalar(pick[:, b2, par * SLOTS:(par + 1) * SLOTS], iota[:, :],
                                          slot[:, b2, bass.ds(i * 2 + par, 1)], None, ALU.is_equal)
                dve.drain().then_inc(pick_ready, 1)

            def low(n, k):
                for half in range(2):
                    h = 2 * k + half
                    dve.wait_ge(hi_ready, n * 2 + (h + 1))
                    dve.tensor_tensor(w_l[h % TURNS][:, :, :], ring[:, k % 4, 2 * half:2 * half + 2, :],
                                      w_h[h % TURNS][:, :, :].bitcast(F32), ALU.subtract).then_inc(lo_ready, 1)

            def gathered(table, r, it, done, gs):
                for g in gs:
                    dve.wait_ge(xgh_ready, done * 4 + (g + 1))
                    dve.tensor_tensor(xg_l[:, 4 * g:4 * g + 4, :], side[g][:, :].rearrange("p (t n) -> p t n", n=P),
                                      xg_h[:, 4 * g:4 * g + 4, :].bitcast(F32), ALU.subtract)\
                        .then_inc(side_free[g], 1)
                    dve.drain().then_inc(xg_ready, 1)

            def add_scattered(table, r, it, ks):
                for k in ks:
                    dve.wait_ge(side_full, r * ROUND_EVENTS + table.full(f"S{k}", it))
                    dve.tensor_tensor(xres[:, k, :], xres[:, k, :], side[k % 4][:, 0:T], ALU.add)\
                        .then_inc(side_free[k % 4], 1)

            def pair(table, r, i, it, first, last):
                done = r * PAIRS + i
                n = r * ROUND_CHUNKS + i * PAIR_CHUNKS
                for k in range(PAIR_CHUNKS):
                    if not (last and k >= PAIR_CHUNKS - AHEAD):
                        low(n, k + AHEAD)
                    if not first and 1 <= k <= 4:
                        add_scattered(table, r, it, range(4 * k - 4, 4 * k))
                    if k == 5:
                        dve.wait_ge(side_full, r * ROUND_EVENTS + table.full("spread", it))
                        dve.tensor_copy(spread[:, :], side[0][:, 0:T])
                        dve.tensor_copy(w_slot[0:SLOTS, :], side[0][0:SLOTS, T:T + 1])
                        dve.tensor_copy(w_slot[SLOTS:P, :], side[0][SLOTS:P, T + 1:T + 2]).then_inc(side_free[0], 1)
                        dve.drain().then_inc(spread_ready, 1)
                        if not last:
                            picks(i + 1)
                    if k in (UP0 + 3, UP1 + 3):
                        half = slice(0, SLOTS) if k < GATE1 else slice(SLOTS, P)
                        j = 1 if k < GATE1 else 3
                        dve.wait_ge(hgate_ready, done * 2 + (1 if k < GATE1 else 2))
                        dve.wait_ge(moe_used, n * 2 + (2 * k + 2))
                        dve.tensor_tensor(hid[half, :], hgate[half, :], acc[j][half, :], ALU.mult)\
                            .then_inc(acc_free[j], 1)
                        dve.drain().then_inc(hid_ready, 1)
                    if k == UP1 + 3:
                        if not last:
                            gathered(table, r, it, done + 1, range(3))
                        dve.wait_ge(hidh_ready, done + 1)
                        dve.tensor_tensor(hid_l[:, :, :], side[0][:, :].rearrange("p (t n) -> p t n", n=P),
                                          hid_h[:, :, :].bitcast(F32), ALU.subtract).then_inc(side_free[0], 1)
                        dve.drain().then_inc(hidt_ready, 1)
                        if not last:
                            gathered(table, r, it, done + 1, range(3, 4))
                    if k >= DOWN0:
                        half = slice(0, SLOTS) if k < DOWN1 else slice(SLOTS, P)
                        q = k % 4
                        c = slice(q * 512, (q + 1) * 512)
                        dve.wait_ge(yh_ready, done * 8 + (k - DOWN0 + 1))
                        dve.scalar_tensor_tensor(y_l[half, c], acc[q][half, :], w_slot[half, 0:1],
                                                 y_h[half, c].bitcast(F32), ALU.mult, ALU.subtract)\
                            .then_inc(acc_free[q], 1)
                        dve.drain().then_inc(y_out, 1)

            with dve.Fori(0, n_rounds) as r:
                picks(0)
                for k in range(AHEAD):
                    low(r * ROUND_CHUNKS, k)
                gathered(MOE_BEGIN, r, 0, r * PAIRS, range(4))
                pair(MOE_FIRST, r, 0, 0, True, False)
                with dve.Fori(1, PAIRS - 1) as i:
                    pair(MOE_MID, r, i, i - 1, False, False)
                pair(MOE_LAST, r, PAIRS - 1, 0, False, True)
                add_scattered(MOE_END, r, 0, range(ND))
                dve.tensor_scalar(slot[:, :, :], slot[:, :, :], float(SLOTS), None, ALU.subtract)
                dve.drain()
            meet(dve, 6)
            norm_scale(1, xres, xn, lambda t: vec[:, V_FIN + t:V_FIN + t + 1], root=fin_root)
            dve.drain().then_inc(xn_ready, 1)
            for k in range(0, 12, 2):
                out_rows(dve, k)

        @block.gpsimd
        def _(pool):
            pool.memset(ident[:, :], 0.0)
            pool.memset(ones[:, :], 1.0)
            pool.memset(mask[:, :], 1.0)
            pool.memset(eps[:, :], EPS)
            pool.memset(xp[:, :, :], 0.0)
            pool.drain().then_inc(consts, 1)
            pool.wait_ge(consts, 1)
            pool.affine_select(out=ident[:, :], in_=ident[:, :], compare_op=ALU.not_equal, fill=1.0, base=0,
                               pattern=[[-1, P]], channel_multiplier=1).then_inc(consts, 1)
            pool.affine_select(out=mask[:, :], in_=mask[:, :], compare_op=ALU.is_ge, fill=0.0, base=0,
                               pattern=[[1, P]], channel_multiplier=-1).then_inc(consts, 1)
            pool.drain().then_inc(consts, 1)
            pool.wait_ge(xn_ready, 1)
            pool.memset(acc_rnn[:, :, :], 0.0)
            pool.memset(acc_ssd[:, :, :], 0.0)
            meet(pool, 1)

            def hist(c, src):
                wait_pos(pool, conv_done, c)
                pool.tensor_copy(xp[:, :, S0:XPW].rearrange("p t (b k) -> p t b k", k=TAPS)[:, :, :, 0:HIST],
                                 src.rearrange("p t (b k) -> p t b k", k=HIST)).then_inc(hist_in, 1)

            def stash(c, dst):
                pool.wait_ge(hist_in, c + 1)
                pool.wait_ge(xp_in, c + 1)
                pool.sem_inc(stash_begun, 1)
                pool.tensor_copy(dst[:, :, 0:24].rearrange("p t (b k) -> p t b k", k=HIST),
                                 xp[:, :, S0:XPW].rearrange("p t (b k) -> p t b k", k=TAPS)[:, :, :, 1:TAPS])
                pool.tensor_copy(dst[:, :, 24:27], xp[:, :, S0 - HIST:S0])
                pool.drain().then_inc(stash_done, 1)

            def rnn(i):
                t4 = bass.ds(i * 4, 4)
                hist(i, hist_r[:, t4, 0:24])
                stash(i, stash_r[:, t4, :])
                pool.wait_ge(y_ready, i + 1)
                pool.tensor_copy(stash_h[:, t4, :], hh[:, :, SEQ - 1:T]).then_inc(h_stashed, 1)

            rnn(0)
            with pool.Fori(1, RNN_N) as i:
                rnn(i)
            with pool.Fori(0, BC_N) as i:
                t4 = bass.ds(i * 4 + 32, 4)
                hist(i + RNN_N, hist_s[:, t4, 0:24])
                stash(i + RNN_N, stash_s[:, t4, :])
            meet(pool, 2)
            pool.tensor_copy(selb[0:NB, :, :], ident[0:NB, 0:NB].unsqueeze(2).broadcast_to([NB, NB, P]))

            def ssd(g, first):
                t4 = bass.ds(g * 4, 4)
                if not first:
                    pool.wait_ge(side_full, SSD.full("sd", g - 1))
                    pool.wait_ge(xd_ready, g)
                    pool.wait_ge(yz_ready, g)
                pool.tensor_copy(bcur[:, :], bc[:, bass.ds(g, 1), :].squeeze(1)).then_inc(cur_ready, 1)
                pool.tensor_copy(ccur[:, :], bc[:, bass.ds(g + GROUPS, 1), :].squeeze(1)).then_inc(cur_ready, 1)
                pool.tensor_copy(sel[0:HEADS, :, :], ident[0:HEADS, bass.ds(g * HG, HG)].unsqueeze(2)
                                 .broadcast_to([HEADS, HG, P])).then_inc(cur_ready, 1)
                pool.tensor_copy(cur_cs[:, :, :], cs_tok[:, :, bass.ds(g * HG, HG)])
                pool.tensor_copy(cur_d[:, :], d_col[:, t4])
                pool.tensor_copy(cur_w[:, :, :], wts[:, :, bass.ds(g * HG, HG)]).then_inc(cur_ready, 1)
                hist(g + (RNN_N + BC_N), hist_s[:, t4, 0:24])
                pool.wait_ge(ecs_ready, g + 1)
                pool.wait_ge(cur_ready, g * 4 + 2)
                pool.tensor_tensor(ec, ec, ccur[:, CH:SEQ].unsqueeze(1).broadcast_to([P, HG, CH]), ALU.mult)\
                    .then_inc(cts_ready, 1)
                stash(g + (RNN_N + BC_N), stash_s[:, t4, :])
                pool.wait_ge(xdts_ready, g + 1)
                pool.wait_ge(bcb_ready, g + 1)
                for q in range(4):
                    if q >= 2:
                        pool.wait_ge(h_new, g * 4 + (q - 1))
                    elif not first:
                        pool.wait_ge(h_new, g * 4 + (q - 1))
                    pool.tensor_tensor(ub[q % 2], bb, xdt_s[:, q, :].unsqueeze(2).broadcast_to([P, NB, NS]),
                                       ALU.mult).then_inc(u_ready, 1)

            ssd(0, True)
            with pool.Fori(1, GROUPS) as g:
                ssd(g, False)
            meet(pool, 3)
            meet(pool, 4)
            pool.wait_ge(x_landed, 64)
            with pool.Fori(0, OUT_N) as j:
                pool.wait_ge(tile_done, j * 16 + (FIRST + 16 * OUT_SLAB))
                pool.tensor_copy(xtile[:, 0:2, :], xtok[:, 0:2, bass.ds(j * 512, 512)])
                pool.tensor_copy(xtile[0:NB, 2, :], xtok[0:NB, 2, bass.ds(j * 512, 512)])
                pool.drain().then_inc(xtile_ready, 1)
            meet(pool, 5)
            pool.memset(valid[:, :], 1.0)
            pool.wait_ge(side_full, ROUTE.full("ss2"))
            pool.memset(xt[:, 2, :], 0.0)
            pool.iota(iota[:, :], pattern=[[1, SLOTS]], base=0, channel_multiplier=0,
                      allow_small_or_imprecise_dtypes=True)
            pool.tensor_tensor(before[:, :], mask[:, :], ident[:, :], ALU.subtract)
            pool.drain().then_inc(xt_clear, 1)
            pool.wait_ge(xt_clear, 1)
            pool.affine_select(out=valid[:, :], in_=valid[:, :], compare_op=ALU.is_ge, fill=0.0, base=T - 1,
                               pattern=[[-P, 3]], channel_multiplier=-1)
            pool.drain().then_inc(moe_consts, 1)
            meet(pool, 6)


_INS = ["x_prompt", "x_sample", "state_rglru_conv", "state_rglru_h", "state_ssd_conv", "state_ssd_h",
        "norm_mix", "w_in", "conv_rnn_w", "conv_rnn_b", "lru_wa", "lru_ba", "lru_wx", "lru_bx", "lru_lambda",
        "conv_ssd_w", "conv_ssd_b", "dt_bias", "a_log", "d_skip", "norm_ssd", "w_up_rnn", "w_up_ssd", "w_out",
        "norm_ffn", "w_route_group", "b_route_group", "w_route_expert", "b_route_expert",
        "w_exp_gate", "w_exp_up", "w_exp_down", "norm_final"]
_OUTS = [("y_p", (1, SEQ, D)), ("y_s", (NB, 1, D)),
         ("p_cr", (1, 1, HIST, D)), ("p_hr", (1, 1, D)), ("p_cs", (1, 1, HIST, D_XBC)),
         ("p_hs", (1, 1, HEADS, HD, NS)),
         ("s_cr", (1, NB, HIST, D)), ("s_hr", (1, NB, D)), ("s_cs", (1, NB, HIST, D_XBC)),
         ("s_hs", (1, NB, HEADS, HD, NS))]


def kernel(**inputs):
    import numpy as np
    import concourse.bacc as bacc
    from concourse.bass_utils import run_bass_kernel_spmd

    nc = bacc.Bacc("TRN2", target_bir_lowering=False, num_devices=1)
    arrays, ins, outs = {}, {}, {}
    for name in _INS:
        arr = np.ascontiguousarray(inputs[name])
        arrays[f"in_{name}"] = arr
        ins[name] = nc.dram_tensor(f"in_{name}", arr.shape, mybir.dt.from_np(arr.dtype), kind="ExternalInput").ap()
    for name, shape in _OUTS:
        outs[name] = nc.dram_tensor(f"out_{name}", shape, F32, kind="ExternalOutput").ap()
    build_program(nc, ins, outs)
    r = run_bass_kernel_spmd(nc, [arrays], core_ids=[0])
    return tuple(r.results[0][f"out_{name}"] for name, _ in _OUTS)
```

```python
from contextlib import ExitStack

import concourse.bass as bass
from concourse import mybir
from concourse.alu_op_type import AluOpType as ALU

F32 = mybir.dt.float32
F32R = mybir.dt.float32r
ACT = mybir.ActivationFunctionType
AX = mybir.AxisListType

P = 128
D = 2048
ND = D // P
SEQ = 256
NB = 8
T = SEQ + NB
CH = 128
HEADS, HD, NS, GROUPS = 64, 64, 128, 8
HG = HEADS // GROUPS
D_SSM = HEADS * HD
D_XBC = D_SSM + 2 * GROUPS * NS
NX = D_XBC // P
TAPS = 4
HIST = TAPS - 1
EXPERTS, EG, FE = 16, 4, 512
SLOTS = 64
PAIRS = EXPERTS // 2
MAX_ROUNDS = -(-T // SLOTS)
ROUND_SLABS = 3 * EXPERTS
EPS = 1e-6
XPW = HIST + SEQ + NB * TAPS
CVW = XPW - HIST
S0 = HIST + SEQ

RX, RY, Z, XBC = 0, D, 2 * D, 2 * D + D_SSM
DT = XBC + D_XBC
GR = DT + HEADS
GS = GR + D

V_MIX, V_CRW, V_CRB, V_BA, V_BX = 0, 16, 80, 96, 112
V_LAM, V_NSSD, V_FFN, V_FIN, V_CSB, V_CSW = 128, 144, 176, 192, 208, 256
NV = V_CSW + TAPS * NX

FIRST = ND

RNN_N, BC_N, SSD_N, GATE_N, OUT_N = 4, 4, GROUPS, 4, 4
BC_SLAB, BC_ROUND = 12, 24
SSD_SLAB, SSD_ROUND = 16, 28
GATE_SLAB, GATE_ROUND = 40, 76
OUT_SLAB, OUT_ROUND = 48, 84
MOE_SLAB, MOE_ROUND = 52, 88

RNN_EVENTS = [("r0", 0), ("r1", 1), ("r2", 2), ("r3", 3), ("i0", 0), ("i1", 1), ("i2", 2), ("i3", 3)]
SSD_EVENTS = [("G", 0), ("cs0", 1), ("cs1", 2), ("cs2", 1), ("cs3", 2), ("btok", 0), ("sd", 3),
              ("Bb0", 0), ("Bb1", 3), ("Cb0", 1), ("Cb1", 2), ("xt0", 0), ("xt1", 3),
              ("st0", 1), ("hf", 2), ("y0", 0), ("y1", 3), ("gn", 1)]
ROW_EVENTS = [(f"row{k}", k % 4) for k in range(20)]
OUTT_EVENTS = [(f"o{k}", (k + 1) % 4) for k in range(12)]


class Events:

    def __init__(self, events, before=None, repeats=1):
        self.events, self.repeats = events, repeats
        self.start = before.end if before else 0
        self.bank_start = list(before.bank_end) if before else [0] * 4
        self.index = {n: k for k, (n, _) in enumerate(events)}
        self.bank = dict(events)
        self.per_bank = [sum(b == k for _, b in events) for k in range(4)]
        self.end = self.start + repeats * len(events)
        self.bank_end = [s + repeats * n for s, n in zip(self.bank_start, self.per_bank)]

    def full(self, name, it=0):
        return it * len(self.events) + (self.start + self.index[name] + 1)

    def earlier(self, name, it=0):
        b, k = self.bank[name], self.index[name]
        return it * self.per_bank[b] + (self.bank_start[b] + sum(x == b for _, x in self.events[:k]))


SETUP = Events([("ss1", 1), ("vec", 0), ("dt", 2), ("hr", 1), ("hs0", 2), ("hs1", 3), ("hs2", 0),
                ("dtt", 3), ("tot", 0)])
RNN = Events(RNN_EVENTS, SETUP, RNN_N)
SSD = Events(SSD_EVENTS, RNN, SSD_N)
ROWS = Events(ROW_EVENTS, SSD)
ROUTE = Events([("ss2", 0), ("logit", 1), ("logit_tok", 2)] + [(f"xt{k}", k % 4) for k in range(12)]
               + [("rank", 2)], ROWS)
SCATTER = [(f"S{k}", k % 4) for k in range(ND)]
GATHER = [(f"G{k}", k) for k in range(4)]
MOE_BEGIN = Events(GATHER, ROUTE)
MOE_FIRST = Events([("spread", 0)] + GATHER[:3] + [("hidT", 0)] + GATHER[3:], MOE_BEGIN)
MOE_MID = Events(SCATTER + [("spread", 0)] + GATHER[:3] + [("hidT", 0)] + GATHER[3:], MOE_FIRST, PAIRS - 2)
MOE_LAST = Events(SCATTER + [("spread", 0), ("hidT", 0)], MOE_MID)
MOE_END = Events(SCATTER, MOE_LAST)
ROUND_EVENTS = MOE_END.end - ROUTE.end
ROUND_BANK = [x - y for x, y in zip(MOE_END.bank_end, ROUTE.bank_end)]
GATE0, UP0, GATE1, UP1, DOWN0, DOWN1 = range(0, 24, 4)
PAIR_CHUNKS = 24
DENSE_TURNS = 4
DENSE_AHEAD = DENSE_TURNS // 2
NO_SPLIT = 4 * (GATE_SLAB - SSD_SLAB)
SCATTER_AT = 5
TURNS = 6
AHEAD = TURNS // 2
ROUND_CHUNKS = PAIRS * PAIR_CHUNKS
FINAL = Events([("ss3", 0)] + OUTT_EVENTS)


def wait_pos(eng, sem, value):
    if not (isinstance(value, int) and value <= 0):
        eng.wait_ge(sem, value)


def build_program(nc, a, o):
    w_in = a["w_in"][0].rearrange("(k p) n -> p k n", p=P)
    w_upr = a["w_up_rnn"][0].rearrange("(s k p) n -> s p k n", p=P, k=4)
    w_ups = a["w_up_ssd"][0].rearrange("(s k p) n -> s p k n", p=P, k=4)
    w_out = a["w_out"][0].rearrange("(k p) n -> p k n", p=P)
    w_gate = a["w_exp_gate"][0].rearrange("e (k p) n -> e p k n", p=P)
    w_up = a["w_exp_up"][0].rearrange("e (k p) n -> e p k n", p=P)
    w_down = a["w_exp_down"][0].rearrange("e (k p) n -> e p k n", p=P)
    h0_dram = a["state_ssd_h"][0].rearrange("b (t h) p n -> t (h p) b n", h=2)
    h1_dram = o["s_hs"][0].rearrange("b (t h) p n -> t (h p) b n", h=2)
    hp_dram = o["p_hs"][0, 0].rearrange("(t h) p n -> (h p) t n", h=2)
    lru_w = [a[n][0].rearrange("t c d -> c t d") for n in ("lru_wa", "lru_wx")]

    with ExitStack() as ctx:
        class Scope(ExitStack):

            def take(self, name, *free, dt=F32):
                return self.enter_context(nc.sbuf_tensor(name, [P, *free], dt))

        def sb(name, *free, dt=F32):
            return ctx.enter_context(nc.sbuf_tensor(name, [P, *free], dt))

        def sem(name):
            return ctx.enter_context(nc.semaphore(name))

        ring = sb("ring", 4, 4, 512)
        with Scope() as s:
            big = s.take("big", 3 * ND * T)
        rnn_r, ssd_r, bc_r = [sb(n, ND, T, dt=F32R) for n in ("rnn_r", "ssd_r", "bc_r")]
        part = [big[:, k * ND * T:(k + 1) * ND * T] for k in range(3)]
        acc_rnn, acc_ssd, bc = [p.rearrange("p (t n) -> p t n", n=T) for p in part]
        vec = sb("vec", NV)
        hist_r = sb("hist_r", ND, 32)
        stash_r = sb("stash_r", ND, 27)
        hist_s = sb("hist_s", NX, 27)
        stash_s = hist_s
        stash_h = sb("stash_h", ND, 9)
        ident = sb("ident", P)
        ones = sb("ones", P)
        mask = sb("mask", P)
        eps = sb("eps", 1)
        c8 = sb("c8", 2, ND)
        d_col = sb("d_col", HEADS // 2)
        cs_tok = sb("cs_tok", 2, HEADS)
        wts = sb("wts", 5, HEADS)
        dt_f = sb("dt_f", T)
        cs_f = sb("cs_f", SEQ)
        sd_f = sb("sd_f", 2 * NB)
        rs = sb("rs", T)

        def weight_parts(scope, name, turns):
            return list(zip(*[(scope.take(f"{name}_h{k}", 2, 512, dt=F32R),
                               scope.take(f"{name}_l{k}", 2, 512, dt=F32R)) for k in range(turns)]))

        with Scope() as s:
            xn = s.take("xn", ND, T)
        norm = Scope()
        xn_r = norm.take("xn_r", ND, T, dt=F32R)
        mixer = Scope()
        xp = mixer.take("xp", 4, XPW)
        cv = mixer.take("cv", 4, CVW)
        cx = mixer.take("cx", 4, T)
        yv = cv[:, :, 0:T]

        dense = Scope()
        parts_rnn = weight_parts(dense, "rnn", DENSE_TURNS)
        with Scope() as s:
            vrow = s.take("vrow", 4, P)
            hrow_r = s.take("hrow_r", D)
            hrow_s = s.take("hrow_s", D_XBC)
            dtw = s.take("dtw", ND, HEADS)
            sm_u, sm_e, sm_r, sm_s, sm_p = [s.take(f"sm{k}", T) for k in range(5)]
            dt_b, a_neg, d_bc = s.take("dt_b", 1), s.take("a_neg", 1), s.take("d_bc", HEADS)
            dt_tok, tot, dg = s.take("dt_tok", 2, HEADS), s.take("tot", 2, HEADS), s.take("dg", 2, HEADS)
            lm = s.take("lm", 5, ND)
        xtok0 = big[:, ND * T:ND * T + 3 * D].rearrange("p (b n) -> p b n", n=D)
        xT0 = acc_rnn

        with Scope() as s:
            gr, gi, ga, gt, gm, hh, ge = [s.take(n, 4, T) for n in ("gr", "gi", "ga", "gt", "gm", "hh", "ge")]
            yr_h, yr_l = s.take("yr_h", 4, T, dt=F32R), s.take("yr_l", 4, T, dt=F32R)
            lruw = s.take("lruw", 2, 4, P)
            gs = s.take("gs", 4, NB)
        xn_h, xn_l = xn_r, ssd_r

        dense.close()
        with Scope() as s:
            sz, yn = s.take("sz", 4, T), s.take("yn", 4, T)
            dm2 = s.take("dm2", 2, HG, CH)
            dm = [dm2[:, c, :, :] for c in range(2)]
            sq_g = dm2[:, :, :, :].rearrange("p c h l -> p (c h l)")[:, 0:4 * T].rearrange("p (t n) -> p t n", n=T)
            ec = s.take("ec", HG, CH)[:, :, :]
            bb, cb = s.take("bb", NB, NS)[:, :, :], s.take("cb", NB, NS)[:, :, :]
            h_ring = s.take("h_ring", 4, NB, NS)
            ub = [s.take(f"ub{k}", NB, NS)[:, :, :] for k in range(2)]
            xd = [s.take(f"xd{k}", 512)[:, :] for k in range(5)]
            st0 = s.take("st0", 512)[:, :]
            btok, gtm = s.take("btok", 2, CH), s.take("gtm", 2, CH)
            bcs, ccs = s.take("bcs", P), s.take("ccs", P)
            sel = s.take("sel", HG, P)
            selb = s.take("selb", NB, P)
            bcur, ccur = s.take("bcur", T), s.take("ccur", T)
            hf = xd[3].rearrange("p (t n) -> p t n", n=NS)
            sd = s.take("sd", 4, 2 * NB)
            xdt_s, ys = s.take("xdt_s", 4, NB), s.take("ys", 4, NB)
            cur_cs, cur_w, cur_d = s.take("cur_cs", 2, HG), s.take("cur_w", 5, HG), s.take("cur_d", 4)

        mixer.close()
        tail = Scope()
        parts_out = weight_parts(tail, "out", DENSE_TURNS)
        with Scope() as s:
            row_s, row_r, row_h = s.take("row_s", D_XBC), s.take("row_r", D), s.take("row_h", D)
            g1, g2 = s.take("g1", 4, T), s.take("g2", 4, T)
        gate_h, gate_l = bc_r, xn_r

        with Scope() as s:
            xtok = s.take("xtok", 3, D)
            xtile = s.take("xtile", 3, 512)
            sq_res = s.take("sq_res", 4, T)
        tail.close()

        xres = bc
        sq2 = acc_rnn
        norm.close()
        with Scope() as s:
            w_h, w_l = weight_parts(s, "moe", TURNS)
            xg_h, xg_l = s.take("xg_h", ND, P, dt=F32R), s.take("xg_l", ND, P, dt=F32R)
            hid_h, hid_l = s.take("hid_h", 4, P, dt=F32R), s.take("hid_l", 4, P, dt=F32R)
            y_h, y_l = s.take("y_h", D, dt=F32R), s.take("y_l", D, dt=F32R)
            wr = s.take("wr", ND, 20)
            br = s.take("br", 20)
            lg = s.take("lg", 3, 20)
            lg_f = s.take("lg_f", T)
            rt = [s.take(f"rt{k}", 3, 16) for k in range(10)]
            comb = s.take("comb", 3, EXPERTS)
            member = s.take("member", 3, EXPERTS)
            slot = s.take("slot", 3, EXPERTS)
            before = s.take("before", P)
            valid = s.take("valid", 3)
            iota = s.take("iota", SLOTS)
            most = s.take("most", 8)
            rounds = s.take("rounds", 1, dt=mybir.dt.int32)
            pick = s.take("pick", 3, 2 * SLOTS)
            spread = s.take("spread", T, dt=F32R)
            w_slot = s.take("w_slot", 1)
        xt = big[:, 0:3 * D].rearrange("p (b n) -> p b n", n=D)
        hgate, hid = big[:, 3 * D:3 * D + FE], big[:, 3 * D + FE:3 * D + 2 * FE]
        ytok = xt

        acc = [ctx.enter_context(nc.psum_tensor(f"acc{j}", [P, 512], F32)) for j in range(4)]
        side = [ctx.enter_context(nc.psum_tensor(f"side{j}", [P, 512], F32)) for j in range(4)]

        landed = [sem(f"chunk_landed{q}") for q in range(4)]
        tile_done = sem("tile_done")
        acc_free = [sem(f"acc_free{j}") for j in range(4)]
        side_full = sem("side_full")
        side_free = [sem(f"side_free{j}") for j in range(4)]
        barrier = sem("barrier")
        x_landed, small_landed = sem("x_landed"), sem("small_landed")
        dtw_landed, lru_landed = sem("dtw_landed"), sem("lru_landed")
        h_landed = [sem(f"h_landed{q}") for q in range(4)]
        h_stored = [sem(f"h_stored{q}") for q in range(4)]
        hf_stored, stored = sem("hf_stored"), sem("stored")
        consts = sem("consts")
        sq_ready, root_ready, xn_ready = sem("sq_ready"), sem("root_ready"), sem("xn_ready")
        xt_done = sem("xt_done")
        hist_in, xp_in, conv_done, stash_done = sem("hist_in"), sem("xp_in"), sem("conv_done"), sem("stash_done")
        stash_begun = sem("stash_begun")
        xt_clear = sem("xt_clear")
        act_step, dve_step = sem("act_step"), sem("dve_step")
        gates_ready, decay_ready = sem("gates_ready"), sem("decay_ready")
        m2_ready, mult_ready, gelu_ready, y_ready = (sem("m2_ready"), sem("mult_ready"), sem("gelu_ready"),
                                                     sem("y_ready"))
        h_stashed = sem("h_stashed")
        bc_ready = sem("bc_ready")
        cur_ready = sem("cur_ready")
        diffed, ecs_ready, cts_ready = sem("diffed"), sem("ecs_ready"), sem("cts_ready")
        exp_ready, m_ready = sem("exp_ready"), sem("m_ready")
        tok_ready, bcb_ready, bcs_ready = sem("tok_ready"), sem("bcb_ready"), sem("bcs_ready")
        xs_ready, xdts_ready, u_ready = sem("xs_ready"), sem("xdts_ready"), sem("u_ready")
        h_new, xd_ready, st_ready, hf_ready = sem("h_new"), sem("xd_ready"), sem("st_ready"), sem("hf_ready")
        sz_ready, yz_ready, sqg_ready, yn_ready = sem("sz_ready"), sem("yz_ready"), sem("sqg_ready"), sem("yn_ready")
        rows_ready = sem("rows_ready")
        sg_ready, merged_ready, xtile_ready = sem("sg_ready"), sem("merged_ready"), sem("xtile_ready")
        wr_landed, member_ready, rounds_ready = sem("wr_landed"), sem("member_ready"), sem("rounds_ready")
        moe_consts, xt_ready, route_exp = sem("moe_consts"), sem("xt_ready"), sem("route_exp")
        pick_ready, spread_ready = sem("pick_ready"), sem("spread_ready")
        hi_ready, lo_ready = sem("hi_ready"), sem("lo_ready")
        dense_high, dense_low = sem("dense_high"), sem("dense_low")
        first_half_used = sem("first_half_used")
        xn_high, xn_split, xn_whole = sem("xn_high"), sem("xn_split"), sem("xn_whole")
        ssd_zeroed = sem("ssd_zeroed")
        logits_out = sem("logits_out")
        projected, sq_summed = sem("projected"), sem("sq_summed")
        moe_used = sem("moe_used")
        xgh_ready, xg_ready = sem("xgh_ready"), sem("xg_ready")
        hgate_ready, hid_ready = sem("hgate_ready"), sem("hid_ready")
        hidh_ready, hidt_ready = sem("hidh_ready"), sem("hidt_ready")
        yh_ready, y_out = sem("yh_ready"), sem("y_out")
        fin_full, fin_free = sem("fin_full"), [sem(f"fin_free{j}") for j in range(4)]
        fin_sq, fin_root = sem("fin_sq"), sem("fin_root")
        ytok_ready = sem("ytok_ready")

        block = ctx.enter_context(nc.Block())
        ENG = 4

        def meet(eng, n):
            eng.drain().then_inc(barrier, 1)
            eng.wait_ge(barrier, ENG * n)

        @block.sync
        def _(sp):
            def chunk(slab, q, src, split=None):
                if isinstance(slab, int) and slab == 0:
                    pass
                elif split is None:
                    sp.wait_ge(tile_done, (slab - 1) * 16 + (FIRST + 4 * q + 4))
                else:
                    sp.wait_ge(dense_low, slab * 8 + (2 * q - 6 - 2 * split))
                sp.dma_start(ring[:, q, :, :], src).then_inc(landed[q], 16)

            def k_chunk(slab, q, w, col, split=None):
                chunk(slab, q, w[:, 4 * q:4 * q + 4, bass.ds(col, 512)], split)

            def row_chunk(slab, q, w, i, split=None):
                chunk(slab, q, w[bass.ds(i, 1), :, :, 512 * q:512 * q + 512].squeeze(0)
                      if not isinstance(i, int) else w[i, :, :, 512 * q:512 * q + 512], split)

            def e_chunk(slab, q, w, e):
                chunk(slab, q, w[bass.ds(e, 1), :, 4 * q:4 * q + 4, :].squeeze(0)
                      if not isinstance(e, int) else w[e, :, 4 * q:4 * q + 4, :])

            xp_rows = a["x_prompt"][0].rearrange("(b p) n -> p b n", p=P)
            sp.dma_start(xtok0[:, 0:2, :], xp_rows).then_inc(x_landed, 16)
            sp.dma_start(xtok0[0:NB, 2, :], a["x_sample"][:, 0, :]).then_inc(x_landed, 16)
            sp.dma_start(dtw[:, :, :], w_in[:, :, DT:DT + HEADS]).then_inc(dtw_landed, 16)

            def rnn_load(i, slab, up):
                for q in range(4):
                    k_chunk(slab, q, w_in, i * 512 + RX, 0)
                if isinstance(i, int) and i == 0:
                    sp.wait_ge(barrier, ENG * 1)
                else:
                    sp.wait_ge(side_full, RNN.full("i3", i - 1))
                for k in range(2):
                    sp.dma_start(lruw[:, k, :, :], lru_w[k][:, bass.ds(i * 4, 4), :]).then_inc(lru_landed, 16)
                for q in range(4):
                    k_chunk(slab + 1, q, w_in, i * 512 + RY, 0)
                if up:
                    for q in range(4):
                        row_chunk(slab + 2, q, w_upr, i - 1, 0)

            rnn_load(0, 0, False)
            with sp.Fori(1, RNN_N) as i:
                rnn_load(i, i * 3 - 1, True)
            for q in range(4):
                k_chunk(BC_SLAB - 1, q, w_in, XBC + D_SSM, 0)
            for q in range(4):
                row_chunk(BC_SLAB, q, w_upr, RNN_N - 1, 0)
            with sp.Fori(1, BC_N) as i:
                for q in range(4):
                    k_chunk(i + BC_SLAB, q, w_in, i * 512 + (XBC + D_SSM), 0)

            def store_states(g):
                for q in range(4):
                    sp.wait_ge(h_new, g * 4 + (q + 1))
                    sp.dma_start(h1_dram[bass.ds(g * 4 + q, 1), :, :, :].squeeze(0), h_ring[:, q, :, :])\
                        .then_inc(h_stored[q], 16)
                sp.wait_ge(hf_ready, g + 1)
                sp.dma_start(hp_dram[:, bass.ds(g * 4, 4), :], hf[:, :, :]).then_inc(hf_stored, 16)

            def ssd_load(g, slab, first):
                for q in range(4):
                    k_chunk(slab, q, w_in, g * 512 + XBC)
                if first:
                    sp.wait_ge(barrier, ENG * 2)
                else:
                    store_states(g - 1)
                for q in range(4):
                    k_chunk(slab + 1, q, w_in, g * 512 + Z)
                    if not first:
                        sp.wait_ge(h_stored[q], g * 16)
                    sp.dma_start(h_ring[:, q, :, :], h0_dram[bass.ds(g * 4 + q, 1), :, :, :].squeeze(0))\
                        .then_inc(h_landed[q], 16)
                if not first:
                    for q in range(4):
                        row_chunk(slab + 2, q, w_ups, g - 1)

            ssd_load(0, SSD_SLAB, True)
            with sp.Fori(1, GROUPS) as g:
                ssd_load(g, g * 3 + (SSD_SLAB - 1), False)
            for q in range(4):
                row_chunk(GATE_SLAB - 1, q, w_ups, GROUPS - 1)
            store_states(GROUPS - 1)
            for q in range(4):
                k_chunk(GATE_SLAB, q, w_in, GR)
            with sp.Fori(0, GATE_N - 1) as j:
                for q in range(4):
                    k_chunk(j * 2 + (GATE_SLAB + 1), q, w_in, j * 512 + GS, NO_SPLIT)
                for q in range(4):
                    k_chunk(j * 2 + (GATE_SLAB + 2), q, w_in, j * 512 + (GR + 512), NO_SPLIT)
            for q in range(4):
                k_chunk(OUT_SLAB - 1, q, w_in, GS + 512 * (GATE_N - 1), NO_SPLIT)
            for q in range(4):
                k_chunk(OUT_SLAB, q, w_out, 0, NO_SPLIT)
            sp.wait_ge(rows_ready, 1)
            for src, dst in ((row_s[0:24, :], o["s_cs"][0].rearrange("b k n -> (b k) n")),
                             (row_s[24:27, :], o["p_cs"][0, 0]),
                             (row_r[0:24, :], o["s_cr"][0].rearrange("b k n -> (b k) n")),
                             (row_r[24:27, :], o["p_cr"][0, 0]),
                             (row_h[0:1, :], o["p_hr"][0]), (row_h[1:9, :], o["s_hr"][0])):
                sp.dma_start(dst, src).then_inc(stored, 16)
            sp.wait_ge(stored, 96)
            sp.wait_ge(barrier, ENG * 4)
            sp.dma_start(xtok[:, 0:2, :], xp_rows).then_inc(x_landed, 16)
            sp.dma_start(xtok[0:NB, 2, :], a["x_sample"][:, 0, :]).then_inc(x_landed, 16)
            with sp.Fori(1, OUT_N) as j:
                for q in range(4):
                    k_chunk(j + OUT_SLAB, q, w_out, j * 512, NO_SPLIT)
            sp.wait_ge(barrier, ENG * 5)
            for c, name in ((slice(0, 4), "w_route_group"), (slice(4, 20), "w_route_expert")):
                sp.dma_start(wr[:, :, c], a[name][0].rearrange("(k p) n -> p k n", p=P)).then_inc(wr_landed, 16)
            sp.dma_start(br[:, 0:4], a["b_route_group"].broadcast_to([P, 4])).then_inc(wr_landed, 16)
            sp.dma_start(br[:, 4:20], a["b_route_expert"].broadcast_to([P, 16])).then_inc(wr_landed, 16)

            def moe_chunk(n, q, src):
                sp.wait_ge(lo_ready, n * 2 - 6)
                sp.dma_start(ring[:, q, :, :], src).then_inc(landed[q], 16)

            def e_src(w, e, q):
                if isinstance(e, int):
                    return w[e, :, 4 * q:4 * q + 4, :]
                return w[bass.ds(e, 1), :, 4 * q:4 * q + 4, :].squeeze(0)

            def d_src(e, q):
                return w_down[bass.ds(e, 1), :, :, 512 * q:512 * q + 512].squeeze(0)

            def pair_load(n, i, skip):
                for k in range(skip, PAIR_CHUNKS):
                    q, e = k % 4, i * 2 + (1 if GATE1 <= k < DOWN0 or k >= DOWN1 else 0)
                    if k >= DOWN0:
                        src = d_src(e, q)
                    else:
                        src = e_src(w_gate if k // 4 in (GATE0 // 4, GATE1 // 4) else w_up, e, q)
                    moe_chunk(n + k, q, src)

            for q in range(4):
                e_chunk(MOE_SLAB, q, w_gate, 0)
            sp.wait_ge(rounds_ready, 1)
            n_rounds = sp.value_load(rounds[0:1, 0:1], min_val=1, max_val=MAX_ROUNDS)
            with sp.Fori(0, n_rounds) as r:
                with sp.If(r > 0):
                    sp.wait_ge(lo_ready, r * (2 * ROUND_CHUNKS))
                    for q in range(4):
                        sp.dma_start(ring[:, q, :, :], e_src(w_gate, 0, q)).then_inc(landed[q], 16)
                pair_load(r * ROUND_CHUNKS, 0, 4)
                with sp.Fori(1, PAIRS) as i:
                    pair_load(r * ROUND_CHUNKS + i * PAIR_CHUNKS, i, 0)
            for g in range(4):
                c = slice(512 * g, 512 * g + 512)
                sp.wait_ge(ytok_ready, g + 1)
                sp.dma_start(o["y_p"][0].rearrange("(b p) n -> p b n", p=P)[:, :, c], ytok[:, 0:2, c])\
                    .then_inc(stored, 16)
                sp.dma_start(o["y_s"][:, 0, c], ytok[0:NB, 2, c]).then_inc(stored, 16)
            sp.wait_ge(stored, 96 + 8 * 16)
            sp.wait_ge(hf_stored, 16 * GROUPS)
            for q in range(4):
                sp.wait_ge(h_stored[q], 16 * GROUPS)

        @block.tensor
        def _(pe):
            def event(table, name, it=0):
                b = table.bank[name]
                wait_pos(pe, side_free[b], table.earlier(name, it))
                return side[b]

            def k_chunk(slab, rnd, q, rhs):
                pe.wait_ge(landed[q], slab * 16 + 16)
                for j in range(4):
                    if q == 0:
                        wait_pos(pe, acc_free[j], rnd)
                    for k in range(4):
                        mm = pe.matmul(acc[j][:, 0:T], ring[:, q, k, j * P:(j + 1) * P], rhs[:, 4 * q + k, :],
                                       start=(q == 0 and k == 0), stop=(q == 3 and k == 3))
                    mm.then_inc(tile_done, 1)

            def k_slab(slab, rnd, rhs):
                for q in range(4):
                    k_chunk(slab, rnd, q, rhs)

            def row_chunk(slab, rnd, q, rhs):
                pe.wait_ge(landed[q], slab * 16 + 16)
                for j in range(4):
                    wait_pos(pe, acc_free[j], rnd + q)
                    for k in range(4):
                        mm = pe.matmul(acc[j][:, 0:T], ring[:, q, k, j * P:(j + 1) * P], rhs[:, k, :],
                                       start=(k == 0), stop=(k == 3))
                    mm.then_inc(tile_done, 1)

            def split_chunk(slab, rnd, q, parts, x_h, x_l, row=False, skipped=0):
                w_h, w_l = parts
                t0 = 0 if row else 4 * q

                def product(j, half):
                    turn = (2 * q + half) % DENSE_TURNS
                    for k in range(2):
                        t, c = t0 + 2 * half + k, slice(j * P, (j + 1) * P)
                        start = half == 0 and k == 0 and (q == 0 or row)
                        stop = half == 1 and k == 1 and (row or q == 3)
                        pe.matmul(acc[j][:, 0:T], w_h[turn][:, k, c], x_h[:, t, :], start=start, stop=False)
                        pe.matmul(acc[j][:, 0:T], w_l[turn][:, k, c], x_h[:, t, :], start=False, stop=False)
                        mm = pe.matmul(acc[j][:, 0:T], w_h[turn][:, k, c], x_l[:, t, :], start=False, stop=stop)
                    if half == 1:
                        mm.then_inc(tile_done, 1)
                    elif j == 3:
                        mm.then_inc(first_half_used, 1)

                low_count = slab * 8 + (2 * q + 1 - 2 * skipped)
                if row or q == 3:
                    pe.wait_ge(dense_low, low_count + 1)
                    for j in range(4):
                        if row:
                            wait_pos(pe, acc_free[j], rnd + q)
                        product(j, 0)
                        product(j, 1)
                else:
                    for half in range(2):
                        pe.wait_ge(dense_low, low_count + half)
                        for j in range(4):
                            if half == 0 and q == 0:
                                wait_pos(pe, acc_free[j], rnd)
                            product(j, half)

            def norm_sum(table, name, squares, n, count):
                b = event(table, name)
                for k in range(n):
                    if k % 4 == 0:
                        pe.wait_ge(sq_ready, 4 * (count - 1) + (k // 4 + 1))
                    mm = pe.matmul(b[:, 0:T], ones[:, :], squares[:, k, :], start=(k == 0), stop=(k == n - 1))
                mm.then_inc(side_full, 1)

            pe.wait_ge(consts, 4)
            pe.wait_ge(x_landed, 32)
            for t in range(ND):
                j = t % 4
                wait_pos(pe, xt_done, t - 3)
                for b2, n in ((0, P), (1, P), (2, NB)):
                    mm = pe.transpose(acc[j][:, b2 * P:b2 * P + n], xtok0[0:n, b2, t * P:(t + 1) * P],
                                      ident[0:n, 0:n])
                mm.then_inc(tile_done, 1)
            norm_sum(SETUP, "ss1", xn, ND, 1)
            pe.wait_ge(small_landed, 16 * 18)
            b = event(SETUP, "vec")
            for k in range(4):
                n = min(P, NV - k * P)
                mm = pe.transpose(b[:, k * P:k * P + n], vrow[0:n, k, :], ident[0:n, 0:n])
            mm.then_inc(side_full, 1)
            pe.wait_ge(dtw_landed, 16)
            b = event(SETUP, "dt")
            for k in range(ND):
                if k % 4 == 0:
                    pe.wait_ge(xn_ready, k // 4 + 1)
                mm = pe.matmul(b[0:HEADS, 0:T], dtw[:, k, :], xT0[:, k, :], start=(k == 0), stop=(k == ND - 1))
            mm.then_inc(side_full, 1)
            b = event(SETUP, "hr")
            for t in range(ND):
                mm = pe.transpose(b[:, 32 * t:32 * t + 32], hrow_r[0:32, t * P:(t + 1) * P], ident[0:32, 0:32])
            mm.then_inc(side_full, 1)
            for m in range(3):
                b = event(SETUP, f"hs{m}")
                for t in range(16):
                    c = (16 * m + t) * P
                    mm = pe.transpose(b[:, 24 * t:24 * t + 24], hrow_s[0:24, c:c + P], ident[0:24, 0:24])
                mm.then_inc(side_full, 1)
            pe.wait_ge(xn_split, 1)
            for q in range(2):
                split_chunk(0, 0, q, parts_rnn, xn_h, xn_l)
            pe.wait_ge(tok_ready, 1)
            b = event(SETUP, "dtt")
            for c in range(2):
                pe.transpose(b[:, c * HEADS:(c + 1) * HEADS], dt_f[0:HEADS, c * CH:(c + 1) * CH],
                             ident[0:HEADS, 0:HEADS])
            for c in range(2):
                mm = pe.transpose(b[:, (2 + c) * HEADS:(3 + c) * HEADS], cs_f[0:HEADS, c * CH:(c + 1) * CH],
                                  ident[0:HEADS, 0:HEADS])
            mm.then_inc(side_full, 1)
            b = event(SETUP, "tot")
            mm = pe.matmul(b[:, 0:2 * HEADS], ones[0:HEADS, :], dg[0:HEADS, :, :], start=True, stop=True)
            mm.then_inc(side_full, 1)
            meet(pe, 1)

            def gates(i, k, name):
                for j in range(4):
                    b = event(RNN, f"{name}{j}", i)
                    pe.matmul(b[:, 0:T], lruw[:, k, j, :], cx[:, j, :], start=True, stop=True)\
                        .then_inc(side_full, 1)

            def rnn(i, slab, rnd, up):
                for k in range(2):
                    for q in range(4) if up or k else range(2, 4):
                        split_chunk(slab + k, rnd + k, q, parts_rnn, xn_h, xn_l)
                pe.wait_ge(conv_done, i + 1)
                pe.wait_ge(lru_landed, i * 32 + 32)
                gates(i, 0, "r")
                if up:
                    pe.wait_ge(y_ready, i)
                    split_chunk(slab + 2, rnd + 2, 0, parts_rnn, yr_h, yr_l, row=True)
                gates(i, 1, "i")
                if up:
                    for q in range(1, 4):
                        split_chunk(slab + 2, rnd + 2, q, parts_rnn, yr_h, yr_l, row=True)

            rnn(0, 0, 0, False)
            with pe.Fori(1, RNN_N) as i:
                rnn(i, i * 3 - 1, i * 6 - 4, True)
            for q in range(4):
                split_chunk(BC_SLAB - 1, BC_ROUND - 4, q, parts_rnn, xn_h, xn_l)
            pe.wait_ge(y_ready, RNN_N)
            for q in range(4):
                split_chunk(BC_SLAB, BC_ROUND - 3, q, parts_rnn, yr_h, yr_l, row=True)
            with pe.Fori(1, BC_N) as i:
                for q in range(4):
                    split_chunk(i + BC_SLAB, i + BC_ROUND, q, parts_rnn, xn_h, xn_l)
            for q in range(2):
                pe.wait_ge(xn_whole, q + 1)
                k_chunk(SSD_SLAB, SSD_ROUND, q, xn)
            pe.wait_ge(xn_whole, 4)
            meet(pe, 2)

            def ssd(g, slab, rnd, up):
                if not up:
                    k_chunk(slab, rnd, 2, xn)
                    k_chunk(slab, rnd, 3, xn)
                pe.wait_ge(cur_ready, g * 4 + 3)
                b = event(SSD, "G", g)
                for c in range(2):
                    mm = pe.matmul(b[:, c * CH:(c + 1) * CH], bcur[:, c * CH:(c + 1) * CH],
                                   ccur[:, c * CH:(c + 1) * CH], start=True, stop=True)
                mm.then_inc(side_full, 1)

                def cs_rows(k):
                    b = event(SSD, f"cs{k}", g)
                    for m in range(2):
                        mm = pe.matmul(b[:, m * SEQ:(m + 1) * SEQ], sel[0:HEADS, 2 * k + m, :],
                                       cs_f[0:HEADS, :], start=True, stop=True)
                    mm.then_inc(side_full, 1)

                cs_rows(0)
                cs_rows(1)
                if up:
                    k_chunk(slab, rnd, 0, xn)
                cs_rows(2)
                cs_rows(3)
                b = event(SSD, "btok", g)
                for c in range(2):
                    pe.transpose(b[:, c * CH:(c + 1) * CH], bcur[:, c * CH:(c + 1) * CH], ident[:, :])
                pe.transpose(b[0:NB, 2 * CH:3 * CH], bcur[:, SEQ:T], ident[:, :])
                pe.transpose(b[0:NB, 3 * CH:4 * CH], ccur[:, SEQ:T], ident[:, :]).then_inc(side_full, 1)
                b = event(SSD, "sd", g)
                sel_rows = sel[0:HEADS, :, :].rearrange("p h m -> p (h m)")
                for m in range(4):
                    at = 2 * m * P + HD
                    mm = pe.matmul(b[:, m * 16:(m + 1) * 16], sel_rows[:, at:at + P], sd_f[0:HEADS, :],
                                   start=True, stop=True)
                mm.then_inc(side_full, 1)
                if up:
                    k_chunk(slab, rnd, 1, xn)
                pe.wait_ge(bcs_ready, g + 1)
                for name, src in (("Bb", bcs), ("Cb", ccs)):
                    for m in range(2):
                        b = event(SSD, f"{name}{m}", g)
                        for n in range(4):
                            mm = pe.matmul(b[:, n * NS:(n + 1) * NS], selb[0:NB, 4 * m + n, :],
                                           src[0:NB, :], start=True, stop=True)
                        mm.then_inc(side_full, 1)
                    if name == "Bb" and up:
                        k_chunk(slab, rnd, 2, xn)
                if up:
                    k_chunk(slab, rnd, 3, xn)
                k_slab(slab + 1, rnd + 1, xn)
                pe.wait_ge(xs_ready, g + 1)
                for c in range(2):
                    b = event(SSD, f"xt{c}", g)
                    for m in range(4):
                        mm = pe.transpose(b[:, m * P:(m + 1) * P], cx[:, m, c * CH:(c + 1) * CH], ident[:, :])
                    mm.then_inc(side_full, 1)
                if up:
                    pe.wait_ge(yn_ready, g)
                    row_chunk(slab + 2, rnd + 2, 0, yn)
                    row_chunk(slab + 2, rnd + 2, 1, yn)
                pe.wait_ge(xd_ready, g + 1)
                b = event(SSD, "st0", g)
                pe.matmul(b[:, :], btok[:, 0, :], xd[2], start=True, stop=True).then_inc(side_full, 1)
                b = event(SSD, "hf", g)
                for m in range(4):
                    pe.matmul(b[:, m * NS:(m + 1) * NS], xd[3][:, m * P:(m + 1) * P], btok[:, 0, :],
                              start=True, stop=False)
                    mm = pe.matmul(b[:, m * NS:(m + 1) * NS], xd[4][:, m * P:(m + 1) * P], btok[:, 1, :],
                                   start=False, stop=True)
                mm.then_inc(side_full, 1)
                if up:
                    row_chunk(slab + 2, rnd + 2, 2, yn)
                pe.wait_ge(m_ready, g + 1)
                pe.wait_ge(cts_ready, g + 1)
                pe.wait_ge(st_ready, g + 1)
                for m in range(2):
                    b = event(SSD, f"y{m}", g)
                    for tt in range(2):
                        for c in range(2):
                            for n in range(2):
                                h = 4 * m + 2 * tt + n
                                to = b[n * HD:(n + 1) * HD, tt * SEQ + c * CH:tt * SEQ + (c + 1) * CH]
                                mm = pe.matmul(to, xd[c][:, h * HD:(h + 1) * HD], dm[c][:, h, :],
                                               start=True, stop=(c == 0))
                                if c == 1:
                                    mm = pe.matmul(to, st0[:, h * HD:(h + 1) * HD], ec[:, h, :],
                                                   start=False, stop=True)
                    mm.then_inc(side_full, 1)
                if up:
                    row_chunk(slab + 2, rnd + 2, 3, yn)
                pe.wait_ge(sqg_ready, g + 1)
                b = event(SSD, "gn", g)
                for m in range(4):
                    mm = pe.matmul(b[:, 0:T], ones[:, :], sq_g[:, m, :], start=(m == 0), stop=(m == 3))
                mm.then_inc(side_full, 1)

            ssd(0, SSD_SLAB, SSD_ROUND, False)
            with pe.Fori(1, GROUPS) as g:
                ssd(g, g * 3 + (SSD_SLAB - 1), g * 6 + (SSD_ROUND - 4), True)
            pe.wait_ge(yn_ready, GROUPS)
            for q in range(4):
                row_chunk(GATE_SLAB - 1, GATE_ROUND - 4, q, yn)
            meet(pe, 3)
            for k in range(20):
                b = event(ROWS, f"row{k}")
                for m in range(4):
                    if k < 12:
                        mm = pe.transpose(b[0:27, m * P:(m + 1) * P], stash_s[:, 4 * k + m, :], ident[:, :])
                    elif k < 16:
                        mm = pe.transpose(b[0:27, m * P:(m + 1) * P], stash_r[:, 4 * (k - 12) + m, :], ident[:, :])
                    else:
                        mm = pe.transpose(b[0:9, m * P:(m + 1) * P], stash_h[:, 4 * (k - 16) + m, :], ident[:, :])
                mm.then_inc(side_full, 1)
            pe.wait_ge(xn_split, 2)
            with pe.Fori(0, GATE_N) as j:
                for k in range(2):
                    for q in range(4):
                        split_chunk(j * 2 + (GATE_SLAB + k), j * 2 + (GATE_ROUND + k), q, parts_out,
                                    gate_h, gate_l, skipped=NO_SPLIT)
            def sum_squares(j, first=False, last=False):
                pe.wait_ge(sq_ready, j + 5)
                b = event(ROUTE, "ss2") if first else side[0]
                for k in range(4):
                    mm = pe.matmul(b[:, 0:T], ones[:, :], sq_res[:, k, :], start=first and k == 0,
                                   stop=last and k == 3)
                mm.then_inc(side_full if last else sq_summed, 1)

            def project(j):
                for q in range(3):
                    if isinstance(j, int) and j == 0:
                        pe.wait_ge(merged_ready, q + 2)
                    split_chunk(j + OUT_SLAB, j + OUT_ROUND, q, parts_out, rnn_r, ssd_r, skipped=NO_SPLIT)
                    if isinstance(j, int) and j == 0 and q == 0:
                        meet(pe, 4)
                if not isinstance(j, int):
                    sum_squares(j - 1)
                elif j == 1:
                    sum_squares(0, first=True)
                pe.wait_ge(xtile_ready, j + 1)
                for m in range(4):
                    for b2, n in ((0, P), (1, P), (2, NB)):
                        pe.matmul(acc[m][:, b2 * P:b2 * P + n], xtile[0:n, b2, m * P:(m + 1) * P],
                                  ident[0:n, 0:n], start=False, stop=False)
                if isinstance(j, int) and j == 0:
                    pe.wait_ge(merged_ready, GATE_N + 1)
                split_chunk(j + OUT_SLAB, j + OUT_ROUND, 3, parts_out, rnn_r, ssd_r, skipped=NO_SPLIT)

            project(0)
            project(1)
            with pe.Fori(2, OUT_N) as j:
                project(j)
            sum_squares(OUT_N - 1, last=True)
            meet(pe, 5)
            pe.wait_ge(wr_landed, 64)
            b = event(ROUTE, "logit")
            for k in range(ND):
                if k % 4 == 0:
                    pe.wait_ge(xn_ready, 4 + k // 4 + 1)
                mm = pe.matmul(b[0:20, 0:T], wr[:, k, :], xn[:, k, :], start=(k == 0), stop=(k == ND - 1))
            mm.then_inc(side_full, 1)
            pe.wait_ge(logits_out, 1)
            b = event(ROUTE, "logit_tok")
            for b2, n in ((0, P), (1, P), (2, NB)):
                mm = pe.transpose(b[0:n, 20 * b2:20 * b2 + 20], lg_f[0:20, b2 * P:b2 * P + n], ident[0:20, 0:20])
            mm.then_inc(side_full, 1)
            for k in range(12):
                b = event(ROUTE, f"xt{k}")
                b2, n = k // 4, (P, P, NB)[k // 4]
                for m in range(4):
                    mm = pe.transpose(b[0:n, m * P:(m + 1) * P], xn[:, 4 * (k % 4) + m, b2 * P:b2 * P + n],
                                      ident[:, :])
                mm.then_inc(side_full, 1)
            pe.wait_ge(member_ready, 1)
            pe.wait_ge(moe_consts, 1)
            b = event(ROUTE, "rank")
            for b2 in range(3):
                for b3 in range(b2 + 1):
                    pe.matmul(b[:, 16 * b2:16 * b2 + 16], before[:, :] if b3 == b2 else ones[:, :],
                              member[:, b3, :], start=(b3 == 0), stop=(b3 == b2))
            for b3 in range(3):
                mm = pe.matmul(b[:, 48:64], ones[:, :], member[:, b3, :], start=(b3 == 0), stop=(b3 == 2))
            mm.then_inc(side_full, 1)
            pe.wait_ge(xt_ready, 1)
            pe.wait_ge(rounds_ready, 1)
            n_rounds = pe.value_load(rounds[0:1, 0:1], min_val=1, max_val=MAX_ROUNDS)

            def moe_event(table, name, r, it=0):
                b = table.bank[name]
                pe.wait_ge(side_free[b], r * ROUND_BANK[b] + table.earlier(name, it))
                return side[b]

            def bank(pair_n, k):
                j = {GATE0: 0, UP0: 1, GATE1: 2, UP1: 3}.get(k - k % 4, k % 4)
                if k >= DOWN0 or k % 4 == 0:
                    uses = MOE_ROUND + (0 if k < DOWN0 else 1 if k < DOWN1 else 2)
                    pe.wait_ge(acc_free[j], pair_n * 3 + uses)
                return acc[j]

            def moe_chunk(n, pair_n, k):
                b, q = bank(pair_n, k), k % 4
                down = k >= DOWN0
                for m in range(4):
                    s = (2 * k + m // 2) % TURNS
                    if m % 2 == 0:
                        pe.wait_ge(lo_ready, n * 2 + (2 * k + m // 2 + 1))
                    t = m if down else 4 * q + m
                    x_h, x_l = (hid_h, hid_l) if down else (xg_h, xg_l)
                    first, last = (down or q == 0) and m == 0, (down or q == 3) and m == 3
                    pe.matmul(b[:, :], x_h[:, t, :], w_h[s][:, m % 2, :], start=first, stop=False)
                    pe.matmul(b[:, :], x_h[:, t, :], w_l[s][:, m % 2, :], start=False, stop=False)
                    mm = pe.matmul(b[:, :], x_l[:, t, :], w_h[s][:, m % 2, :], start=False, stop=last)
                    if m % 2 == 1:
                        mm.then_inc(moe_used, 1)

            def gather(table, r, it, gs):
                for g in gs:
                    b = moe_event(table, f"G{g}", r, it)
                    for m in range(4):
                        c = (4 * g + m) * P
                        for b2 in range(3):
                            mm = pe.matmul(b[:, m * P:(m + 1) * P], xt[:, b2, c:c + P], pick[:, b2, :],
                                           start=(b2 == 0), stop=(b2 == 2))
                    mm.then_inc(side_full, 1)

            def scatter(table, r, it, ks):
                for k in ks:
                    b = moe_event(table, f"S{k}", r, it)
                    c = slice(k * P, (k + 1) * P)
                    pe.matmul(b[:, 0:T], y_h[:, c], spread[:, :], start=True, stop=False)
                    pe.matmul(b[:, 0:T], y_l[:, c], spread[:, :], start=False, stop=True).then_inc(side_full, 1)

            def pair(table, r, i, it, first, last):
                done = r * PAIRS + i
                n = r * ROUND_CHUNKS + i * PAIR_CHUNKS
                pe.wait_ge(xg_ready, done * 4 + 4)
                for k in range(PAIR_CHUNKS):
                    if k == DOWN0:
                        if not last:
                            pe.wait_ge(pick_ready, done + 2)
                            gather(table, r, it, range(3))
                        pe.wait_ge(hid_ready, done * 2 + 2)
                        b = moe_event(table, "hidT", r, it)
                        for m in range(4):
                            mm = pe.transpose(b[:, m * P:(m + 1) * P], hid[:, m * P:(m + 1) * P], ident[:, :])
                        mm.then_inc(side_full, 1)
                        if not last:
                            gather(table, r, it, range(3, 4))
                        pe.wait_ge(hidt_ready, done + 1)
                    moe_chunk(n, done, k)
                    if not first and 0 <= k - SCATTER_AT < 4:
                        if k == SCATTER_AT:
                            pe.wait_ge(y_out, done * 8)
                            pe.wait_ge(spread_ready, done)
                        s0 = 4 * (k - SCATTER_AT)
                        scatter(table, r, it, range(s0, s0 + 4))
                    if k == SCATTER_AT + 4:
                        b = moe_event(table, "spread", r, it)
                        for b2, m in ((0, P), (1, P), (2, NB)):
                            pe.transpose(b[:, b2 * P:b2 * P + m], pick[0:m, b2, :], ident[0:m, 0:m])
                        for b2 in range(3):
                            mm = pe.matmul(b[:, T:T + 2], pick[:, b2, :], comb[:, b2, bass.ds(i * 2, 2)],
                                           start=(b2 == 0), stop=(b2 == 2))
                        mm.then_inc(side_full, 1)

            with pe.Fori(0, n_rounds) as r:
                pe.wait_ge(pick_ready, r * PAIRS + 1)
                gather(MOE_BEGIN, r, 0, range(4))
                pair(MOE_FIRST, r, 0, 0, True, False)
                with pe.Fori(1, PAIRS - 1) as i:
                    pair(MOE_MID, r, i, i - 1, False, False)
                pair(MOE_LAST, r, PAIRS - 1, 0, False, True)
                pe.wait_ge(y_out, r * (8 * PAIRS) + 8 * PAIRS)
                pe.wait_ge(spread_ready, r * PAIRS + PAIRS)
                scatter(MOE_END, r, 0, range(ND))
            meet(pe, 6)
            for k in range(ND):
                if k % 4 == 0:
                    pe.wait_ge(fin_sq, k // 4 + 1)
                mm = pe.matmul(side[0][:, 0:T], ones[:, :], sq2[:, k, :], start=(k == 0), stop=(k == ND - 1))
            mm.then_inc(fin_full, 1)
            for k in range(12):
                g, b2, n = k // 3, k % 3, (P, P, NB)[k % 3]
                if b2 == 0:
                    pe.wait_ge(xn_ready, 8 + g + 1)
                b = FINAL.bank[f"o{k}"]
                wait_pos(pe, fin_free[b], FINAL.earlier(f"o{k}"))
                for m in range(4):
                    mm = pe.transpose(side[b][0:n, m * P:(m + 1) * P], xn[:, 4 * g + m, b2 * P:b2 * P + n],
                                      ident[:, :])
                mm.then_inc(fin_full, 1)

        def copy_out(eng, dst, src):
            if eng.engine == mybir.EngineType.Activation:
                return eng.activation(dst, src, ACT.Copy)
            return eng.tensor_copy(dst, src)

        def states_stored(eng):
            for q in range(4):
                eng.wait_ge(h_stored[q], 16 * GROUPS)
            eng.wait_ge(hf_stored, 16 * GROUPS)

        def rows_out(eng, k):
            eng.wait_ge(side_full, ROWS.full(f"row{k}"))
            b = ROWS.bank[f"row{k}"]
            if k < 12:
                dst, n = row_s[0:27, k * 512:(k + 1) * 512], 27
            elif k < 16:
                dst, n = row_r[0:27, (k - 12) * 512:(k - 11) * 512], 27
            else:
                dst, n = row_h[0:9, (k - 16) * 512:(k - 15) * 512], 9
            copy_out(eng, dst, side[b][0:n, :]).then_inc(side_free[b], 1)

        @block.scalar
        def _(act):
            def acc_wait(slab, j):
                act.wait_ge(tile_done, slab * 16 + (FIRST + 12 + j + 1))

            def dense_highs(parts, slab, ks, skipped=0):
                for k in ks:
                    act.wait_ge(landed[k % 4], slab * 16 + (16 * (k // 4) + 16))
                    for half in range(2):
                        if half == 0:
                            wait_pos(act, first_half_used, slab * 4 + (k - DENSE_AHEAD + 1 - skipped))
                        else:
                            act.wait_ge(tile_done, slab * 16 + (FIRST + 4 * (k - DENSE_AHEAD) + 4))
                        act.activation(parts[0][(2 * k + half) % DENSE_TURNS][:, :, :],
                                       ring[:, k % 4, 2 * half:2 * half + 2, :], ACT.Copy).then_inc(dense_high, 1)

            def pad_in(c, slab):
                wait_pos(act, conv_done, c)
                wait_pos(act, stash_done, c)
                for j in range(4):
                    acc_wait(slab, j)
                    act.activation(xp[:, j, HIST:S0], acc[j][:, 0:SEQ], ACT.Copy)
                    act.activation(xp[:, j, S0:XPW].rearrange("p (b k) -> p b k", k=TAPS)[:, :, HIST],
                                   acc[j][:, SEQ:T], ACT.Copy).then_inc(acc_free[j], 1)
                act.drain().then_inc(xp_in, 1)

            def squares(dst, src):
                for k in range(4):
                    act.activation(dst[:, 4 * k:4 * k + 4, :], src[:, 4 * k:4 * k + 4, :], ACT.Square)\
                        .then_inc(sq_ready, 1)

            def root(table, name, n, it=0):
                act.wait_ge(side_full, table.full(name, it))
                act.activation(rs[:, :], side[table.bank[name]][:, 0:T], ACT.Sqrt, bias=eps[:, 0:1],
                               scale=1.0 / n).then_inc(side_free[table.bank[name]], 1)
                act.drain().then_inc(root_ready, 1)

            def rows(dst, src):
                act.dma_start(dst, src).then_inc(small_landed, 16)

            def vrows(col, name, n, view="o (r c) -> (o r) c"):
                v = a[name].rearrange(view, c=P)
                done = 0
                while done < n:
                    k, r = divmod(col + done, P)
                    m = min(n - done, P - r)
                    rows(vrow[r:r + m, k, :], v[done:done + m, :])
                    done += m

            vrows(V_MIX, "norm_mix", 16)
            vrows(V_CRW, "conv_rnn_w", 64, "o k (r c) -> (o k r) c")
            vrows(V_CRB, "conv_rnn_b", 16)
            rows(vrow[V_BA:V_BA + 16, 0, :], a["lru_ba"][0])
            rows(vrow[V_BX:V_BX + 16, 0, :], a["lru_bx"][0])
            vrows(V_LAM, "lru_lambda", 16)
            vrows(V_NSSD, "norm_ssd", 32)
            vrows(V_FFN, "norm_ffn", 16)
            rows(vrow[V_FIN - P:V_FIN - P + 16, 1, :], a["norm_final"].rearrange("(r c) -> r c", c=P))
            vrows(V_CSB, "conv_ssd_b", 48)
            vrows(V_CSW, "conv_ssd_w", 192, "o k (r c) -> (o k r) c")
            rows(hrow_r[0:24, :], a["state_rglru_conv"][0].rearrange("b k n -> (b k) n"))
            rows(hrow_r[24:32, :], a["state_rglru_h"][0])
            rows(hrow_s[0:24, :], a["state_ssd_conv"][0].rearrange("b k n -> (b k) n"))
            rows(dt_b[0:HEADS, :], a["dt_bias"].rearrange("o h -> h o"))
            rows(a_neg[0:HEADS, :], a["a_log"].rearrange("o h -> h o"))
            rows(d_bc[:, :], a["d_skip"].broadcast_to([P, HEADS]))

            for t in range(ND):
                act.wait_ge(tile_done, t + 1)
                act.activation(xT0[:, t, :], acc[t % 4][:, 0:T], ACT.Copy).then_inc(xt_done, 1)
            act.wait_ge(xt_done, ND)
            squares(xn, xT0)
            root(SETUP, "ss1", D)
            for k in range(4):
                act.wait_ge(xn_ready, k + 1)
                act.activation(xn_h[:, 4 * k:4 * k + 4, :], xT0[:, 4 * k:4 * k + 4, :], ACT.Copy).then_inc(xn_high, 1)
            def highs(slab, ks):
                dense_highs(parts_rnn, slab, ks)

            highs(0, range(2))
            act.wait_ge(dve_step, 1)
            act.activation(lm[:, 1, :], lm[:, 0, :], ACT.Exp, scale=-1.0).then_inc(act_step, 1)
            act.wait_ge(small_landed, 16 * 18)
            act.activation(a_neg[0:HEADS, :], a_neg[0:HEADS, :], ACT.Exp).then_inc(act_step, 1)
            act.wait_ge(dve_step, 2)
            act.activation(sm_e[0:HEADS, :], sm_u[0:HEADS, :], ACT.Exp, scale=-1.0).then_inc(act_step, 1)
            act.wait_ge(dve_step, 3)
            act.activation(sd_f[0:HEADS, 0:NB], sm_r[0:HEADS, SEQ:T], ACT.Exp).then_inc(act_step, 1)
            act.wait_ge(dve_step, 4)
            act.activation(wts[:, 2:5, :], wts[:, 2:5, :], ACT.Exp).then_inc(act_step, 1)
            meet(act, 1)

            def rnn(i, slab, up):
                highs(slab, range(2, 5))
                pad_in(i, slab)
                highs(slab, range(5, 9) if up else range(5, 8))
                wait_pos(act, y_ready, i)
                for j in range(4):
                    acc_wait(slab + 1, j)
                    act.activation(ge[:, j, :], acc[j][:, 0:T], ACT.Gelu_apprx_tanh).then_inc(acc_free[j], 1)
                act.drain().then_inc(gelu_ready, 1)
                highs(slab, range(9, 10) if up else range(8, 10))
                for name, dst, col in (("r", gr, V_BA), ("i", gi, V_BX)):
                    for j in range(4):
                        act.wait_ge(side_full, RNN.full(f"{name}{j}", i))
                        act.activation(dst[:, j, :], side[j][:, 0:T], ACT.Sigmoid,
                                       bias=vec[:, bass.ds(i * 4 + (col + j), 1)]).then_inc(side_free[j], 1)
                    if up and name == "r":
                        highs(slab, range(10, 11))
                act.drain().then_inc(gates_ready, 1)
                for j in range(4):
                    act.activation(ga[:, j, :], gr[:, j, :], ACT.Exp, scale=c8[:, 0, bass.ds(i * 4 + j, 1)])
                if up:
                    highs(slab, range(11, 12))
                for j in range(4):
                    act.activation(gt[:, j, :], gr[:, j, :], ACT.Tanh, scale=c8[:, 1, bass.ds(i * 4 + j, 1)])
                act.drain().then_inc(decay_ready, 1)
                act.wait_ge(m2_ready, i + 1)
                act.activation(gm[:, :, :], gm[:, :, :], ACT.Sqrt).then_inc(mult_ready, 1)
                if up:
                    highs(slab, range(12, 14))

            rnn(0, 0, False)
            with act.Fori(1, RNN_N) as i:
                rnn(i, i * 3 - 1, True)

            def silu_bc(i):
                act.wait_ge(conv_done, i + (RNN_N + 1))
                act.activation(bc[:, bass.ds(i * 4, 4), :], cx[:, :, :], ACT.Silu).then_inc(bc_ready, 1)

            highs(BC_SLAB - 1, range(2, 5))
            pad_in(RNN_N, BC_SLAB - 1)
            highs(BC_SLAB - 1, range(5, 6))
            highs(BC_SLAB, range(2, 6))
            with act.Fori(1, BC_N - 1) as i:
                highs(i + BC_SLAB, range(2, 4))
                silu_bc(i - 1)
                highs(i + BC_SLAB, range(4, 5))
                pad_in(i + RNN_N, i + BC_SLAB)
                highs(i + BC_SLAB, range(5, 6))
            highs(BC_SLAB + BC_N - 1, range(2, 4))
            silu_bc(BC_N - 2)
            pad_in(BC_N - 1 + RNN_N, BC_SLAB + BC_N - 1)
            silu_bc(BC_N - 1)
            meet(act, 2)

            def ssd(g, slab, first):
                if not first:
                    act.wait_ge(side_full, SSD.full("y1", g - 1))
                for k in range(4):
                    act.wait_ge(diffed, g * 4 + (k + 1))
                    b = SSD.bank[f"cs{k}"]
                    act.activation(ec[:, 2 * k:2 * k + 2, :],
                                   side[b][:, :].rearrange("p (h l) -> p h l", h=2)[:, :, CH:SEQ],
                                   ACT.Exp).then_inc(side_free[b], 1)
                act.drain().then_inc(ecs_ready, 1)
                for c in range(2):
                    act.activation(dm[c], dm[c], ACT.Exp).then_inc(exp_ready, 1)
                for name, dst in (("Bb", bb), ("Cb", cb)):
                    for m in range(2):
                        act.wait_ge(side_full, SSD.full(f"{name}{m}", g))
                        b = SSD.bank[f"{name}{m}"]
                        act.activation(dst[:, 4 * m:4 * m + 4, :], side[b][:, :].rearrange("p (b n) -> p b n", b=4),
                                       ACT.Copy).then_inc(side_free[b], 1)
                act.drain().then_inc(bcb_ready, 1)
                pad_in(g + (RNN_N + BC_N), slab)
                act.wait_ge(conv_done, g + (RNN_N + BC_N + 1))
                act.activation(cx[:, :, :], cx[:, :, :], ACT.Silu).then_inc(xs_ready, 1)
                wait_pos(act, yz_ready, g)
                for j in range(4):
                    acc_wait(slab + 1, j)
                    act.activation(sz[:, j, :], acc[j][:, 0:T], ACT.Silu).then_inc(acc_free[j], 1)
                act.drain().then_inc(sz_ready, 1)
                act.wait_ge(yz_ready, g + 1)
                act.wait_ge(side_full, SSD.full("y1", g))
                act.activation(sq_g, yv, ACT.Square).then_inc(sqg_ready, 1)
                root(SSD, "gn", 4 * P, g)

            ssd(0, SSD_SLAB, True)
            with act.Fori(1, GROUPS) as g:
                ssd(g, g * 3 + (SSD_SLAB - 1), False)
            act.wait_ge(cur_ready, 4 * GROUPS)
            for k in range(4):
                act.activation(gate_h[:, 4 * k:4 * k + 4, :], xn[:, 4 * k:4 * k + 4, :], ACT.Copy).then_inc(xn_high, 1)
            meet(act, 3)
            states_stored(act)

            def highs(slab, ks):
                dense_highs(parts_out, slab, ks, NO_SPLIT)

            highs(GATE_SLAB, range(2))
            for k in range(1, 20, 2):
                rows_out(act, k)

            def sigmoids(slab, dst):
                for j in range(4):
                    acc_wait(slab, j)
                    act.activation(dst[:, j, :], acc[j][:, 0:T], ACT.Sigmoid).then_inc(acc_free[j], 1)
                act.drain().then_inc(sg_ready, 1)

            with act.Fori(0, GATE_N) as j:
                highs(j * 2 + GATE_SLAB, range(2, 5))
                act.wait_ge(merged_ready, j + 1)
                sigmoids(j * 2 + GATE_SLAB, g1)
                highs(j * 2 + (GATE_SLAB + 1), range(1, 5))
                sigmoids(j * 2 + (GATE_SLAB + 1), g2)
                highs(j * 2 + (GATE_SLAB + 1), range(5, 6))
            meet(act, 4)

            def square_slab(j):
                wait_pos(act, sq_summed, j)
                act.wait_ge(projected, j + 1)
                act.activation(sq_res[:, :, :], xres[:, bass.ds(j * 4, 4), :], ACT.Square).then_inc(sq_ready, 1)

            with act.Fori(0, OUT_N - 1) as j:
                highs(j + OUT_SLAB, range(2, 6))
                square_slab(j)
            highs(OUT_SLAB + OUT_N - 1, range(2, 4))
            square_slab(OUT_N - 1)
            root(ROUTE, "ss2", D)
            meet(act, 5)
            act.wait_ge(side_full, ROUTE.full("logit"))
            act.activation(lg_f[0:20, :], side[1][0:20, 0:T], ACT.Copy).then_inc(side_free[1], 1)
            act.drain().then_inc(logits_out, 1)
            act.wait_ge(xt_clear, 1)
            for k in range(12):
                act.wait_ge(side_full, ROUTE.full(f"xt{k}"))
                b, n = ROUTE.bank[f"xt{k}"], (P, P, NB)[k // 4]
                act.activation(xt[0:n, k // 4, (k % 4) * 512:(k % 4 + 1) * 512], side[b][0:n, :], ACT.Copy)\
                    .then_inc(side_free[b], 1)
            act.drain().then_inc(xt_ready, 1)
            act.wait_ge(dve_step, 5)
            act.activation(rt[0][:, :, :], rt[0][:, :, :], ACT.Exp).then_inc(route_exp, 1)
            act.wait_ge(xt_ready, 1)
            act.wait_ge(rounds_ready, 1)
            n_rounds = act.value_load(rounds[0:1, 0:1], min_val=1, max_val=MAX_ROUNDS)

            def high(n, slab, k, first=False):
                act.wait_ge(landed[k % 4], slab * 16 + (16 * (k // 4) + 16))
                for half in range(2):
                    h = 2 * k + half
                    if not first:
                        act.wait_ge(moe_used, n * 2 + (h - TURNS + 1))
                    act.activation(w_h[h % TURNS][:, :, :], ring[:, k % 4, 2 * half:2 * half + 2, :], ACT.Copy)\
                        .then_inc(hi_ready, 1)

            def gathered(table, r, it, gs):
                for g in gs:
                    act.wait_ge(side_full, r * ROUND_EVENTS + table.full(f"G{g}", it))
                    act.activation(xg_h[:, 4 * g:4 * g + 4, :], side[g][:, :].rearrange("p (t n) -> p t n", n=P),
                                   ACT.Copy).then_inc(xgh_ready, 1)

            def pair(table, r, i, it, last):
                done = r * PAIRS + i
                n = r * ROUND_CHUNKS + i * PAIR_CHUNKS
                slab = r * ROUND_SLABS + i * 6 + MOE_SLAB
                for k in range(PAIR_CHUNKS):
                    if not (last and k >= PAIR_CHUNKS - AHEAD):
                        high(n, slab, k + AHEAD)
                    if k in (GATE0 + 3, GATE1 + 3):
                        half = slice(0, SLOTS) if k < GATE1 else slice(SLOTS, P)
                        j = 0 if k < GATE1 else 2
                        act.wait_ge(moe_used, n * 2 + (2 * k + 2))
                        act.activation(hgate[half, :], acc[j][half, :], ACT.Silu).then_inc(acc_free[j], 1)
                        act.drain().then_inc(hgate_ready, 1)
                    if k == UP1 + 3:
                        if not last:
                            gathered(table, r, it, range(3))
                        act.wait_ge(side_full, r * ROUND_EVENTS + table.full("hidT", it))
                        act.activation(hid_h[:, :, :], side[0][:, :].rearrange("p (t n) -> p t n", n=P), ACT.Copy)\
                            .then_inc(hidh_ready, 1)
                        if not last:
                            gathered(table, r, it, range(3, 4))
                    if k >= DOWN0:
                        half = slice(0, SLOTS) if k < DOWN1 else slice(SLOTS, P)
                        q = k % 4
                        act.wait_ge(spread_ready, done + 1)
                        act.wait_ge(moe_used, n * 2 + (2 * k + 2))
                        act.activation(y_h[half, q * 512:(q + 1) * 512], acc[q][half, :], ACT.Copy,
                                       scale=w_slot[half, 0:1]).then_inc(yh_ready, 1)

            with act.Fori(0, n_rounds) as r:
                act.wait_ge(pick_ready, r * PAIRS + 1)
                for k in range(AHEAD):
                    high(0, r * ROUND_SLABS + MOE_SLAB, k, first=True)
                gathered(MOE_BEGIN, r, 0, range(4))
                pair(MOE_FIRST, r, 0, 0, False)
                with act.Fori(1, PAIRS - 1) as i:
                    pair(MOE_MID, r, i, i - 1, False)
                pair(MOE_LAST, r, PAIRS - 1, 0, True)
            meet(act, 6)
            for k in range(4):
                act.activation(sq2[:, 4 * k:4 * k + 4, :], xres[:, 4 * k:4 * k + 4, :], ACT.Square)\
                    .then_inc(fin_sq, 1)
            act.wait_ge(fin_full, 1)
            act.activation(rs[:, :], side[0][:, 0:T], ACT.Sqrt, bias=eps[:, 0:1], scale=1.0 / D)\
                .then_inc(fin_free[0], 1)
            act.drain().then_inc(fin_root, 1)
            for k in range(12):
                act.wait_ge(fin_full, FINAL.full(f"o{k}"))
                b, n = FINAL.bank[f"o{k}"], (P, P, NB)[k % 3]
                act.activation(ytok[0:n, k % 3, (k // 3) * 512:(k // 3 + 1) * 512], side[b][0:n, :], ACT.Copy)\
                    .then_inc(fin_free[b], 1)
                if k % 3 == 2:
                    act.drain().then_inc(ytok_ready, 1)

        @block.vector
        def _(dve):
            def acc_wait(slab, q, j):
                dve.wait_ge(tile_done, slab * 16 + (FIRST + 4 * q + j + 1))

            def free(table, name):
                return side_free[table.bank[name]]

            def evac(table, name, it, dst, src):
                dve.wait_ge(side_full, table.full(name, it))
                dve.tensor_copy(dst, src).then_inc(free(table, name), 1)

            def conv(c, w_col, w_step, b_col, between=None):
                dve.wait_ge(xp_in, c + 1)
                dve.wait_ge(hist_in, c + 1)

                def tap(k, j):
                    return vec[:, bass.ds(w_col + (k * w_step + j), 1)]

                for j in range(4):
                    dve.tensor_scalar(cv[:, j, :], xp[:, j, 0:CVW], tap(0, j), vec[:, bass.ds(b_col + j, 1)],
                                      ALU.mult, ALU.add)
                for k in (1, 2):
                    dve.drain()
                    for j in range(4):
                        dve.scalar_tensor_tensor(cv[:, j, :], xp[:, j, k:k + CVW], tap(k, j), cv[:, j, :],
                                                 ALU.mult, ALU.add)
                dve.drain()
                if between is not None:
                    between()
                for j in range(4):
                    dve.scalar_tensor_tensor(cx[:, j, 0:SEQ], xp[:, j, 3:3 + SEQ], tap(3, j), cv[:, j, 0:SEQ],
                                             ALU.mult, ALU.add)
                    dve.scalar_tensor_tensor(
                        cx[:, j, SEQ:T],
                        xp[:, j, S0:XPW].rearrange("p (b k) -> p b k", k=TAPS)[:, :, HIST], tap(3, j),
                        cvs(j), ALU.mult, ALU.add)
                dve.drain().then_inc(conv_done, 1)

            def cvs(j):
                return cv[:, j, S0:CVW:TAPS]

            def add_round(slab, q, dst):
                for j in range(4):
                    acc_wait(slab, q, j)
                    dve.tensor_tensor(dst[:, 4 * q + j, :], dst[:, 4 * q + j, :], acc[j][:, 0:T], ALU.add)\
                        .then_inc(acc_free[j], 1)

            def dense_lows(parts, slab, ks, skipped=0):
                w_h, w_l = parts
                for k in ks:
                    for half in range(2):
                        turn = (2 * k + half) % DENSE_TURNS
                        dve.wait_ge(dense_high, slab * 8 + (2 * k + half + 1 - 2 * skipped))
                        dve.tensor_tensor(w_l[turn][:, :, :], ring[:, k % 4, 2 * half:2 * half + 2, :],
                                          w_h[turn][:, :, :].bitcast(F32), ALU.subtract).then_inc(dense_low, 1)

            def norm_scale(count, src, dst, gain, ready, n=ND, root=root_ready):
                dve.wait_ge(root, count)
                dve.reciprocal(rs[:, :], rs[:, :])
                dve.drain()
                for t in range(n):
                    ins = dve.scalar_tensor_tensor(dst[:, t, :], src[:, t, :], gain(t), rs[:, :], ALU.mult, ALU.mult)
                    if t % 4 == 3:
                        ins.then_inc(ready, 1)

            def softplus(dst, v, u, e, r, s2, p, wait):
                dve.scalar_tensor_tensor(u, v, -1.0, v, ALU.mult, ALU.max).then_inc(dve_step, 1)
                dve.wait_ge(act_step, wait)
                dve.tensor_scalar(r, e, 2.0, None, ALU.add)
                dve.drain()
                dve.reciprocal(r, r)
                dve.drain()
                dve.tensor_tensor(r, r, e, ALU.mult)
                dve.drain()
                dve.tensor_tensor(s2, r, r, ALU.mult)
                dve.drain()
                dve.tensor_scalar(p, s2, 1.0 / 17, None, ALU.mult)
                for k in (15, 13, 11, 9, 7, 5, 3):
                    dve.drain()
                    dve.scalar_tensor_tensor(p, p, 1.0 / k, s2, ALU.add, ALU.mult)
                dve.drain()
                dve.scalar_tensor_tensor(p, p, 1.0, r, ALU.add, ALU.mult)
                dve.tensor_scalar(u, v, 0.0, None, ALU.max)
                dve.drain()
                dve.scalar_tensor_tensor(dst, p, 2.0, u, ALU.mult, ALU.add)
                dve.drain()

            dve.wait_ge(side_full, SETUP.full("vec"))
            dve.tensor_copy(vec[:, :], side[0][:, 0:NV]).then_inc(side_free[0], 1)
            dve.drain()
            norm_scale(1, xT0, xT0, lambda t: vec[:, V_MIX + t:V_MIX + t + 1], xn_ready)
            for k in range(4):
                dve.wait_ge(xn_high, k + 1)
                dve.tensor_tensor(xn_l[:, 4 * k:4 * k + 4, :], xT0[:, 4 * k:4 * k + 4, :],
                                  xn_h[:, 4 * k:4 * k + 4, :].bitcast(F32), ALU.subtract)
            dve.drain().then_inc(xn_split, 1)

            def lows(slab, ks):
                dense_lows(parts_rnn, slab, ks)

            dve.wait_ge(side_full, SETUP.full("dt"))
            dve.wait_ge(small_landed, 16 * 18)
            dve.tensor_scalar(sm_s[0:HEADS, :], side[2][0:HEADS, 0:T], dt_b[0:HEADS, :], None, ALU.add)\
                .then_inc(side_free[2], 1)
            lows(0, range(2))
            dve.wait_ge(small_landed, 16 * 18)
            dve.tensor_copy(d_col[0:HD, :], d_bc[0:HD, 0:HEADS:2])
            dve.tensor_copy(d_col[HD:P, :], d_bc[HD:P, 1:HEADS:2])
            dve.tensor_scalar(lm[:, 4, :], vec[:, V_LAM:V_LAM + ND], -1.0, None, ALU.mult)
            dve.drain()
            softplus(lm[:, 2, :], lm[:, 4, :], lm[:, 0, :], lm[:, 1, :], lm[:, 2, :], lm[:, 3, :],
                     sm_p[:, 0:ND], 1)
            dve.tensor_scalar(c8[:, 0, :], lm[:, 2, :], -8.0, None, ALU.mult)
            dve.tensor_scalar(c8[:, 1, :], lm[:, 2, :], 8.0, None, ALU.mult)
            h = slice(0, HEADS)
            softplus(dt_f[h, :], sm_s[h, :], sm_u[h, :], sm_e[h, :], dt_f[h, :], sm_r[h, :], sm_p[h, :], 3)
            dve.tensor_scalar(a_neg[h, :], a_neg[h, :], -1.0, None, ALU.mult)
            dve.drain()
            dve.tensor_scalar(sm_r[h, :], dt_f[h, :], a_neg[h, :], None, ALU.mult)
            dve.tensor_copy(sd_f[h, NB:2 * NB], dt_f[h, SEQ:T])
            dve.drain().then_inc(dve_step, 1)
            evac(SETUP, "hr", 0, hist_r[:, :, :], side[1][:, :].rearrange("p (t n) -> p t n", n=32))
            for m in range(3):
                evac(SETUP, f"hs{m}", 0, hist_s[:, 16 * m:16 * m + 16, 0:24],
                     side[(2, 3, 0)[m]][:, 0:384].rearrange("p (t n) -> p t n", n=24))
            dve.drain()
            for c in range(2):
                dve.tensor_tensor_scan(cs_f[h, c * CH:(c + 1) * CH], ones[h, :], sm_r[h, c * CH:(c + 1) * CH],
                                       0.0, ALU.mult, ALU.add)
            dve.drain()
            for c in range(2):
                dve.tensor_scalar(dg[h, c, :], ident[h, 0:HEADS], cs_f[h, (c + 1) * CH - 1:(c + 1) * CH], None,
                                  ALU.mult)
            dve.drain().then_inc(tok_ready, 1)
            dve.wait_ge(side_full, SETUP.full("tot"))
            dve.tensor_copy(dt_tok[:, :, :], side[3][:, 0:P].rearrange("p (c h) -> p c h", c=2))
            dve.tensor_copy(cs_tok[:, :, :], side[3][:, P:2 * P].rearrange("p (c h) -> p c h", c=2))\
                .then_inc(side_free[3], 1)
            dve.tensor_copy(tot[:, :, :], side[0][:, 0:P].rearrange("p (c h) -> p c h", c=2))\
                .then_inc(side_free[0], 1)
            dve.drain()
            dve.tensor_tensor(wts[:, 2, :], tot[:, 0, :], cs_tok[:, 0, :], ALU.subtract)
            dve.tensor_tensor(wts[:, 4, :], tot[:, 1, :], cs_tok[:, 1, :], ALU.subtract)
            dve.drain()
            dve.tensor_tensor(wts[:, 3, :], wts[:, 2, :], tot[:, 1, :], ALU.add)
            dve.tensor_copy(wts[:, 0:2, :], dt_tok[:, :, :])
            dve.drain().then_inc(dve_step, 1)
            dve.wait_ge(act_step, 5)
            for k, c in ((2, 0), (3, 0), (4, 1)):
                dve.tensor_tensor(wts[:, k, :], wts[:, k, :], dt_tok[:, c, :], ALU.mult)
            meet(dve, 1)

            def rnn(i, slab, up):
                lows(slab, range(2, 6))
                conv(i, i * 4 + V_CRW, ND, i * 4 + V_CRB, lambda: lows(slab, range(6, 7)))
                lows(slab, range(7, 10))
                if up:
                    add_round(slab + 2, 0, acc_rnn)
                    lows(slab, range(10, 11))
                    add_round(slab + 2, 1, acc_rnn)
                    lows(slab, range(11, 12))
                dve.wait_ge(decay_ready, i + 1)
                dve.tensor_tensor(gr[:, :, :], ga[:, :, :], ga[:, :, :], ALU.mult)
                dve.drain()
                dve.scalar_tensor_tensor(gm[:, :, :], gr[:, :, :], 1.0, gt[:, :, :], ALU.add, ALU.mult)\
                    .then_inc(m2_ready, 1)
                dve.tensor_tensor(gi[:, :, :], gi[:, :, :], cx[:, :, :], ALU.mult)
                if up:
                    add_round(slab + 2, 2, acc_rnn)
                    lows(slab, range(12, 13))
                    add_round(slab + 2, 3, acc_rnn)
                    lows(slab, range(13, 14))
                dve.wait_ge(mult_ready, i + 1)
                dve.memset(gm[:, :, 0:1], 1.0)
                dve.drain()
                dve.tensor_tensor(gi[:, :, :], gi[:, :, :], gm[:, :, :], ALU.mult)
                dve.tensor_tensor(gs[:, :, :], ga[:, :, SEQ:T], hist_r[:, bass.ds(i * 4, 4), 24:32], ALU.mult)
                dve.drain()
                wait_pos(dve, h_stashed, i)
                for j in range(4):
                    dve.tensor_tensor_scan(hh[:, j, 0:SEQ], ga[:, j, 0:SEQ], gi[:, j, 0:SEQ], 0.0,
                                           ALU.mult, ALU.add)
                dve.tensor_tensor(hh[:, :, SEQ:T], gs[:, :, :], gi[:, :, SEQ:T], ALU.add)
                dve.drain()
                dve.wait_ge(gelu_ready, i + 1)
                dve.tensor_tensor(gm[:, :, :], hh[:, :, :], ge[:, :, :], ALU.mult)
                dve.drain()
                dve.tensor_copy(yr_h[:, :, :], gm[:, :, :])
                dve.drain()
                dve.tensor_tensor(yr_l[:, :, :], gm[:, :, :], yr_h[:, :, :].bitcast(F32), ALU.subtract)\
                    .then_inc(y_ready, 1)

            rnn(0, 0, False)
            with dve.Fori(1, RNN_N) as i:
                rnn(i, i * 3 - 1, True)
            lows(BC_SLAB - 1, range(2, 6))
            for q in range(4):
                add_round(BC_SLAB, q, acc_rnn)
                lows(BC_SLAB, range(q + 2, q + 3))
            conv(RNN_N, V_CSW + 32, NX, V_CSB + 32, lambda: lows(BC_SLAB, range(6, 7)))

            def b_and_c(i, last):
                lows(i + BC_SLAB, range(3, 4) if last else range(3, 6))
                if last:
                    acc_wait(i + BC_SLAB, 3, 3)
                    for k in range(4):
                        t4 = slice(4 * k, 4 * k + 4)
                        dve.tensor_tensor(xn[:, t4, :], xn_h[:, t4, :].bitcast(F32), xn_l[:, t4, :].bitcast(F32),
                                          ALU.add).then_inc(xn_whole, 1)
                dve.wait_ge(bc_ready, i)
                conv(i + RNN_N, i * 4 + (V_CSW + 32), NX, i * 4 + (V_CSB + 32),
                     None if last else lambda: lows(i + BC_SLAB, range(6, 7)))

            with dve.Fori(1, BC_N - 1) as i:
                b_and_c(i, False)
            b_and_c(BC_N - 1, True)
            meet(dve, 2)

            def ssd(g, slab, up):
                dve.wait_ge(side_full, SSD.full("G", g))
                dve.tensor_tensor(gtm[:, :, :], side[0][:, 0:2 * CH].rearrange("p (c l) -> p c l", c=2),
                                  mask[:, :].unsqueeze(1).broadcast_to([P, 2, CH]), ALU.mult)\
                    .then_inc(side_free[0], 1)
                dve.wait_ge(cur_ready, g * 4 + 4)
                for k in range(4):
                    dve.wait_ge(side_full, SSD.full(f"cs{k}", g))
                    b = SSD.bank[f"cs{k}"]
                    for m in range(2):
                        for c in range(2):
                            dve.tensor_scalar(dm[c][:, 2 * k + m, :],
                                              side[b][:, m * SEQ + c * CH:m * SEQ + (c + 1) * CH],
                                              cur_cs[:, c, 2 * k + m:2 * k + m + 1], 0.0,
                                              ALU.subtract, ALU.min)
                    dve.drain().then_inc(diffed, 1)
                dve.wait_ge(side_full, SSD.full("btok", g))
                dve.tensor_copy(bcs[0:NB, :], side[0][0:NB, 2 * CH:3 * CH])
                dve.tensor_copy(ccs[0:NB, :], side[0][0:NB, 3 * CH:4 * CH])
                dve.tensor_copy(btok[:, :, :], side[0][:, 0:2 * CH].rearrange("p (c n) -> p c n", c=2))\
                    .then_inc(side_free[0], 1)
                dve.drain().then_inc(bcs_ready, 1)
                evac(SSD, "sd", g, sd[:, :, :], side[3][:, 0:64].rearrange("p (t n) -> p t n", t=4))
                for c in range(2):
                    dve.wait_ge(exp_ready, g * 2 + (c + 1))
                    dve.tensor_tensor(dm[c], dm[c], gtm[:, c, :].unsqueeze(1).broadcast_to([P, HG, CH]), ALU.mult)
                dve.drain().then_inc(m_ready, 1)
                conv(g + (RNN_N + BC_N), g * 4 + V_CSW, NX, g * 4 + V_CSB)
                dve.wait_ge(xs_ready, g + 1)
                dve.tensor_tensor(xdt_s[:, :, :], cx[:, :, SEQ:T], sd[:, :, NB:2 * NB], ALU.mult)\
                    .then_inc(xdts_ready, 1)
                dve.wait_ge(bcb_ready, g + 1)

                def decode(q):
                    dve.wait_ge(h_landed[q], g * 16 + 16)
                    hq, u = h_ring[:, q, :, :], ub[q % 2]
                    dve.tensor_tensor(hq, hq, sd[:, q, 0:NB].unsqueeze(2).broadcast_to([P, NB, NS]), ALU.mult)
                    dve.drain()
                    dve.wait_ge(u_ready, g * 4 + (q + 1))
                    dve.tensor_tensor(hq, hq, u, ALU.add)
                    dve.drain()
                    dve.tensor_tensor(u, hq, cb, ALU.mult)
                    dve.drain()
                    dve.tensor_reduce(ys[:, q, :], u, AX.X, ALU.add).then_inc(h_new, 1)

                for q in range(3):
                    decode(q)
                wait_pos(dve, hf_stored, g * 16)
                for c, ks in ((0, (0, 2, 3)), (1, (1, 4))):
                    dve.wait_ge(side_full, SSD.full(f"xt{c}", g))
                    b = SSD.bank[f"xt{c}"]
                    for k in ks:
                        ins = dve.tensor_tensor(
                            xd[k].rearrange("p (h n) -> p h n", h=HG),
                            side[b][:, :].rearrange("p (h n) -> p h n", h=HG),
                            cur_w[:, k, :].unsqueeze(2).broadcast_to([P, HG, HD]), ALU.mult)
                    ins.then_inc(side_free[b], 1)
                dve.drain().then_inc(xd_ready, 1)
                if up:
                    add_round(slab + 2, 0, acc_ssd)
                decode(3)
                if up:
                    add_round(slab + 2, 1, acc_ssd)
                dve.wait_ge(side_full, SSD.full("st0", g))
                dve.tensor_copy(st0, side[1][:, :]).then_inc(side_free[1], 1)
                dve.drain().then_inc(st_ready, 1)
                dve.wait_ge(side_full, SSD.full("hf", g))
                dve.tensor_copy(hf[:, :, :], side[2][:, :].rearrange("p (t n) -> p t n", t=4))\
                    .then_inc(side_free[2], 1)
                dve.drain().then_inc(hf_ready, 1)
                if up:
                    add_round(slab + 2, 2, acc_ssd)
                for m in range(4):
                    if m % 2 == 0:
                        dve.wait_ge(side_full, SSD.full(f"y{m // 2}", g))
                    b = SSD.bank[f"y{m // 2}"]
                    ins = dve.scalar_tensor_tensor(yv[:, m, 0:SEQ], cx[:, m, 0:SEQ], cur_d[:, m:m + 1],
                                                   side[b][:, (m % 2) * SEQ:(m % 2 + 1) * SEQ], ALU.mult, ALU.add)
                    if m % 2 == 1:
                        ins.then_inc(side_free[b], 1)
                    dve.scalar_tensor_tensor(yv[:, m, SEQ:T], cx[:, m, SEQ:T], cur_d[:, m:m + 1], ys[:, m, :],
                                             ALU.mult, ALU.add)
                dve.drain()
                dve.wait_ge(sz_ready, g + 1)
                dve.tensor_tensor(yv, yv, sz[:, :, :], ALU.mult).then_inc(yz_ready, 1)
                if up:
                    add_round(slab + 2, 3, acc_ssd)
                norm_scale(g + 2, yv, yn, lambda t: vec[:, bass.ds(g * 4 + (V_NSSD + t), 1)], yn_ready, n=4)

            ssd(0, SSD_SLAB, False)
            dve.wait_ge(ssd_zeroed, 1)
            with dve.Fori(1, GROUPS) as g:
                ssd(g, g * 3 + (SSD_SLAB - 1), True)
            for k in range(4):
                dve.wait_ge(xn_high, k + 5)
                acc_wait(GATE_SLAB - 2, 3, 3)
                dve.tensor_tensor(gate_l[:, 4 * k:4 * k + 4, :], xn[:, 4 * k:4 * k + 4, :],
                                  gate_h[:, 4 * k:4 * k + 4, :].bitcast(F32), ALU.subtract)
                add_round(GATE_SLAB - 1, k, acc_ssd)
            dve.drain().then_inc(xn_split, 1)
            meet(dve, 3)
            states_stored(dve)

            def lows(slab, ks):
                dense_lows(parts_out, slab, ks, NO_SPLIT)

            lows(GATE_SLAB, range(2))
            for k in range(0, 20, 2):
                rows_out(dve, k)
            dve.drain()
            dve.drain().then_inc(merged_ready, 1)
            for n in range(4):
                dve.wait_ge(side_free[n], ROWS.bank_end[n])
            dve.drain().then_inc(rows_ready, 1)
            with dve.Fori(0, GATE_N) as j:
                t4 = bass.ds(j * 4, 4)
                lows(j * 2 + GATE_SLAB, range(2, 6))
                dve.wait_ge(sg_ready, j * 2 + 1)
                dve.tensor_tensor(g1[:, :, :], acc_rnn[:, t4, :], g1[:, :, :], ALU.mult)
                lows(j * 2 + (GATE_SLAB + 1), range(2, 6))
                dve.wait_ge(sg_ready, j * 2 + 2)
                dve.tensor_tensor(g2[:, :, :], acc_ssd[:, t4, :], g2[:, :, :], ALU.mult)
                dve.drain()
                dve.tensor_tensor(g1[:, :, :], g1[:, :, :], g2[:, :, :], ALU.add)
                dve.drain()
                dve.tensor_copy(rnn_r[:, t4, :], g1[:, :, :])
                dve.drain()
                dve.tensor_tensor(ssd_r[:, t4, :], g1[:, :, :], rnn_r[:, t4, :].bitcast(F32), ALU.subtract)\
                    .then_inc(merged_ready, 1)
            meet(dve, 4)

            def take_slab(j):
                for m in range(4):
                    acc_wait(j + OUT_SLAB, 3, m)
                    dve.tensor_copy(xres[:, bass.ds(j * 4 + m, 1), :].squeeze(1), acc[m][:, 0:T])\
                        .then_inc(acc_free[m], 1)
                dve.drain().then_inc(projected, 1)

            with dve.Fori(0, OUT_N - 1) as j:
                lows(j + OUT_SLAB, range(2, 5))
                take_slab(j)
                lows(j + OUT_SLAB, range(5, 6))
            lows(OUT_SLAB + OUT_N - 1, range(2, 4))
            take_slab(OUT_N - 1)
            meet(dve, 5)
            norm_scale(GROUPS + 2, xres, xn, lambda t: vec[:, V_FFN + t:V_FFN + t + 1], xn_ready)

            def tt(out, x, y, op):
                dve.drain()
                return dve.tensor_tensor(out, x, y, op)

            def first_of(eq, tmp):
                dve.drain()
                dve.tensor_copy(tmp[:, :, 0:1], eq[:, :, 0:1])
                for k in range(1, 4):
                    dve.drain()
                    dve.tensor_tensor(tmp[:, :, 1:2], eq[:, :, k:k + 1], tmp[:, :, 0:1], ALU.is_gt)
                    dve.drain()
                    dve.tensor_tensor(tmp[:, :, 0:1], tmp[:, :, 0:1], eq[:, :, k:k + 1], ALU.max)
                    dve.drain()
                    dve.tensor_copy(eq[:, :, k:k + 1], tmp[:, :, 1:2])
                dve.drain()

            dve.memset(lg[:, :, :], 0.0)
            dve.drain()
            dve.wait_ge(side_full, ROUTE.full("logit_tok"))
            dve.wait_ge(wr_landed, 64)
            for b2, n in ((0, P), (1, P), (2, NB)):
                ins = dve.tensor_tensor(lg[0:n, b2, :], side[2][0:n, 20 * b2:20 * b2 + 20], br[0:n, :], ALU.add)
            ins.then_inc(side_free[2], 1)
            dve.drain()
            gl, el = lg[:, :, 0:4], lg[:, :, 4:20]
            m1, goh, es, oh1, esm, m2, oh2, tmp = [r[:, :, 0:4] for r in rt[1:9]]
            ex = rt[0]

            def wide(x):
                return x[:, :, 0:1].broadcast_to([P, 3, 4])

            dve.tensor_reduce(m1[:, :, 0:1], gl, AX.X, ALU.max)
            tt(goh, gl, wide(m1), ALU.is_equal)
            tt(ex[:, :, 0:4], gl, wide(m1), ALU.subtract)
            first_of(goh, tmp)
            for k in range(4):
                tt(rt[9][:, :, 0:4], el[:, :, 4 * k:4 * k + 4], goh[:, :, k:k + 1].broadcast_to([P, 3, 4]), ALU.mult)
                if k == 0:
                    dve.drain()
                    dve.tensor_copy(es, rt[9][:, :, 0:4])
                else:
                    tt(es, es, rt[9][:, :, 0:4], ALU.add)
            dve.drain()
            dve.tensor_reduce(m2[:, :, 0:1], es, AX.X, ALU.max)
            tt(oh1, es, wide(m2), ALU.is_equal)
            tt(ex[:, :, 4:8], es, wide(m2), ALU.subtract)
            first_of(oh1, tmp)
            dve.tensor_scalar(tmp, oh1, -3.0e38, None, ALU.mult)
            dve.tensor_scalar(esm, oh1, -1.0, 1.0, ALU.mult, ALU.add)
            tt(esm, esm, es, ALU.mult)
            tt(esm, esm, tmp, ALU.add)
            dve.drain()
            dve.tensor_reduce(m2[:, :, 0:1], esm, AX.X, ALU.max)
            tt(oh2, esm, wide(m2), ALU.is_equal)
            first_of(oh2, tmp)
            dve.memset(ex[:, :, 8:16], 0.0)
            dve.drain().then_inc(dve_step, 1)
            dve.wait_ge(route_exp, 1)
            dve.tensor_reduce(m1[:, :, 0:1], ex[:, :, 0:4], AX.X, ALU.add)
            dve.tensor_tensor(tmp, oh2, ex[:, :, 4:8], ALU.mult)
            dve.drain()
            dve.tensor_reduce(m1[:, :, 1:2], tmp, AX.X, ALU.add)
            dve.drain()
            dve.tensor_scalar(m1[:, :, 1:2], m1[:, :, 1:2], 1.0, None, ALU.add)
            dve.drain()
            dve.tensor_tensor(m1[:, :, 0:1], m1[:, :, 0:1], m1[:, :, 1:2], ALU.mult)
            dve.drain()
            dve.reciprocal(m1[:, :, 0:1], m1[:, :, 0:1])
            tt(tmp, tmp, oh1, ALU.add)
            tt(tmp, tmp, wide(m1), ALU.mult)
            for k in range(4):
                tt(comb[:, :, 4 * k:4 * k + 4], tmp, goh[:, :, k:k + 1].broadcast_to([P, 3, 4]), ALU.mult)
            dve.drain()
            tt(tmp, oh1, oh2, ALU.add)
            dve.wait_ge(moe_consts, 1)
            for k in range(4):
                tt(member[:, :, 4 * k:4 * k + 4], tmp, goh[:, :, k:k + 1].broadcast_to([P, 3, 4]), ALU.mult)
            tt(member[:, :, :], member[:, :, :], valid[:, :].unsqueeze(2).broadcast_to([P, 3, EXPERTS]), ALU.mult)
            dve.drain().then_inc(member_ready, 1)
            dve.memset(most[:, :], 0.0)
            dve.wait_ge(side_full, ROUTE.full("rank"))
            dve.tensor_scalar(slot[:, :, :], member[:, :, :], -4096.0, 4096.0, ALU.mult, ALU.add)
            dve.drain()
            dve.tensor_tensor(slot[:, :, :], side[2][:, 0:48].rearrange("p (b e) -> p b e", b=3), slot[:, :, :],
                              ALU.add)
            dve.tensor_reduce(most[:, 0:1], side[2][:, 48:64], AX.X, ALU.max).then_inc(side_free[2], 1)
            dve.drain()
            for k in range(1, MAX_ROUNDS):
                dve.tensor_scalar(most[:, k:k + 1], most[:, 0:1], float(k * SLOTS), None, ALU.is_gt)
            dve.memset(most[:, MAX_ROUNDS:MAX_ROUNDS + 1], 1.0)
            dve.drain()
            dve.tensor_reduce(most[:, 7:8], most[:, 1:MAX_ROUNDS + 1], AX.X, ALU.add)
            dve.drain()
            dve.tensor_copy(rounds[:, :], most[:, 7:8])
            dve.drain().then_inc(rounds_ready, 1)
            dve.wait_ge(xt_ready, 1)
            dve.wait_ge(rounds_ready, 1)
            n_rounds = dve.value_load(rounds[0:1, 0:1], min_val=1, max_val=MAX_ROUNDS)

            def picks(i):
                for par in range(2):
                    for b2 in range(3):
                        dve.tensor_scalar(pick[:, b2, par * SLOTS:(par + 1) * SLOTS], iota[:, :],
                                          slot[:, b2, bass.ds(i * 2 + par, 1)], None, ALU.is_equal)
                dve.drain().then_inc(pick_ready, 1)

            def low(n, k):
                for half in range(2):
                    h = 2 * k + half
                    dve.wait_ge(hi_ready, n * 2 + (h + 1))
                    dve.tensor_tensor(w_l[h % TURNS][:, :, :], ring[:, k % 4, 2 * half:2 * half + 2, :],
                                      w_h[h % TURNS][:, :, :].bitcast(F32), ALU.subtract).then_inc(lo_ready, 1)

            def gathered(table, r, it, done, gs):
                for g in gs:
                    dve.wait_ge(xgh_ready, done * 4 + (g + 1))
                    dve.tensor_tensor(xg_l[:, 4 * g:4 * g + 4, :], side[g][:, :].rearrange("p (t n) -> p t n", n=P),
                                      xg_h[:, 4 * g:4 * g + 4, :].bitcast(F32), ALU.subtract)\
                        .then_inc(side_free[g], 1)
                    dve.drain().then_inc(xg_ready, 1)

            def add_scattered(table, r, it, ks):
                for k in ks:
                    dve.wait_ge(side_full, r * ROUND_EVENTS + table.full(f"S{k}", it))
                    dve.tensor_tensor(xres[:, k, :], xres[:, k, :], side[k % 4][:, 0:T], ALU.add)\
                        .then_inc(side_free[k % 4], 1)

            def pair(table, r, i, it, first, last):
                done = r * PAIRS + i
                n = r * ROUND_CHUNKS + i * PAIR_CHUNKS
                for k in range(PAIR_CHUNKS):
                    if not (last and k >= PAIR_CHUNKS - AHEAD):
                        low(n, k + AHEAD)
                    if not first and 0 <= k - SCATTER_AT < 4:
                        s0 = 4 * (k - SCATTER_AT)
                        add_scattered(table, r, it, range(s0, s0 + 4))
                    if k == SCATTER_AT + 4:
                        dve.wait_ge(side_full, r * ROUND_EVENTS + table.full("spread", it))
                        dve.tensor_copy(spread[:, :], side[0][:, 0:T])
                        dve.tensor_copy(w_slot[0:SLOTS, :], side[0][0:SLOTS, T:T + 1])
                        dve.tensor_copy(w_slot[SLOTS:P, :], side[0][SLOTS:P, T + 1:T + 2]).then_inc(side_free[0], 1)
                        dve.drain().then_inc(spread_ready, 1)
                        if not last:
                            picks(i + 1)
                    if k in (UP0 + 3, UP1 + 3):
                        half = slice(0, SLOTS) if k < GATE1 else slice(SLOTS, P)
                        j = 1 if k < GATE1 else 3
                        dve.wait_ge(hgate_ready, done * 2 + (1 if k < GATE1 else 2))
                        dve.wait_ge(moe_used, n * 2 + (2 * k + 2))
                        dve.tensor_tensor(hid[half, :], hgate[half, :], acc[j][half, :], ALU.mult)\
                            .then_inc(acc_free[j], 1)
                        dve.drain().then_inc(hid_ready, 1)
                    if k == UP1 + 3:
                        if not last:
                            gathered(table, r, it, done + 1, range(3))
                        dve.wait_ge(hidh_ready, done + 1)
                        dve.tensor_tensor(hid_l[:, :, :], side[0][:, :].rearrange("p (t n) -> p t n", n=P),
                                          hid_h[:, :, :].bitcast(F32), ALU.subtract).then_inc(side_free[0], 1)
                        dve.drain().then_inc(hidt_ready, 1)
                        if not last:
                            gathered(table, r, it, done + 1, range(3, 4))
                    if k >= DOWN0:
                        half = slice(0, SLOTS) if k < DOWN1 else slice(SLOTS, P)
                        q = k % 4
                        c = slice(q * 512, (q + 1) * 512)
                        dve.wait_ge(yh_ready, done * 8 + (k - DOWN0 + 1))
                        dve.scalar_tensor_tensor(y_l[half, c], acc[q][half, :], w_slot[half, 0:1],
                                                 y_h[half, c].bitcast(F32), ALU.mult, ALU.subtract)\
                            .then_inc(acc_free[q], 1)
                        dve.drain().then_inc(y_out, 1)

            with dve.Fori(0, n_rounds) as r:
                picks(0)
                for k in range(AHEAD):
                    low(r * ROUND_CHUNKS, k)
                gathered(MOE_BEGIN, r, 0, r * PAIRS, range(4))
                pair(MOE_FIRST, r, 0, 0, True, False)
                with dve.Fori(1, PAIRS - 1) as i:
                    pair(MOE_MID, r, i, i - 1, False, False)
                pair(MOE_LAST, r, PAIRS - 1, 0, False, True)
                add_scattered(MOE_END, r, 0, range(ND))
                dve.tensor_scalar(slot[:, :, :], slot[:, :, :], float(SLOTS), None, ALU.subtract)
                dve.drain()
            meet(dve, 6)
            norm_scale(1, xres, xn, lambda t: vec[:, V_FIN + t:V_FIN + t + 1], xn_ready, root=fin_root)

        @block.gpsimd
        def _(pool):
            pool.memset(ident[:, :], 0.0)
            pool.memset(ones[:, :], 1.0)
            pool.memset(mask[:, :], 1.0)
            pool.memset(eps[:, :], EPS)
            pool.memset(xp[:, :, :], 0.0)
            pool.drain().then_inc(consts, 1)
            pool.wait_ge(consts, 1)
            pool.affine_select(out=ident[:, :], in_=ident[:, :], compare_op=ALU.not_equal, fill=1.0, base=0,
                               pattern=[[-1, P]], channel_multiplier=1).then_inc(consts, 1)
            pool.affine_select(out=mask[:, :], in_=mask[:, :], compare_op=ALU.is_ge, fill=0.0, base=0,
                               pattern=[[1, P]], channel_multiplier=-1).then_inc(consts, 1)
            pool.drain().then_inc(consts, 1)
            pool.wait_ge(xn_split, 1)
            pool.wait_ge(side_full, SETUP.full("dt"))
            pool.memset(acc_rnn[:, :, :], 0.0)
            meet(pool, 1)

            def hist(c, src):
                wait_pos(pool, conv_done, c)
                pool.tensor_copy(xp[:, :, S0:XPW].rearrange("p t (b k) -> p t b k", k=TAPS)[:, :, :, 0:HIST],
                                 src.rearrange("p t (b k) -> p t b k", k=HIST)).then_inc(hist_in, 1)

            def stash(c, dst):
                pool.wait_ge(hist_in, c + 1)
                pool.wait_ge(xp_in, c + 1)
                pool.sem_inc(stash_begun, 1)
                pool.tensor_copy(dst[:, :, 0:24].rearrange("p t (b k) -> p t b k", k=HIST),
                                 xp[:, :, S0:XPW].rearrange("p t (b k) -> p t b k", k=TAPS)[:, :, :, 1:TAPS])
                pool.tensor_copy(dst[:, :, 24:27], xp[:, :, S0 - HIST:S0])
                pool.drain().then_inc(stash_done, 1)

            def rnn(i):
                t4 = bass.ds(i * 4, 4)
                hist(i, hist_r[:, t4, 0:24])
                stash(i, stash_r[:, t4, :])
                pool.wait_ge(y_ready, i + 1)
                pool.tensor_copy(stash_h[:, t4, :], hh[:, :, SEQ - 1:T]).then_inc(h_stashed, 1)

            rnn(0)
            with pool.Fori(1, RNN_N) as i:
                rnn(i)
            with pool.Fori(0, BC_N) as i:
                t4 = bass.ds(i * 4 + 32, 4)
                hist(i + RNN_N, hist_s[:, t4, 0:24])
                stash(i + RNN_N, stash_s[:, t4, :])
            meet(pool, 2)
            pool.tensor_copy(selb[0:NB, :, :], ident[0:NB, 0:NB].unsqueeze(2).broadcast_to([NB, NB, P]))

            def ssd(g, first):
                t4 = bass.ds(g * 4, 4)
                if not first:
                    pool.wait_ge(side_full, SSD.full("sd", g - 1))
                    pool.wait_ge(xd_ready, g)
                    pool.wait_ge(yz_ready, g)
                pool.tensor_copy(bcur[:, :], bc[:, bass.ds(g, 1), :].squeeze(1)).then_inc(cur_ready, 1)
                pool.tensor_copy(ccur[:, :], bc[:, bass.ds(g + GROUPS, 1), :].squeeze(1)).then_inc(cur_ready, 1)
                pool.tensor_copy(sel[0:HEADS, :, :], ident[0:HEADS, bass.ds(g * HG, HG)].unsqueeze(2)
                                 .broadcast_to([HEADS, HG, P])).then_inc(cur_ready, 1)
                pool.tensor_copy(cur_cs[:, :, :], cs_tok[:, :, bass.ds(g * HG, HG)])
                pool.tensor_copy(cur_d[:, :], d_col[:, t4])
                pool.tensor_copy(cur_w[:, :, :], wts[:, :, bass.ds(g * HG, HG)]).then_inc(cur_ready, 1)
                hist(g + (RNN_N + BC_N), hist_s[:, t4, 0:24])
                pool.wait_ge(ecs_ready, g + 1)
                pool.wait_ge(cur_ready, g * 4 + 2)
                pool.tensor_tensor(ec, ec, ccur[:, CH:SEQ].unsqueeze(1).broadcast_to([P, HG, CH]), ALU.mult)\
                    .then_inc(cts_ready, 1)
                stash(g + (RNN_N + BC_N), stash_s[:, t4, :])
                pool.wait_ge(xdts_ready, g + 1)
                pool.wait_ge(bcb_ready, g + 1)
                for q in range(4):
                    if q >= 2:
                        pool.wait_ge(h_new, g * 4 + (q - 1))
                    elif not first:
                        pool.wait_ge(h_new, g * 4 + (q - 1))
                    pool.tensor_tensor(ub[q % 2], bb, xdt_s[:, q, :].unsqueeze(2).broadcast_to([P, NB, NS]),
                                       ALU.mult).then_inc(u_ready, 1)

            ssd(0, True)
            pool.wait_ge(xn_whole, 4)
            pool.memset(acc_ssd[:, :, :], 0.0)
            pool.drain().then_inc(ssd_zeroed, 1)
            with pool.Fori(1, GROUPS) as g:
                ssd(g, False)
            meet(pool, 3)
            meet(pool, 4)
            pool.wait_ge(x_landed, 64)
            with pool.Fori(0, OUT_N) as j:
                pool.wait_ge(tile_done, j * 16 + (FIRST + 16 * OUT_SLAB))
                pool.tensor_copy(xtile[:, 0:2, :], xtok[:, 0:2, bass.ds(j * 512, 512)])
                pool.tensor_copy(xtile[0:NB, 2, :], xtok[0:NB, 2, bass.ds(j * 512, 512)])
                pool.drain().then_inc(xtile_ready, 1)
            meet(pool, 5)
            pool.memset(valid[:, :], 1.0)
            pool.memset(xt[:, 2, :], 0.0)
            pool.iota(iota[:, :], pattern=[[1, SLOTS]], base=0, channel_multiplier=0,
                      allow_small_or_imprecise_dtypes=True)
            pool.tensor_tensor(before[:, :], mask[:, :], ident[:, :], ALU.subtract)
            pool.drain().then_inc(xt_clear, 1)
            pool.wait_ge(xt_clear, 1)
            pool.affine_select(out=valid[:, :], in_=valid[:, :], compare_op=ALU.is_ge, fill=0.0, base=T - 1,
                               pattern=[[-P, 3]], channel_multiplier=-1)
            pool.drain().then_inc(moe_consts, 1)
            meet(pool, 6)


_INS = ["x_prompt", "x_sample", "state_rglru_conv", "state_rglru_h", "state_ssd_conv", "state_ssd_h",
        "norm_mix", "w_in", "conv_rnn_w", "conv_rnn_b", "lru_wa", "lru_ba", "lru_wx", "lru_bx", "lru_lambda",
        "conv_ssd_w", "conv_ssd_b", "dt_bias", "a_log", "d_skip", "norm_ssd", "w_up_rnn", "w_up_ssd", "w_out",
        "norm_ffn", "w_route_group", "b_route_group", "w_route_expert", "b_route_expert",
        "w_exp_gate", "w_exp_up", "w_exp_down", "norm_final"]
_OUTS = [("y_p", (1, SEQ, D)), ("y_s", (NB, 1, D)),
         ("p_cr", (1, 1, HIST, D)), ("p_hr", (1, 1, D)), ("p_cs", (1, 1, HIST, D_XBC)),
         ("p_hs", (1, 1, HEADS, HD, NS)),
         ("s_cr", (1, NB, HIST, D)), ("s_hr", (1, NB, D)), ("s_cs", (1, NB, HIST, D_XBC)),
         ("s_hs", (1, NB, HEADS, HD, NS))]


def kernel(**inputs):
    import numpy as np
    import concourse.bacc as bacc
    from concourse.bass_utils import run_bass_kernel_spmd

    nc = bacc.Bacc("TRN2", target_bir_lowering=False, num_devices=1)
    arrays, ins, outs = {}, {}, {}
    for name in _INS:
        arr = np.ascontiguousarray(inputs[name])
        arrays[f"in_{name}"] = arr
        ins[name] = nc.dram_tensor(f"in_{name}", arr.shape, mybir.dt.from_np(arr.dtype), kind="ExternalInput").ap()
    for name, shape in _OUTS:
        outs[name] = nc.dram_tensor(f"out_{name}", shape, F32, kind="ExternalOutput").ap()
    build_program(nc, ins, outs)
    r = run_bass_kernel_spmd(nc, [arrays], core_ids=[0])
    return tuple(r.results[0][f"out_{name}"] for name, _ in _OUTS)
```
